# Optimizing a Trainium2 kernel written in Bass

```python
import jax
import jax.numpy as jnp
from jax import lax
import numpy as np
import math
import jax, jax.numpy as jnp

D_MODEL = 1024
BATCH = 1
SEQ = 256
DEPTH = 2

HEAD_DIM = 64
SB_HEADS = 8
FOX_HEADS = 8
DSA_HEADS = 8
DSA_KV_HEADS = 2
DSA_GROUP = DSA_HEADS // DSA_KV_HEADS
IDX_HEADS = 4
IDX_DIM = 64
BRANCH_WIDTH = SB_HEADS * HEAD_DIM
N_BRANCH = 3
D_FF = 4 * D_MODEL
ROPE_THETA = 500000.0
ROT_DIM = HEAD_DIM // 4
Q_BLOCK = 128
TOPK_MAX = 256
NORM_EPS = 1e-6

COL_SIZES = (
    SB_HEADS * HEAD_DIM, SB_HEADS * HEAD_DIM, SB_HEADS * HEAD_DIM,
    FOX_HEADS * HEAD_DIM, FOX_HEADS * HEAD_DIM, FOX_HEADS * HEAD_DIM,
    FOX_HEADS,
    DSA_HEADS * HEAD_DIM, DSA_KV_HEADS * HEAD_DIM, DSA_KV_HEADS * HEAD_DIM,
    IDX_HEADS * IDX_DIM, IDX_DIM, IDX_HEADS,
    N_BRANCH * D_MODEL,
)
COL_TOTAL = sum(COL_SIZES)
COL_SPLITS = tuple(sum(COL_SIZES[:i + 1]) for i in range(len(COL_SIZES) - 1))


def _rmsnorm(x, g):
    xf = x.astype(jnp.float32)
    y = xf * lax.rsqrt(jnp.mean(xf * xf, axis=-1, keepdims=True) + NORM_EPS)
    return (y * g.astype(jnp.float32)).astype(x.dtype)

def _partial_rope(x, positions):
    half = ROT_DIM // 2
    inv_freq = ROPE_THETA ** (-jnp.arange(0, ROT_DIM, 2, dtype=jnp.float32) / ROT_DIM)
    ang = positions.astype(jnp.float32)[:, :, None] * inv_freq
    cos = jnp.cos(ang)[:, :, None, :]
    sin = jnp.sin(ang)[:, :, None, :]
    xf = x.astype(jnp.float32)
    x1, x2, rest = xf[..., :half], xf[..., half:ROT_DIM], xf[..., ROT_DIM:]
    out = jnp.concatenate([x1 * cos - x2 * sin, x2 * cos + x1 * sin, rest], axis=-1)
    return out.astype(x.dtype)

def _to_blocks(a):
    b, s = a.shape[0], a.shape[1]
    return jnp.moveaxis(a.reshape(b, s // Q_BLOCK, Q_BLOCK, *a.shape[2:]), 1, 0)

def _from_blocks(a):
    a = jnp.moveaxis(a, 0, 1)
    return a.reshape(a.shape[0], a.shape[1] * a.shape[2], *a.shape[3:])

def _stick_breaking_attention(q, k, v):
    b, s, h, dh = q.shape
    scale = dh ** -0.5
    kf = k.astype(jnp.float32)
    vf = v.astype(jnp.float32)
    s_idx = jnp.arange(s)
    t_blk = jnp.arange(s).reshape(s // Q_BLOCK, Q_BLOCK)

    def block(args):
        qb, tb = args
        z = jnp.einsum('bthd,bshd->bhts', qb.astype(jnp.float32), kf) * scale
        strict = s_idx[None, :] < tb[:, None]
        log_beta = jax.nn.log_sigmoid(z)
        log_1m = jnp.where(strict, jax.nn.log_sigmoid(-z), 0.0)
        later = lax.cumsum(log_1m, axis=3, reverse=True) - log_1m
        w = jnp.where(strict, jnp.exp(log_beta + later), 0.0)
        return jnp.einsum('bhts,bshd->bthd', w, vf)

    out = lax.map(block, (_to_blocks(q), t_blk))
    return _from_blocks(out).reshape(b, s, h * dh).astype(q.dtype)

def _forgetting_attention(q, k, v, log_f):
    b, s, h, dh = q.shape
    scale = dh ** -0.5
    kf = k.astype(jnp.float32)
    vf = v.astype(jnp.float32)
    c = jnp.cumsum(log_f, axis=1).transpose(0, 2, 1)
    c_blk = jnp.moveaxis(c.reshape(b, h, s // Q_BLOCK, Q_BLOCK), 2, 0)
    s_idx = jnp.arange(s)
    t_blk = jnp.arange(s).reshape(s // Q_BLOCK, Q_BLOCK)

    def block(args):
        qb, cb, tb = args
        z = jnp.einsum('bthd,bshd->bhts', qb.astype(jnp.float32), kf) * scale
        z = z + cb[..., None] - c[:, :, None, :]
        causal = s_idx[None, :] <= tb[:, None]
        p = jax.nn.softmax(jnp.where(causal, z, -jnp.inf), axis=-1)
        return jnp.einsum('bhts,bshd->bthd', p, vf)

    out = lax.map(block, (_to_blocks(q), c_blk, t_blk))
    return _from_blocks(out).reshape(b, s, h * dh).astype(q.dtype)

def _indexed_sparse_attention(q, k, v, q_idx, k_idx, w_idx, top_k):
    b, s, g, r, dh = q.shape
    scale = dh ** -0.5
    kif = k_idx.astype(jnp.float32)
    s_idx = jnp.arange(s)
    t_blk = jnp.arange(s).reshape(s // Q_BLOCK, Q_BLOCK)
    gather = jax.vmap(lambda a, i: a[i])

    def block(args):
        qb, qib, wb, tb = args
        dots = jnp.einsum('bthi,bsi->bths', qib.astype(jnp.float32), kif) * (IDX_DIM ** -0.5)
        score = jnp.einsum('bth,bths->bts', wb.astype(jnp.float32) * (IDX_HEADS ** -0.5),
                           jax.nn.relu(dots))
        causal = s_idx[None, :] <= tb[:, None]
        score = jnp.where(causal[None], score, -jnp.inf)
        _, sel = lax.top_k(score, top_k)
        valid = sel <= tb[None, :, None]
        k_sel = gather(k, sel).astype(jnp.float32)
        v_sel = gather(v, sel).astype(jnp.float32)
        z = jnp.einsum('btgrd,btkgd->btgrk', qb.astype(jnp.float32), k_sel) * scale
        z = jnp.where(valid[:, :, None, None, :], z, -jnp.inf)
        p = jax.nn.softmax(z, axis=-1)
        return jnp.einsum('btgrk,btkgd->btgrd', p, v_sel)

    out = lax.map(block, (_to_blocks(q), _to_blocks(q_idx), _to_blocks(w_idx), t_blk))
    return _from_blocks(out).reshape(b, s, g * r * dh).astype(q.dtype)

def _layer(x, positions, g_mix, w_in, b_forget, w_branch, w_out, g_mlp, w_up, w_down):
    b, s, _ = x.shape
    h = _rmsnorm(x, g_mix)
    proj = h @ w_in
    (qa, ka, va, qb, kb, vb, fl, qc, kc, vc, qi, ki, wi, gl) = jnp.split(proj, COL_SPLITS, axis=-1)

    def heads(a, n):
        return a.reshape(b, s, n, -1)

    br_a = _stick_breaking_attention(heads(qa, SB_HEADS), heads(ka, SB_HEADS), heads(va, SB_HEADS))
    log_f = jax.nn.log_sigmoid((fl + b_forget).astype(jnp.float32))
    br_b = _forgetting_attention(heads(qb, FOX_HEADS), heads(kb, FOX_HEADS),
                                 heads(vb, FOX_HEADS), log_f)
    qc = _partial_rope(heads(qc, DSA_HEADS), positions).reshape(b, s, DSA_KV_HEADS, DSA_GROUP, HEAD_DIM)
    kc = _partial_rope(heads(kc, DSA_KV_HEADS), positions)
    vc = heads(vc, DSA_KV_HEADS)
    qi = _partial_rope(heads(qi, IDX_HEADS), positions)
    ki = _partial_rope(ki[:, :, None, :], positions)[:, :, 0, :]
    top_k = min(TOPK_MAX, s // 4)
    br_c = _indexed_sparse_attention(qc, kc, vc, qi, ki, wi, top_k)

    gates = jax.nn.sigmoid(gl.reshape(b, s, N_BRANCH, D_MODEL))
    y = (gates[:, :, 0, :] * (br_a @ w_branch[0])
         + gates[:, :, 1, :] * (br_b @ w_branch[1])
         + gates[:, :, 2, :] * (br_c @ w_branch[2]))
    x = x + y @ w_out

    h2 = _rmsnorm(x, g_mlp)
    x = x + jnp.square(jax.nn.relu(h2 @ w_up)) @ w_down
    return x

def first_inputs(seed: int = 0) -> dict:
    key = jax.random.key(seed)
    ks = jax.random.split(key, 12)
    f32 = jnp.float32
    x = jax.random.normal(ks[0], (BATCH, SEQ, D_MODEL), f32)
    positions = jnp.broadcast_to(jnp.arange(SEQ, dtype=jnp.int32), (BATCH, SEQ))
    g_mix = 1.0 + 0.02 * jax.random.normal(ks[1], (DEPTH, D_MODEL), f32)
    w_in = jax.random.normal(ks[2], (DEPTH, D_MODEL, COL_TOTAL), f32) * D_MODEL ** -0.5
    b_forget = jax.random.uniform(ks[3], (DEPTH, FOX_HEADS), f32, minval=1.0, maxval=4.0)
    w_branch = jax.random.normal(ks[4], (DEPTH, N_BRANCH, BRANCH_WIDTH, D_MODEL), f32) * BRANCH_WIDTH ** -0.5
    w_out = jax.random.normal(ks[5], (DEPTH, D_MODEL, D_MODEL), f32) * D_MODEL ** -0.5
    g_mlp = 1.0 + 0.02 * jax.random.normal(ks[6], (DEPTH, D_MODEL), f32)
    w_up = jax.random.normal(ks[7], (DEPTH, D_MODEL, D_FF), f32) * D_MODEL ** -0.5
    w_down = jax.random.normal(ks[8], (DEPTH, D_FF, D_MODEL), f32) * D_FF ** -0.5
    g_final = 1.0 + 0.02 * jax.random.normal(ks[9], (D_MODEL,), f32)
    return {'x': x, 'positions': positions, 'g_mix': g_mix, 'w_in': w_in,
            'b_forget': b_forget, 'w_branch': w_branch, 'w_out': w_out,
            'g_mlp': g_mlp, 'w_up': w_up, 'w_down': w_down, 'g_final': g_final}

def first_block(x, positions, g_mix, w_in, b_forget, w_branch, w_out, g_mlp, w_up, w_down, g_final):
    for layer in range(DEPTH):
        x = _layer(x, positions, g_mix[layer], w_in[layer], b_forget[layer], w_branch[layer],
                   w_out[layer], g_mlp[layer], w_up[layer], w_down[layer])
    return _rmsnorm(x, g_final)


N_MIXERS = 2
N_EVEN = (DEPTH + 1) // 2
N_ODD = DEPTH // 2
ALPHA = (2.0 * DEPTH) ** 0.25
BETA_INIT = (8.0 * DEPTH) ** -0.25
LN_EPS = 1e-5

GDN_K_HEADS = 4
GDN_V_HEADS = 8
GDN_HEAD_K = 128
GDN_HEAD_V = 128
GDN_KDIM = GDN_K_HEADS * GDN_HEAD_K
GDN_VDIM = GDN_V_HEADS * GDN_HEAD_V
GDN_CONV = 4
GDN_CHUNK = 64
GDN_QKV = 2 * GDN_KDIM + GDN_VDIM
GDN_IN = GDN_QKV + GDN_VDIM + 2 * GDN_V_HEADS
GDN_EPS = 1e-6

SWA_Q_HEADS = 16
SWA_KV_HEADS = 2
SWA_GROUP = SWA_Q_HEADS // SWA_KV_HEADS
SWA_HEAD_DIM = 64
SWA_WINDOW = 128
SWA_BLOCK = 128
SWA_QDIM = SWA_Q_HEADS * SWA_HEAD_DIM
SWA_KVDIM = SWA_KV_HEADS * SWA_HEAD_DIM
SWA_IN = SWA_QDIM + 2 * SWA_KVDIM

REL_BUCKETS = 32
REL_MAX_DIST = 128

FFN_DIM = 2816
N_EXPERTS = 8
TOP_K = 2
EXPERT_DIM = 3584


def layer_norm(x, g, b):
    xf = x.astype(jnp.float32)
    mu = jnp.mean(xf, axis=-1, keepdims=True)
    var = jnp.mean(jnp.square(xf - mu), axis=-1, keepdims=True)
    return ((xf - mu) * lax.rsqrt(var + LN_EPS) * g.astype(jnp.float32) + b.astype(jnp.float32)).astype(x.dtype)

def l2_normalize(x):
    xf = x.astype(jnp.float32)
    return xf * lax.rsqrt(jnp.sum(xf * xf, axis=-1, keepdims=True) + GDN_EPS)

def causal_depthwise_conv(x, w):
    width = w.shape[0]
    return lax.conv_general_dilated(
        x, w[:, None, :].astype(x.dtype), window_strides=(1,), padding=[(width - 1, 0)],
        dimension_numbers=('NWC', 'WIO', 'NWC'), feature_group_count=x.shape[-1])

def gated_delta_rule_chunked(q, k, v, g, beta):
    bsz, t, h, dk = q.shape
    dv = v.shape[-1]
    c = GDN_CHUNK
    n = t // c
    f32 = jnp.float32

    def blocks(a):
        a = a.astype(f32).reshape((bsz, n, c, h) + a.shape[3:])
        return jnp.moveaxis(a, 2, 3)

    q, k, v, g, beta = blocks(q), blocks(k), blocks(v), blocks(g), blocks(beta)
    g_cum = jnp.cumsum(g, axis=-1)
    causal = jnp.tril(jnp.ones((c, c), dtype=bool))
    strict = jnp.tril(jnp.ones((c, c), dtype=bool), -1)
    diff = g_cum[..., :, None] - g_cum[..., None, :]
    decay = jnp.exp(jnp.where(causal, diff, -jnp.inf))
    k_beta = k * beta[..., None]
    v_beta = v * beta[..., None]
    a_kk = jnp.where(strict, jnp.einsum('bnhid,bnhjd->bnhij', k_beta, k) * decay, 0.0)
    eye = jnp.eye(c, dtype=f32)
    t_inv = lax.linalg.triangular_solve(eye + a_kk, jnp.broadcast_to(eye, a_kk.shape),
                                        left_side=True, lower=True, unit_diagonal=True)
    u = jnp.einsum('bnhij,bnhje->bnhie', t_inv, v_beta)
    w = jnp.einsum('bnhij,bnhjd->bnhid', t_inv, k_beta * jnp.exp(g_cum)[..., None])
    a_qk = jnp.einsum('bnhid,bnhjd->bnhij', q, k) * decay
    g_last = g_cum[..., -1]
    q_dec = q * jnp.exp(g_cum)[..., None]
    k_dec = k * jnp.exp(g_last[..., None] - g_cum)[..., None]
    xs = (jnp.moveaxis(q_dec, 1, 0), jnp.moveaxis(k_dec, 1, 0), jnp.moveaxis(u, 1, 0),
          jnp.moveaxis(w, 1, 0), jnp.moveaxis(a_qk, 1, 0), jnp.moveaxis(jnp.exp(g_last), 1, 0))

    def step(s, inp):
        qd, kd, uc, wc, aqk, dl = inp
        v_new = uc - jnp.einsum('bhcd,bhde->bhce', wc, s)
        o = jnp.einsum('bhcd,bhde->bhce', qd, s) + jnp.einsum('bhcs,bhse->bhce', aqk, v_new)
        s = s * dl[..., None, None] + jnp.einsum('bhcd,bhce->bhde', kd, v_new)
        return s, o

    s0 = jnp.zeros((bsz, h, dk, dv), f32)
    _, o = lax.scan(step, s0, xs)
    o = jnp.moveaxis(o, 0, 1)
    return jnp.moveaxis(o, 2, 3).reshape(bsz, t, h, dv)

def gated_deltanet(x, w_in, conv_w, a_log, dt_bias, norm_w, w_out):
    bsz, t, _ = x.shape
    proj = x @ w_in
    o1 = GDN_QKV
    o2 = o1 + GDN_VDIM
    o3 = o2 + GDN_V_HEADS
    qkv = jax.nn.silu(causal_depthwise_conv(proj[..., :o1], conv_w))
    z = proj[..., o1:o2].reshape(bsz, t, GDN_V_HEADS, GDN_HEAD_V)
    b_logit = proj[..., o2:o3]
    a_logit = proj[..., o3:]
    q = qkv[..., :GDN_KDIM].reshape(bsz, t, GDN_K_HEADS, GDN_HEAD_K)
    k = qkv[..., GDN_KDIM:2 * GDN_KDIM].reshape(bsz, t, GDN_K_HEADS, GDN_HEAD_K)
    v = qkv[..., 2 * GDN_KDIM:].reshape(bsz, t, GDN_V_HEADS, GDN_HEAD_V)
    rep = GDN_V_HEADS // GDN_K_HEADS
    q = jnp.repeat(l2_normalize(q) * (GDN_HEAD_K ** -0.5), rep, axis=2)
    k = jnp.repeat(l2_normalize(k), rep, axis=2)
    beta = jax.nn.sigmoid(b_logit.astype(jnp.float32))
    g = -jnp.exp(a_log.astype(jnp.float32)) * jax.nn.softplus(
        a_logit.astype(jnp.float32) + dt_bias.astype(jnp.float32))
    o = gated_delta_rule_chunked(q, k, v, g, beta)
    o = o * lax.rsqrt(jnp.mean(o * o, axis=-1, keepdims=True) + GDN_EPS) * norm_w.astype(jnp.float32)
    o = o * jax.nn.silu(z.astype(jnp.float32))
    return o.reshape(bsz, t, GDN_VDIM).astype(x.dtype) @ w_out

def t5_bucket(dist):
    max_exact = REL_BUCKETS // 2
    df = jnp.maximum(dist, 1).astype(jnp.float32)
    large = max_exact + (jnp.log(df / max_exact) / math.log(REL_MAX_DIST / max_exact)
                         * (REL_BUCKETS - max_exact)).astype(jnp.int32)
    large = jnp.minimum(large, REL_BUCKETS - 1)
    return jnp.where(dist < max_exact, dist, large)

def swa_sink_attention(x, w_in, b_in, sinks, rel_bias, w_out):
    bsz, t, _ = x.shape
    nb = t // SWA_BLOCK
    proj = x @ w_in + b_in
    q = proj[..., :SWA_QDIM].reshape(bsz, nb, SWA_BLOCK, SWA_KV_HEADS, SWA_GROUP, SWA_HEAD_DIM)
    k = proj[..., SWA_QDIM:SWA_QDIM + SWA_KVDIM]
    v = proj[..., SWA_QDIM + SWA_KVDIM:]

    def band(a):
        ab = a.reshape(bsz, nb, SWA_BLOCK, SWA_KV_HEADS, SWA_HEAD_DIM)
        prev = jnp.pad(ab, ((0, 0), (1, 0), (0, 0), (0, 0), (0, 0)))[:, :-1]
        return jnp.concatenate([prev, ab], axis=2)

    kb, vb = band(k), band(v)
    s = jnp.einsum('bnqkgd,bnskd->bnkgqs', q, kb).astype(jnp.float32) * (SWA_HEAD_DIM ** -0.5)
    qi = jnp.arange(SWA_BLOCK)[:, None]
    kj = jnp.arange(2 * SWA_BLOCK)[None, :]
    dist = qi + SWA_BLOCK - kj
    bias = rel_bias.astype(jnp.float32)[t5_bucket(jnp.maximum(dist, 0))]
    bias = jnp.transpose(bias, (2, 0, 1)).reshape(SWA_KV_HEADS, SWA_GROUP, SWA_BLOCK, 2 * SWA_BLOCK)
    band_ok = (dist >= 0) & (dist < SWA_WINDOW)
    blk = jnp.arange(nb)[:, None, None]
    mask = band_ok[None] & ((blk > 0) | (kj >= SWA_BLOCK)[None])
    s = jnp.where(mask[None, :, None, None], s + bias, -jnp.inf)
    sink = jnp.broadcast_to(sinks.astype(jnp.float32).reshape(SWA_KV_HEADS, SWA_GROUP, 1, 1),
                            s.shape[:-1] + (1,))
    p = jax.nn.softmax(jnp.concatenate([s, sink], axis=-1), axis=-1)[..., :-1]
    o = jnp.einsum('bnkgqs,bnskd->bnqkgd', p.astype(vb.dtype), vb).reshape(bsz, t, SWA_QDIM)
    return o @ w_out

def swiglu(x, w_gate, w_up, w_down):
    return (jax.nn.silu(x @ w_gate) * (x @ w_up)) @ w_down

def moe_swiglu(x, w_router, w_gate, w_up, w_down):
    bsz, t, d = x.shape
    xf = x.reshape(bsz * t, d)
    logits = (xf @ w_router).astype(jnp.float32)
    top_val, top_idx = lax.top_k(logits, TOP_K)
    top_w = jax.nn.softmax(top_val, axis=-1)
    gates = jnp.einsum('nk,nke->ne', top_w, jax.nn.one_hot(top_idx, N_EXPERTS, dtype=jnp.float32))
    out = jnp.zeros_like(xf)
    for e in range(N_EXPERTS):
        h = jax.nn.silu(xf @ w_gate[e]) * (xf @ w_up[e])
        out = out + gates[:, e:e + 1].astype(xf.dtype) * (h @ w_down[e])
    return out.reshape(bsz, t, d)

def second_inputs(seed: int = 0) -> dict:
    key = jax.random.key(seed)
    ks = jax.random.split(key, 24)

    def nrm(k, shape, scale):
        return jax.random.normal(k, shape, jnp.float32) * scale

    x = nrm(ks[0], (BATCH, SEQ, D_MODEL), 1.0)
    a_w_in = nrm(ks[1], (N_EVEN, D_MODEL, GDN_IN), D_MODEL ** -0.5)
    a_conv_w = nrm(ks[2], (N_EVEN, GDN_CONV, GDN_QKV), GDN_CONV ** -0.5)
    a_a_log = jnp.log(jax.random.uniform(ks[3], (N_EVEN, GDN_V_HEADS), jnp.float32, 1.0, 16.0))
    dt = jnp.exp(jax.random.uniform(ks[4], (N_EVEN, GDN_V_HEADS), jnp.float32,
                                    math.log(1e-3), math.log(1e-1)))
    a_dt_bias = dt + jnp.log(-jnp.expm1(-dt))
    a_norm_w = 1.0 + nrm(ks[5], (N_EVEN, GDN_HEAD_V), 0.02)
    a_w_out = nrm(ks[6], (N_EVEN, GDN_VDIM, D_MODEL), GDN_VDIM ** -0.5 * BETA_INIT)
    b_w_in = nrm(ks[7], (N_ODD, D_MODEL, SWA_IN), D_MODEL ** -0.5)
    b_b_in = nrm(ks[8], (N_ODD, SWA_IN), 0.02)
    b_sinks = nrm(ks[9], (N_ODD, SWA_Q_HEADS), 1.0)
    b_w_out = nrm(ks[10], (N_ODD, SWA_QDIM, D_MODEL), SWA_QDIM ** -0.5 * BETA_INIT)
    rel_bias = nrm(ks[11], (REL_BUCKETS, SWA_Q_HEADS), 0.3)
    ffn_w_gate = nrm(ks[12], (N_EVEN, D_MODEL, FFN_DIM), D_MODEL ** -0.5)
    ffn_w_up = nrm(ks[13], (N_EVEN, D_MODEL, FFN_DIM), D_MODEL ** -0.5)
    ffn_w_down = nrm(ks[14], (N_EVEN, FFN_DIM, D_MODEL), FFN_DIM ** -0.5 * BETA_INIT)
    moe_router = nrm(ks[15], (N_ODD, D_MODEL, N_EXPERTS), D_MODEL ** -0.5)
    moe_w_gate = nrm(ks[16], (N_ODD, N_EXPERTS, D_MODEL, EXPERT_DIM), D_MODEL ** -0.5)
    moe_w_up = nrm(ks[17], (N_ODD, N_EXPERTS, D_MODEL, EXPERT_DIM), D_MODEL ** -0.5)
    moe_w_down = nrm(ks[18], (N_ODD, N_EXPERTS, EXPERT_DIM, D_MODEL), EXPERT_DIM ** -0.5 * BETA_INIT)
    ln_g = 1.0 + nrm(ks[19], (DEPTH, 2, D_MODEL), 0.02)
    ln_b = nrm(ks[20], (DEPTH, 2, D_MODEL), 0.02)
    return {'x': x, 'a_w_in': a_w_in, 'a_conv_w': a_conv_w, 'a_a_log': a_a_log, 'a_dt_bias': a_dt_bias,
            'a_norm_w': a_norm_w, 'a_w_out': a_w_out, 'b_w_in': b_w_in, 'b_b_in': b_b_in,
            'b_sinks': b_sinks, 'b_w_out': b_w_out, 'rel_bias': rel_bias, 'ffn_w_gate': ffn_w_gate,
            'ffn_w_up': ffn_w_up, 'ffn_w_down': ffn_w_down, 'moe_router': moe_router,
            'moe_w_gate': moe_w_gate, 'moe_w_up': moe_w_up, 'moe_w_down': moe_w_down,
            'ln_g': ln_g, 'ln_b': ln_b}

def second_block(x, a_w_in, a_conv_w, a_a_log, a_dt_bias, a_norm_w, a_w_out, b_w_in, b_b_in, b_sinks,
              b_w_out, rel_bias, ffn_w_gate, ffn_w_up, ffn_w_down, moe_router, moe_w_gate, moe_w_up,
              moe_w_down, ln_g, ln_b):
    for i in range(DEPTH):
        j = i // N_MIXERS
        if i % N_MIXERS == 0:
            h = gated_deltanet(x, a_w_in[j], a_conv_w[j], a_a_log[j], a_dt_bias[j], a_norm_w[j], a_w_out[j])
        else:
            h = swa_sink_attention(x, b_w_in[j], b_b_in[j], b_sinks[j], rel_bias, b_w_out[j])
        x = layer_norm(ALPHA * x + h, ln_g[i, 0], ln_b[i, 0])
        if i % 2 == 0:
            f = swiglu(x, ffn_w_gate[j], ffn_w_up[j], ffn_w_down[j])
        else:
            f = moe_swiglu(x, moe_router[j], moe_w_gate[j], moe_w_up[j], moe_w_down[j])
        x = layer_norm(ALPHA * x + f, ln_g[i, 1], ln_b[i, 1])
    return x


def setup_inputs(seed=0):
    out = dict(first_inputs(seed))
    for name, value in second_inputs(seed + 1).items():
        if name != "x":
            out[name + "_2"] = value
    return out


def reference(
    x, positions, g_mix, w_in, b_forget, w_branch, w_out, g_mlp, w_up, w_down, g_final,
    a_w_in_2, a_conv_w_2, a_a_log_2, a_dt_bias_2, a_norm_w_2, a_w_out_2, b_w_in_2, b_b_in_2,
    b_sinks_2, b_w_out_2, rel_bias_2, ffn_w_gate_2, ffn_w_up_2, ffn_w_down_2, moe_router_2,
    moe_w_gate_2, moe_w_up_2, moe_w_down_2, ln_g_2, ln_b_2,
):
    x = first_block(
        x, positions, g_mix, w_in, b_forget, w_branch, w_out, g_mlp, w_up, w_down, g_final,
    )
    return second_block(
        x, a_w_in_2, a_conv_w_2, a_a_log_2, a_dt_bias_2, a_norm_w_2, a_w_out_2, b_w_in_2,
        b_b_in_2, b_sinks_2, b_w_out_2, rel_bias_2, ffn_w_gate_2, ffn_w_up_2, ffn_w_down_2,
        moe_router_2, moe_w_gate_2, moe_w_up_2, moe_w_down_2, ln_g_2, ln_b_2,
    )


_drawn_inputs = setup_inputs


def setup_inputs(seed=0):
    import zlib

    import numpy as np

    out = dict(_drawn_inputs(seed))
    spreads = {}
    factors = {'a_norm_w_2': 8.0, 'b_b_in_2': 4.734, 'b_sinks_2': 8.0, 'rel_bias_2': 2.714}
    for name, (base, spread) in spreads.items():
        noise = np.random.default_rng([zlib.crc32(name.encode()), seed]).standard_normal(out[name].shape)
        drawn = base * np.exp(spread * noise) if base else spread * noise
        out[name] = jnp.asarray(drawn.astype(out[name].dtype))
    for name, factor in factors.items():
        out[name] = (out[name] * factor).astype(out[name].dtype)
    return out
```

```python
from contextlib import ExitStack, contextmanager

import numpy as np

import concourse.bass as bass
from concourse import mybir

F32 = mybir.dt.float32
I32 = mybir.dt.int32
U32 = mybir.dt.uint32
ALU = mybir.AluOpType
ACT = mybir.ActivationFunctionType
AX_X = mybir.AxisListType.X

P = 128
T = 256
NT = T // P
D = 1024
KC = D // P
DEPTH = 2
HD = 64
BW = 512
BANK = 512
SLOT = KC * BW
TRI = 3 * P
NEG = -1.0e30
MASKED = -3.0e38
TAKEN = -3.4e38
DSA_TOPK = T // 4
ROPE_THETA, ROT = 500000.0, 16
ROPE_COLS = 8 + 640, 776, 1096
C_COLS = 1100
D_FF = 4096
RMS_EPS, LN_EPS, GDN_EPS = 1e-6, 1e-5, 1e-6
ALPHA = (2.0 * DEPTH) ** 0.25
GK_HEADS, GV_HEADS, GDK = 4, 8, 128
CONV = 4
PAD = CONV - 1
SWA_HEADS, SWA_WINDOW = 16, 128
BUCKETS, MAX_DIST = 32, 128
FFN_DIM, EXPERT_DIM, E = 2816, 3584, 8
FB = 256
CAP = 112
ROUNDS = -(-T // CAP)
LEVELS = 7


def constants():
    p = np.arange(P)[:, None]
    m = np.arange(P)[None, :]
    parts = {
        "ident": p == m, "ones": p >= 0 * m, "le": p <= m, "lt": p < m, "ge": p >= m,
        "neg": np.concatenate([np.where(m > p, NEG, 0), 0.0 * (p + m), np.where(m > p, NEG, 0)], 1),
        "level": np.concatenate([(p // (2 << k) == m // (2 << k)) & (m % (2 << k) >= 1 << k)
                                 & (p % (2 << k) < 1 << k) for k in range(LEVELS)], 1),
        "freq": np.tile((ROPE_THETA ** (-np.arange(0, ROT, 2, dtype=np.float32) / ROT)).astype(np.float32), (P, 1)),
        "slot": np.tile(np.arange(CAP), (P, 1)),
        "expert": np.tile(np.arange(E), (P, 1)),
    }
    v = np.arange(TRI)
    dist = (2 * P - 1) - v
    exact = BUCKETS // 2
    df = np.maximum(dist, 1).astype(np.float32)
    large = exact + (np.log(df / np.float32(exact)) / np.float32(np.log(MAX_DIST / exact))
                     * (BUCKETS - exact)).astype(np.int32)
    bucket = np.where(dist < exact, dist, np.minimum(large, BUCKETS - 1))
    ok = (dist >= 0) & (dist < SWA_WINDOW)
    onehot = np.zeros((P, TRI))
    onehot[:BUCKETS] = (bucket[None] == np.arange(BUCKETS)[:, None]) & ok[None]
    parts["bucket"] = onehot
    parts["window"] = np.tile(np.where(ok, 0.0, NEG), (P, 1))
    at, cols = {}, 0
    for name, a in parts.items():
        at[name] = (cols, a.shape[1])
        cols += a.shape[1]
    return np.concatenate([np.asarray(a, np.float32) for a in parts.values()], 1).copy(), at


CONSTS, CONST_AT = constants()


class Core:

    def __init__(self, nc, ctx):
        self.nc, self.ctx = nc, ctx
        self.ring = self.sbuf("ring", [P, 7, SLOT])
        self.consts = self.sbuf("consts", [P, CONSTS.shape[1]])
        self.x = self.sbuf("x", [P, NT, D])
        self.xT = self.sbuf("xT", [P, KC, T])
        self.arena = self.sbuf("arena", [P, 15232])
        self.banks = [ctx.enter_context(nc.psum_tensor(f"bank{i}", [P, BANK], F32)) for i in range(8)]
        self.scope, self.sems = ctx, []

    def sbuf(self, name, shape, dt=F32):
        return self.ctx.enter_context(self.nc.sbuf_tensor(name, shape, dt))[:]

    def sem(self, name):
        s = self.scope.enter_context(self.nc.semaphore(name))
        self.sems.append(s)
        return s

    @contextmanager
    def semaphores(self):
        outer, self.sems = (self.scope, self.sems), []
        with ExitStack() as self.scope:
            yield self.sems
        self.scope, self.sems = outer

    def const(self, name):
        a, n = CONST_AT[name]
        return self.consts[:, a:a + n]

    def level(self, k):
        a = CONST_AT["level"][0] + k * P
        return self.consts[:, a:a + P]

    def part(self, at, *shape):
        n = int(np.prod(shape))
        assert at + n <= 15232, (at, n)
        v = self.arena[:, at:at + n]
        if len(shape) == 2:
            v = v.rearrange("p (a b) -> p a b", a=shape[0])
        if len(shape) == 3:
            v = v.rearrange("p (a b c) -> p a b c", a=shape[0], b=shape[1])
        return v, at + n


class Weights:

    def __init__(self, core, tag, slots, plan):
        self.core, self.slots, self.plan = core, slots, plan
        self.landed = [core.sem(f"{tag}_landed{i}") for i in range(slots)]
        self.tile_used = core.sem(f"{tag}_tile_used")

    def tile(self, n, chunks, cols):
        return self.core.ring[:, n % self.slots, 0:chunks * cols].rearrange("p (c n) -> p c n", c=chunks)

    def load(self, sp, n):
        chunks, parts = self.plan[n]
        cols = sum(a.shape[2] for a in parts)
        at = 0
        for i, a in enumerate(parts):
            w = a.shape[2]
            dma = sp.dma_start(self.tile(n, chunks, cols)[:, :, at:at + w], a)
            at += w
            dma.then_inc(self.landed[n % self.slots], 16)

    def fill(self, sp):
        for n in range(min(self.slots, len(self.plan))):
            self.load(sp, n)

    def refill(self, sp, first, last):
        for n in range(first, last):
            if n + self.slots < len(self.plan):
                sp.wait_ge(self.tile_used, n + 1)
                self.load(sp, n + self.slots)

    def wait(self, pe, n):
        before = sum(len(self.plan[i][1]) for i in range(n % self.slots, n + 1, self.slots))
        pe.wait_ge(self.landed[n % self.slots], 16 * before)


def rows(a, chunks):
    return a.rearrange("(p k) n -> p k n", k=chunks)


def rows_by_chunk(a):
    return a.rearrange("(k p) n -> p k n", p=P)


def tidy(core, sems):
    with core.nc.Block() as block:
        @block.sync
        def _(sp):
            for s in sems:
                sp.sem_clear(s)


def row_broadcast(a):
    return a.rearrange("(o n) -> o n", o=1).broadcast_to([P, a.shape[0]])


def norm_stage(core, tag, gain, shift, eps, out=None, add=None, before=None):
    nc = core.nc
    y, at = core.part(0, NT, D)
    g, at = core.part(at, D)
    b, at = core.part(at, D)
    stats, at = core.part(at, NT, 12)
    mv, at = core.part(at, NT, 2)
    rstd, at = core.part(at, NT, 1)
    x = core.x
    if out is not None:
        y = out
    gains = core.sem(f"{tag}_gains")
    squares = core.sem(f"{tag}_squares")
    variance = core.sem(f"{tag}_variance")
    root = core.sem(f"{tag}_root")
    inverse = core.sem(f"{tag}_inverse")
    centred = core.sem(f"{tag}_centred")
    scaled = core.sem(f"{tag}_scaled")
    normed = core.sem(f"{tag}_normed")
    turned = core.sem(f"{tag}_turned")
    rms = shift is None
    with nc.Block() as block:
        @block.sync
        def _(sp):
            sp.dma_start(g, row_broadcast(gain)).then_inc(gains, 16)
            if not rms:
                sp.dma_start(b, row_broadcast(shift)).then_inc(gains, 16)
            if before is not None:
                before(sp)

        @block.scalar
        def _(act):
            if rms:
                for t in range(NT):
                    act.activation(core.xT[:, 4 * t:4 * t + 4, :].rearrange("p a b -> p (a b)"), x[:, t, :],
                                   ACT.Square, accum_out=mv[:, t, 1:2]).then_inc(squares, 1)
            act.wait_ge(variance, 1)
            act.activation(rstd, mv[:, :, 1:2], ACT.Sqrt).then_inc(root, 1)
            for bank in range(0, 4, 2):
                act.wait_ge(turned, bank + 1)
                act.copy(core.xT[:, 2 * bank:2 * bank + 2, :].rearrange("p a b -> p (a b)"), core.banks[bank][:])

        @block.vector
        def _(dve):
            if rms:
                dve.wait_ge(squares, NT)
                dve.tensor_scalar(mv[:, :, 1:2], mv[:, :, 1:2], 1.0 / D, eps, ALU.mult, ALU.add).then_inc(variance, 1)
            else:
                for t in range(NT):
                    for half in range(2):
                        dve.bn_stats(stats[:, t, 6 * half:6 * half + 6],
                                     x[:, t, half * BANK:(half + 1) * BANK]).then_inc(squares, 1)
                for t in range(NT):
                    dve.wait_ge(squares, 2 * (t + 1))
                    dve.bn_aggr(mv[:, t, :], stats[:, t, :]).then_inc(squares, 1)
                dve.wait_ge(squares, 6)
                dve.tensor_scalar(mv[:, :, 1:2], mv[:, :, 1:2], eps, None, ALU.add).then_inc(variance, 1)
            dve.wait_ge(root, 1)
            dve.reciprocal(rstd, rstd).then_inc(inverse, 1)
            dve.wait_ge(inverse, 1)
            dve.wait_ge(gains, 16 if rms else 32)
            for t in range(NT):
                if rms:
                    dve.scalar_tensor_tensor(out=y[:, t, :], in0=x[:, t, :], scalar=rstd[:, t, :], in1=g,
                                             op0=ALU.mult, op1=ALU.mult).then_inc(normed, 1)
                else:
                    dve.tensor_scalar(y[:, t, :], x[:, t, :], mv[:, t, 0:1], rstd[:, t, :], ALU.subtract,
                                      ALU.mult).then_inc(centred, 1)
                    dve.wait_ge(centred, t + 1)
                    dve.tensor_tensor(y[:, t, :], y[:, t, :], g, ALU.mult).then_inc(scaled, 1)
                    dve.wait_ge(scaled, t + 1)
                    dve.tensor_tensor(y[:, t, :], y[:, t, :], b, ALU.add).then_inc(normed, 1)
            for bank in range(1, 4, 2):
                dve.wait_ge(turned, bank + 1)
                dve.tensor_copy(core.xT[:, 2 * bank:2 * bank + 2, :].rearrange("p a b -> p (a b)"),
                                core.banks[bank][:])

        @block.tensor
        def _(pe):
            pe.wait_ge(normed, NT)
            pe.wait_ge(squares, NT)
            for bank in range(4):
                for c in range(2):
                    for t in range(NT):
                        mm = pe.transpose(core.banks[bank][:, c * T + t * P:c * T + (t + 1) * P],
                                          y[:, t, 2 * bank + c::KC], core.const("ident"))
                mm.then_inc(turned, 1)


def pair(core, n):
    return core.banks[2 * (n % 2)], core.banks[2 * (n % 2) + 1]


def projection_stage(core, tag, w, jobs, lhs=None, setup=None):
    nc = core.nc
    act_stored = core.sem(f"{tag}_act_stored")
    dve_stored = core.sem(f"{tag}_dve_stored")
    first, last = jobs[0][0], jobs[-1][0] + 1
    with nc.Block() as block:
        @block.sync
        def _(sp):
            w.refill(sp, first, last)

        @block.tensor
        def _(pe):
            for n, (tile, form, cols, store) in enumerate(jobs):
                w.wait(pe, tile)
                if n >= 2:
                    pe.wait_ge(act_stored, n - 1)
                    pe.wait_ge(dve_stored, n - 1)
                wt = w.tile(tile, KC, sum(a.shape[2] for a in w.plan[tile][1]))
                for half, bank in enumerate(pair(core, n)):
                    if form == "KV" and half == 1:
                        for t in range(NT):
                            for c in range(KC):
                                mm = pe.matmul(bank[:, t * P:(t + 1) * P], core.xT[:, c, t * P:(t + 1) * P],
                                               wt[:, c, 2 * P:3 * P], start=(c == 0), stop=(c == KC - 1))
                    elif form == "N":
                        for c in range(KC):
                            mm = pe.matmul(bank[:, 0:cols], core.xT[:, c, half * P:(half + 1) * P],
                                           wt[:, c, 0:cols], start=(c == 0), stop=(c == KC - 1))
                    else:
                        for f in range(2 * half, min(2 * half + 2, cols // P)):
                            for c in range(KC):
                                mm = pe.matmul(bank[:, (f % 2) * T:(f % 2 + 1) * T], wt[:, c, f * P:(f + 1) * P],
                                               core.xT[:, c, :], start=(c == 0), stop=(c == KC - 1))
                mm.then_inc(w.tile_used, 1)

        @block.scalar
        def _(act):
            for n, (tile, form, cols, store) in enumerate(jobs):
                act.wait_ge(w.tile_used, tile + 1)
                store(act, 0, pair(core, n)[0]).then_inc(act_stored, 1)

        @block.vector
        def _(dve):
            for n, (tile, form, cols, store) in enumerate(jobs):
                dve.wait_ge(w.tile_used, tile + 1)
                store(dve, 1, pair(core, n)[1]).then_inc(dve_stored, 1)


def copy(eng, core, out, in_):
    return eng.copy(out, in_) if eng is core.nc.scalar else eng.tensor_copy(out, in_)


def scaled(eng, core, out, in_, factor):
    if eng is core.nc.scalar:
        return eng.mul(out, in_, factor)
    return eng.tensor_scalar(out, in_, factor, None, ALU.mult)


def keep_T(core, dst, factor=None):
    def store(eng, half, bank):
        out = dst[:, 2 * half:2 * half + 2, :]
        in_ = bank[:].rearrange("p (a b) -> p a b", a=2)
        return copy(eng, core, out, in_) if factor is None else scaled(eng, core, out, in_, factor)
    return store


def keep_N(core, dst):
    def store(eng, half, bank):
        out = dst[:, half, :]
        return copy(eng, core, out, bank[:, 0:out.shape[1]])
    return store


def turn_stage(core, tag, src, dst, chunks, column=None):
    nc = core.nc
    turned = core.sem(f"{tag}_turned")
    act_stored = core.sem(f"{tag}_act_stored")
    dve_stored = core.sem(f"{tag}_dve_stored")
    column = column or (lambda t, c: src[:, t, c * P:(c + 1) * P])
    steps = [(n, range(2 * n, min(2 * n + 2, chunks))) for n in range(-(-chunks // 2))]
    with nc.Block() as block:
        @block.tensor
        def _(pe):
            for n, cs in steps:
                if n >= 8:
                    pe.wait_ge(act_stored, (n - 8) // 2 + 1)
                    pe.wait_ge(dve_stored, (n - 8) // 2 + 1)
                for c in cs:
                    for t in range(NT):
                        mm = pe.transpose(core.banks[n % 8][:, (c % 2) * T + t * P:(c % 2) * T + (t + 1) * P],
                                          column(t, c), core.const("ident"))
                mm.then_inc(turned, 1)

        def store(eng, n, cs):
            eng.wait_ge(turned, n + 1)
            out = dst[:, cs[0]:cs[-1] + 1, :]
            return copy(eng, core, out, core.banks[n % 8][:, 0:len(cs) * T].rearrange("p (a b) -> p a b", b=T))

        @block.scalar
        def _(act):
            for n, cs in steps[0::2]:
                store(act, n, cs).then_inc(act_stored, 1)

        @block.vector
        def _(dve):
            for n, cs in steps[1::2]:
                store(dve, n, cs).then_inc(dve_stored, 1)


def softmax_stage(core, tag, at, heads, q, k, v, mask, out, bias=None, sink=None):
    nc = core.nc
    z, at = core.part(at, 2, TRI)
    p, at = core.part(at, 2, TRI)
    pT, at = core.part(at, 2, TRI)
    top, at = core.part(at, heads, NT)
    minus, at = core.part(at, heads, NT)
    total, at = core.part(at, heads, NT)
    extra, at = core.part(at, heads, NT)
    s = {n: core.sem(f"{tag}_{n}") for n in ("scores", "masked", "sunk", "negated", "probs", "turned", "copied",
                                               "summed", "sink_exp", "added", "inverse")}
    if bias is not None:
        bias_lhs, bias_rhs = bias
    per_bank = BANK // HD
    obank = [[core.banks[4 + t * (heads // per_bank) + g] for g in range(heads // per_bank)] for t in range(NT)]
    edges = (0, P), (P, TRI)

    with nc.Block() as block:
        @block.tensor
        def _(pe):
            for i in range(heads + 2):
                h = i
                if h < heads:
                    if h >= 2:
                        pe.wait_ge(s["masked"], h - 1)
                    bank = core.banks[h % 2]
                    for t, (a, b) in enumerate(edges):
                        mm = pe.matmul(bank[:, a:b], q(h)[:, t * P:(t + 1) * P], k(h)[:, 0:b - a],
                                       start=True, stop=(bias is None))
                        if bias is not None:
                            mm = pe.matmul(bank[:, a:b], bias_lhs(h), bias_rhs[:, 0:b - a], start=False, stop=True)
                    mm.then_inc(s["scores"], 1)
                h = i - 1
                if 0 <= h < heads:
                    pe.wait_ge(s["probs"], h + 1)
                    if h >= 2:
                        pe.wait_ge(s["copied"], h - 1)
                    for j in range(3):
                        mm = pe.transpose(core.banks[2 + h % 2][:, j * P:(j + 1) * P],
                                          p[:, h % 2, j * P:(j + 1) * P], core.const("ident"))
                    mm.then_inc(s["turned"], 1)
                h = i - 2
                if h >= 0:
                    pe.wait_ge(s["copied"], h + 1)
                    g, c = h // per_bank, (h % per_bank) * HD
                    w = pT[:, h % 2, :]
                    pe.matmul(obank[0][g][:, c:c + HD], w[:, 0:P], v(h, 0), start=True, stop=True)
                    pe.matmul(obank[1][g][:, c:c + HD], w[:, P:2 * P], v(h, 0), start=True, stop=False)
                    pe.matmul(obank[1][g][:, c:c + HD], w[:, 2 * P:TRI], v(h, 1), start=False,
                              stop=True).then_inc(s["summed"], 1)

        @block.vector
        def _(dve):
            for i in range(heads + 2):
                h = i
                if h < heads:
                    dve.wait_ge(s["scores"], h + 1)
                    if h >= 2:
                        dve.wait_ge(s["probs"], h - 1)
                    for t, (a, b) in enumerate(edges):
                        op = dve.tensor_tensor_reduce(z[:, h % 2, a:b], core.banks[h % 2][:, a:b], mask(h, t),
                                                      1.0, -3.0e38, ALU.add, ALU.max, top[:, h, t:t + 1])
                    op.then_inc(s["masked"], 1)
                    dve.wait_ge(s["masked"], h + 1)
                    if sink is not None:
                        dve.tensor_scalar(top[:, h, :], top[:, h, :], sink[:, h:h + 1], None,
                                          ALU.max).then_inc(s["sunk"], 1)
                        dve.wait_ge(s["sunk"], h + 1)
                    dve.tensor_scalar(minus[:, h, :], top[:, h, :], -1.0, None, ALU.mult).then_inc(s["negated"], 1)
                h = i - 2
                if h >= 0:
                    dve.wait_ge(s["turned"], h + 1)
                    if h >= 2:
                        dve.wait_ge(s["summed"], h - 1)
                    dve.tensor_copy(pT[:, h % 2, :], core.banks[2 + h % 2][:, 0:TRI]).then_inc(s["copied"], 1)
            if sink is not None:
                dve.wait_ge(s["sink_exp"], heads)
                dve.tensor_tensor(total, total, extra, ALU.add).then_inc(s["added"], 1)
                dve.wait_ge(s["added"], 1)
            dve.wait_ge(s["probs"], heads)
            dve.reciprocal(total, total).then_inc(s["inverse"], 1)
            dve.wait_ge(s["inverse"], 1)
            dve.wait_ge(s["summed"], heads)
            for t in range(NT):
                for g in range(heads // per_bank):
                    hs = slice(g * per_bank, (g + 1) * per_bank)
                    dve.tensor_tensor(out[:, t, g * BANK:(g + 1) * BANK].rearrange("p (h d) -> p h d", d=HD),
                                      obank[t][g][:].rearrange("p (h d) -> p h d", d=HD),
                                      total[:, hs, t:t + 1].broadcast_to([P, per_bank, HD]), ALU.mult)

        @block.scalar
        def _(act):
            for h in range(heads):
                act.wait_ge(s["negated"], h + 1)
                if h >= 2:
                    act.wait_ge(s["turned"], h - 1)
                if sink is not None:
                    for t in range(NT):
                        op = act.activation(extra[:, h, t:t + 1], sink[:, h:h + 1], ACT.Exp, bias=minus[:, h, t:t + 1])
                    op.then_inc(s["sink_exp"], 1)
                for t, (a, b) in enumerate(edges):
                    op = act.activation(p[:, h % 2, a:b], z[:, h % 2, a:b], ACT.Exp, bias=minus[:, h, t:t + 1],
                                        accum_out=total[:, h, t:t + 1])
                op.then_inc(s["probs"], 1)


def stick_stage(core, tag, at, qT, kT, v, out):
    nc = core.nc
    z, at = core.part(at, 2, TRI)
    small, at = core.part(at, 2, TRI)
    sp_, at = core.part(at, 2, TRI)
    w, at = core.part(at, 2, TRI)
    s = {n: core.sem(f"{tag}_{n}") for n in ("scores", "kept", "minus_abs", "exp", "log", "soft", "soft_masked",
                                               "cum", "diff", "weights", "masked", "summed")}
    H = 8

    def q(h):
        return qT[HD * (h % 2):HD * (h % 2) + HD, h // 2, :]

    def k(h):
        return kT[HD * (h % 2):HD * (h % 2) + HD, h // 2, :]

    with nc.Block() as block:
        @block.tensor
        def _(pe):
            for i in range(H + 2):
                h = i
                if h < H:
                    if h >= 2:
                        pe.wait_ge(s["soft"], h - 1)
                        pe.wait_ge(s["kept"], h - 1)
                    bank = core.banks[h % 2]
                    pe.matmul(bank[:, 0:T], k(h)[:, 0:P], q(h), start=True, stop=True)
                    pe.matmul(bank[:, T:TRI], k(h)[:, P:T], q(h)[:, P:T], start=True, stop=True)\
                      .then_inc(s["scores"], 1)
                h = i - 1
                if 0 <= h < H:
                    pe.wait_ge(s["soft_masked"], h + 1)
                    if h >= 2:
                        pe.wait_ge(s["diff"], h - 1)
                    bank = core.banks[2 + h % 2]
                    pe.matmul(bank[:, 0:P], core.const("ge"), sp_[:, h % 2, 0:P], start=True, stop=True)
                    pe.matmul(bank[:, P:T], core.const("ge"), sp_[:, h % 2, P:T], start=True, stop=False)
                    pe.matmul(bank[:, P:T], core.const("ones"), sp_[:, h % 2, T:TRI], start=False, stop=True)
                    pe.matmul(bank[:, T:TRI], core.const("ge"), sp_[:, h % 2, T:TRI], start=True, stop=True)\
                      .then_inc(s["cum"], 1)
                h = i - 2
                if h >= 0:
                    pe.wait_ge(s["masked"], h + 1)
                    c = h * HD
                    u = w[:, h % 2, :]
                    pe.matmul(core.banks[4][:, c:c + HD], u[:, 0:P], v[:, 0, c:c + HD], start=True, stop=True)
                    pe.matmul(core.banks[5][:, c:c + HD], u[:, P:T], v[:, 0, c:c + HD], start=True, stop=False)
                    pe.matmul(core.banks[5][:, c:c + HD], u[:, T:TRI], v[:, 1, c:c + HD], start=False,
                              stop=True).then_inc(s["summed"], 1)

        @block.vector
        def _(dve):
            for i in range(H + 1):
                h = i
                if h < H:
                    if h >= 2:
                        dve.wait_ge(s["log"], h - 1)
                        dve.wait_ge(s["soft"], h - 1)
                    dve.wait_ge(s["kept"], h + 1)
                    dve.scalar_tensor_tensor(out=small[:, h % 2, :], in0=z[:, h % 2, :], scalar=-1.0,
                                             in1=z[:, h % 2, :], op0=ALU.mult, op1=ALU.min)\
                       .then_inc(s["minus_abs"], 1)
                    dve.wait_ge(s["log"], h + 1)
                    if h >= 2:
                        dve.wait_ge(s["cum"], h - 1)
                    dve.scalar_tensor_tensor(out=sp_[:, h % 2, :], in0=z[:, h % 2, :], scalar=0.0,
                                             in1=small[:, h % 2, :], op0=ALU.max, op1=ALU.add)\
                       .then_inc(s["soft"], 1)
                h = i - 1
                if h >= 0:
                    dve.wait_ge(s["cum"], h + 1)
                    if h >= 2:
                        dve.wait_ge(s["summed"], h - 1)
                    dve.scalar_tensor_tensor(out=w[:, h % 2, :], in0=core.banks[2 + h % 2][:, 0:TRI], scalar=-1.0,
                                             in1=z[:, h % 2, :], op0=ALU.mult, op1=ALU.add).then_inc(s["diff"], 1)
            dve.wait_ge(s["summed"], H)
            dve.tensor_copy(out[:, 0, :], core.banks[4][:])

        @block.scalar
        def _(act):
            for i in range(H + 1):
                h = i
                if h < H:
                    act.wait_ge(s["scores"], h + 1)
                    if h >= 2:
                        act.wait_ge(s["diff"], h - 1)
                    act.copy(z[:, h % 2, :], core.banks[h % 2][:, 0:TRI]).then_inc(s["kept"], 1)
                    act.wait_ge(s["minus_abs"], h + 1)
                    act.activation(small[:, h % 2, :], small[:, h % 2, :], ACT.Exp).then_inc(s["exp"], 1)
                    act.wait_ge(s["exp"], h + 1)
                    act.activation(small[:, h % 2, :], small[:, h % 2, :], ACT.Ln, bias=1.0).then_inc(s["log"], 1)
                h = i - 1
                if h >= 0:
                    act.wait_ge(s["diff"], h + 1)
                    act.activation(w[:, h % 2, :], w[:, h % 2, :], ACT.Exp).then_inc(s["weights"], 1)
            act.wait_ge(s["summed"], H)
            act.copy(out[:, 1, :], core.banks[5][:])

        @block.gpsimd
        def _(pool):
            def strictly_later(a):
                for c in (0, T):
                    op = pool.affine_select(out=a[:, c:c + P], in_=a[:, c:c + P], pattern=[[1, P]],
                                            compare_op=ALU.is_gt, fill=0.0, base=0, channel_multiplier=-1)
                return op
            for i in range(H + 1):
                if i < H:
                    pool.wait_ge(s["soft"], i + 1)
                    strictly_later(sp_[:, i % 2, :]).then_inc(s["soft_masked"], 1)
                if i >= 1:
                    pool.wait_ge(s["weights"], i)
                    strictly_later(w[:, (i - 1) % 2, :]).then_inc(s["masked"], 1)


def decay_stage(core, tag, fl, b_forget, cT, tmp):
    nc = core.nc
    s = {n: core.sem(f"{tag}_{n}") for n in ("loaded", "step", "exp", "log", "soft", "sums")}
    b, u, e = tmp[:, 0:8], tmp[:, 8:24], tmp[:, 24:40]
    u2 = u.rearrange("p (t h) -> p t h", t=NT)
    with nc.Block() as block:
        @block.sync
        def _(sp):
            sp.dma_start(b, row_broadcast(b_forget)).then_inc(s["loaded"], 16)

        @block.vector
        def _(dve):
            dve.wait_ge(s["loaded"], 16)
            for t in range(NT):
                op = dve.tensor_tensor(u2[:, t, :], fl[:, t, :], b, ALU.add)
            op.then_inc(s["step"], 1)
            dve.wait_ge(s["step"], 1)
            dve.scalar_tensor_tensor(out=e, in0=u, scalar=-1.0, in1=u, op0=ALU.mult, op1=ALU.min).then_inc(s["step"], 1)
            dve.wait_ge(s["step"], 2)
            dve.tensor_scalar(u, u, -1.0, 0.0, ALU.mult, ALU.max).then_inc(s["step"], 1)
            dve.wait_ge(s["step"], 3)
            dve.wait_ge(s["log"], 1)
            dve.tensor_tensor(u, u, e, ALU.add).then_inc(s["soft"], 1)
            dve.wait_ge(s["sums"], 1)
            dve.tensor_copy(cT[0:8, :], core.banks[0][0:8, 0:T])

        @block.scalar
        def _(act):
            act.wait_ge(s["step"], 2)
            act.activation(e, e, ACT.Exp).then_inc(s["exp"], 1)
            act.wait_ge(s["exp"], 1)
            act.activation(e, e, ACT.Ln, bias=1.0).then_inc(s["log"], 1)

        @block.tensor
        def _(pe):
            pe.wait_ge(s["soft"], 1)
            bank = core.banks[0]
            pe.matmul(bank[0:8, 0:P], u2[:, 0, :], core.const("le"), start=True, stop=True)
            pe.matmul(bank[0:8, P:T], u2[:, 0, :], core.const("ones"), start=True, stop=False)
            pe.matmul(bank[0:8, P:T], u2[:, 1, :], core.const("le"), start=False, stop=True).then_inc(s["sums"], 1)


def angles_stage(core, positions, cos, sin, tmp):
    nc = core.nc
    s = {n: core.sem(f"angle_{n}") for n in ("loaded", "step", "done")}
    pos = tmp[:, 0:2].bitcast(I32)
    posf = tmp[:, 2:4]
    ang = tmp[:, 4:20].rearrange("p (t f) -> p t f", t=NT)
    turns = tmp[:, 20:36].rearrange("p (t f) -> p t f", t=NT)
    two_pi = (6.28125, 0.0019350051879882812, 3.019915981956753e-07)
    with nc.Block() as block:
        @block.sync
        def _(sp):
            sp.dma_start(pos, positions.rearrange("o (t p) -> p (o t)", p=P), allow_slow_non_contiguous=True)\
              .then_inc(s["loaded"], 16)

        @block.vector
        def _(dve):
            step = [0]

            def then(op):
                op.then_inc(s["step"], 1)
                step[0] += 1
                dve.wait_ge(s["step"], step[0])

            dve.wait_ge(s["loaded"], 16)
            then(dve.tensor_copy(posf, pos))
            for t in range(NT):
                then(dve.tensor_scalar(ang[:, t, :], core.const("freq"), posf[:, t:t + 1], None, ALU.mult))
            then(dve.tensor_scalar(turns, ang, 1.0 / (2.0 * np.pi), 12582912.0, ALU.mult, ALU.add))
            then(dve.tensor_scalar(turns, turns, 12582912.0, None, ALU.subtract))
            for c in two_pi:
                then(dve.scalar_tensor_tensor(out=ang, in0=turns, scalar=-c, in1=ang, op0=ALU.mult, op1=ALU.add))
            then(dve.tensor_scalar(sin, ang, np.pi - 1e-6, -np.pi + 1e-6, ALU.min, ALU.max))
            then(dve.tensor_scalar(ang, ang, np.pi / 2, None, ALU.add))
            then(dve.tensor_scalar(turns, ang, np.pi, -2.0 * np.pi, ALU.is_gt, ALU.mult))
            then(dve.tensor_tensor(ang, ang, turns, ALU.add))
            dve.tensor_scalar(cos, ang, np.pi - 1e-6, -np.pi + 1e-6, ALU.min, ALU.max).then_inc(s["done"], 1)

        @block.scalar
        def _(act):
            act.wait_ge(s["done"], 1)
            act.activation(sin, sin, ACT.Sin)
            act.activation(cos, cos, ACT.Sin)


def rope_stage(core, tag, proj, flat, cos, sin, tmp):
    nc = core.nc
    s = {n: core.sem(f"{tag}_{n}") for n in ("parts", "x1", "x2", "rotated")}
    half = ROT // 2
    with nc.Block() as block:
        @block.vector
        def _(dve):
            done = 0
            for a, b in ((8, ROPE_COLS[0]), ROPE_COLS[1:3]):
                n = (b - a) // HD
                for t in range(NT):
                    x = proj[:, t, a:b].rearrange("p (h d) -> p h d", d=HD)
                    x1, x2 = x[:, :, 0:half], x[:, :, half:ROT]
                    c = cos[:, t:t + 1, :].broadcast_to([P, n, half])
                    si = sin[:, t:t + 1, :].broadcast_to([P, n, half])
                    u = [tmp[:, i * 80:i * 80 + n * half].rearrange("p (h d) -> p h d", d=half) for i in range(4)]
                    if done:
                        dve.wait_ge(s["rotated"], done)
                    dve.tensor_tensor(u[0], x1, c, ALU.mult)
                    dve.tensor_tensor(u[1], x2, si, ALU.mult)
                    dve.tensor_tensor(u[2], x2, c, ALU.mult)
                    dve.tensor_tensor(u[3], x1, si, ALU.mult).then_inc(s["parts"], 1)
                    done += 1
                    dve.wait_ge(s["parts"], done)
                    dve.tensor_tensor(x1, u[0], u[1], ALU.subtract)
                    dve.tensor_tensor(x2, u[2], u[3], ALU.add).then_inc(s["rotated"], 1)

        @block.scalar
        def _(act):
            act.wait_ge(s["rotated"], 2 * NT)
            for t in range(NT):
                act.mul(flat[:, t, 0:512], proj[:, t, 8:520], HD ** -0.5)
                act.copy(flat[:, t, 768:1024], proj[:, t, 776:1032])

        @block.gpsimd
        def _(pool):
            pool.wait_ge(s["rotated"], 2 * NT)
            for t in range(NT):
                for g in range(2):
                    pool.tensor_copy(flat[:, t, 512 + P * g:512 + P * g + P].rearrange("p (r d) -> p r d", r=2),
                                     proj[:, t:t + 1, 520 + HD * g:584 + HD * g].broadcast_to([P, 2, HD]))
                pool.tensor_copy(flat[:, t, 1024:1152].rearrange("p (r d) -> p r d", r=2),
                                 proj[:, t:t + 1, 1032:1096].broadcast_to([P, 2, HD]))


def indexer_stage(core, tag, at, cT, wi, mask):
    nc = core.nc
    relu, at = core.part(at, 2, TRI)
    score, at = core.part(at, TRI)
    best, at = core.part(at, NT, 8)
    w, at = core.part(at, NT, 4)
    s = {n: core.sem(f"{tag}_{n}") for n in ("scaled", "dots", "relu", "added", "causal", "best", "taken", "chosen")}
    HI = 4
    edges = (0, P), (P, TRI)
    with nc.Block() as block:
        @block.tensor
        def _(pe):
            for h in range(HI):
                r = slice(HD * (h % 2), HD * (h % 2) + HD)
                for t, (a, b) in enumerate(edges):
                    mm = pe.matmul(core.banks[h][:, a:b], cT[r, 6 + h // 2, t * P:(t + 1) * P], cT[r, 8, 0:b - a],
                                   start=True, stop=True)
                mm.then_inc(s["dots"], 1)

        @block.scalar
        def _(act):
            for h in range(HI):
                act.wait_ge(s["dots"], h + 1)
                if h >= 2:
                    act.wait_ge(s["added"], NT * (h - 1))
                act.activation(relu[:, h % 2, :], core.banks[h][:, 0:TRI], ACT.Relu, scale=HD ** -0.5)\
                   .then_inc(s["relu"], 1)

        @block.vector
        def _(dve):
            dve.tensor_scalar(w, wi, HI ** -0.5, None, ALU.mult).then_inc(s["scaled"], 1)
            dve.wait_ge(s["scaled"], 1)
            for h in range(HI):
                dve.wait_ge(s["relu"], h + 1)
                if h:
                    dve.wait_ge(s["added"], NT * h)
                for t, (a, b) in enumerate(edges):
                    if h == 0:
                        op = dve.tensor_scalar(score[:, a:b], relu[:, 0, a:b], w[:, t, 0:1], None, ALU.mult)
                    else:
                        op = dve.scalar_tensor_tensor(out=score[:, a:b], in0=relu[:, h % 2, a:b],
                                                      scalar=w[:, t, h:h + 1], in1=score[:, a:b],
                                                      op0=ALU.mult, op1=ALU.add)
                    op.then_inc(s["added"], 1)
            dve.wait_ge(s["causal"], 1)
            for n in range(DSA_TOPK // 8):
                for t, (a, b) in enumerate(edges):
                    if n:
                        dve.wait_ge(s["taken"], NT * (n - 1) + t + 1)
                    dve.max(best[:, t, :], score[:, a:b]).then_inc(s["best"], 1)
                for t, (a, b) in enumerate(edges):
                    dve.wait_ge(s["best"], NT * n + t + 1)
                    dve.match_replace(score[:, a:b], best[:, t, :], score[:, a:b], TAKEN).then_inc(s["taken"], 1)
            dve.wait_ge(s["taken"], NT * DSA_TOPK // 8)
            dve.tensor_scalar(mask, score, -3.2e38, NEG, ALU.is_gt, ALU.mult).then_inc(s["chosen"], 1)
            dve.wait_ge(s["chosen"], 1)
            dve.tensor_tensor(mask, mask, core.const("neg"), ALU.add)

        @block.gpsimd
        def _(pool):
            pool.wait_ge(s["added"], NT * HI)
            for c in (0, T):
                op = pool.affine_select(out=score[:, c:c + P], in_=score[:, c:c + P], pattern=[[-1, P]],
                                        compare_op=ALU.is_ge, fill=MASKED, base=0, channel_multiplier=1)
                if c == 0:
                    continue
            op.then_inc(s["causal"], 1)


def gate_stage(core, tag, at, w, first, branches, y):
    nc = core.nc
    sig, at = core.part(at, 4, BANK)
    prod, at = core.part(at, 4, BANK)
    s = {n: core.sem(f"{tag}_{n}") for n in ("sigmoid", "product", "sum")}
    NB = len(branches)
    with nc.Block() as block:
        @block.sync
        def _(sp):
            w.refill(sp, first, first + 3 * NB)

        @block.tensor
        def _(pe):
            for b in range(NB):
                for half in range(2):
                    n = first + 3 * b + half
                    w.wait(pe, n)
                    if b:
                        pe.wait_ge(s["sigmoid"], 4 * b - 2 + 2 * half)
                    wt = w.tile(n, KC, BW)
                    for t in range(NT):
                        for c in range(KC):
                            mm = pe.matmul(core.banks[2 * half + t][:], core.xT[:, c, t * P:(t + 1) * P],
                                           wt[:, c, :], start=(c == 0), stop=(c == KC - 1))
                    mm.then_inc(w.tile_used, 1)
                n = first + 3 * b + 2
                w.wait(pe, n)
                if b:
                    pe.wait_ge(s["product"], 4 * b)
                wt = w.tile(n, BW // P, D)
                for half in range(2):
                    for t in range(NT):
                        for c in range(BW // P):
                            mm = pe.matmul(core.banks[4 + 2 * half + t][:], branches[b][:, c, t * P:(t + 1) * P],
                                           wt[:, c, half * BANK:(half + 1) * BANK], start=(c == 0),
                                           stop=(c == BW // P - 1))
                mm.then_inc(w.tile_used, 1)

        @block.scalar
        def _(act):
            for b in range(NB):
                for half in range(2):
                    act.wait_ge(w.tile_used, first + 3 * b + half + 1)
                    for t in range(NT):
                        if b:
                            act.wait_ge(s["product"], 4 * b - 3 + 2 * half + t)
                        act.activation(sig[:, 2 * half + t, :], core.banks[2 * half + t][:], ACT.Sigmoid)\
                           .then_inc(s["sigmoid"], 1)

        @block.vector
        def _(dve):
            for b in range(NB):
                dve.wait_ge(w.tile_used, first + 3 * b + 3)
                for half in range(2):
                    for t in range(NT):
                        n = 2 * half + t
                        dve.wait_ge(s["sigmoid"], 4 * b + n + 1)
                        if b >= 2:
                            dve.wait_ge(s["sum"], 4 * (b - 2) + n + 1)
                        out = y[:, t, half * BANK:(half + 1) * BANK] if b == 0 else prod[:, n, :]
                        dve.tensor_tensor(out, core.banks[4 + n][:], sig[:, n, :], ALU.mult)\
                           .then_inc(s["product"], 1)

        @block.gpsimd
        def _(pool):
            for b in range(1, NB):
                for n in range(4):
                    pool.wait_ge(s["product"], 4 * b + n + 1)
                    if b >= 2:
                        pool.wait_ge(s["sum"], 4 * (b - 2) + n + 1)
                    out = y[:, n % 2, (n // 2) * BANK:(n // 2 + 1) * BANK]
                    pool.tensor_tensor(out, out, prod[:, n, :], ALU.add).then_inc(s["sum"], 1)


def output_stage(core, tag, w, first, yT, alpha=None):
    nc = core.nc
    added = core.sem(f"{tag}_added")
    with nc.Block() as block:
        @block.sync
        def _(sp):
            w.refill(sp, first, first + 2)

        @block.tensor
        def _(pe):
            for half in range(2):
                w.wait(pe, first + half)
                wt = w.tile(first + half, KC, BW)
                for t in range(NT):
                    for c in range(KC):
                        mm = pe.matmul(core.banks[2 * half + t][:], yT[:, c, t * P:(t + 1) * P], wt[:, c, :],
                                       start=(c == 0), stop=(c == KC - 1))
                mm.then_inc(w.tile_used, 1)

        @block.vector
        def _(dve):
            for half in range(2):
                dve.wait_ge(w.tile_used, first + half + 1)
                for t in range(NT):
                    xs = core.x[:, t, half * BANK:(half + 1) * BANK]
                    add_to_x(dve, xs, core.banks[2 * half + t][:], alpha)


def add_to_x(dve, xs, more, alpha):
    if alpha is None:
        return dve.tensor_tensor(xs, more, xs, ALU.add)
    return dve.scalar_tensor_tensor(out=xs, in0=xs, scalar=alpha, in1=more, op0=ALU.mult, op1=ALU.add)


def down_products(pe, core, h, wt, chunks, first, last):
    for t in range(NT):
        for half in range(2):
            for c in range(chunks):
                mm = pe.matmul(core.banks[4 + 2 * t + half][:], h[:, c, t * P:(t + 1) * P],
                               wt[:, c, half * BANK:(half + 1) * BANK], start=(first and c == 0),
                               stop=(last and c == chunks - 1))
    return mm


def relu2_stage(core, tag, w, first):
    nc = core.nc
    n_f = D_FF // BW
    r, at = core.part(0, 2, SLOT // 4)
    hT, at = core.part(at, 2, SLOT // 4)
    h4 = [hT[:, i, :].rearrange("p (c t) -> p c t", t=T) for i in range(2)]
    s = {n: core.sem(f"{tag}_{n}") for n in ("relu", "square", "down")}

    def up(i):
        return first + (0 if i == 0 else 2 * i - 1)

    def down(i):
        return first + (2 * i + 2 if i < n_f - 1 else 2 * n_f - 1)

    with nc.Block() as block:
        @block.sync
        def _(sp):
            w.refill(sp, first, first + 2 * n_f)

        @block.tensor
        def _(pe):
            for i in range(n_f + 1):
                if i < n_f:
                    w.wait(pe, up(i))
                    if i >= 2:
                        pe.wait_ge(s["relu"], 2 * (i - 1))
                    wt = w.tile(up(i), KC, BW)
                    for half, bank in enumerate(pair(core, i)):
                        for f in range(2 * half, 2 * half + 2):
                            for c in range(KC):
                                mm = pe.matmul(bank[:, (f % 2) * T:(f % 2 + 1) * T], wt[:, c, f * P:(f + 1) * P],
                                               core.xT[:, c, :], start=(c == 0), stop=(c == KC - 1))
                    mm.then_inc(w.tile_used, 1)
                if i >= 1:
                    w.wait(pe, down(i - 1))
                    pe.wait_ge(s["square"], 2 * i)
                    down_products(pe, core, h4[(i - 1) % 2], w.tile(down(i - 1), BW // P, D), BW // P,
                                  i == 1, i == n_f).then_inc(w.tile_used, 1)

        @block.scalar
        def _(act):
            for i in range(n_f):
                act.wait_ge(w.tile_used, up(i) + 1 - first + first)
                for half in range(2):
                    if i >= 2:
                        act.wait_ge(s["square"], 2 * (i - 2) + half + 1)
                    act.activation(r[:, i % 2, half * BANK:(half + 1) * BANK], pair(core, i)[half][:], ACT.Relu)\
                       .then_inc(s["relu"], 1)

        @block.vector
        def _(dve):
            for i in range(n_f):
                for half in range(2):
                    dve.wait_ge(s["relu"], 2 * i + half + 1)
                    if i >= 2:
                        dve.wait_ge(w.tile_used, down(i - 2) + 1)
                    v = r[:, i % 2, half * BANK:(half + 1) * BANK]
                    dve.tensor_tensor(hT[:, i % 2, half * BANK:(half + 1) * BANK], v, v, ALU.mult)\
                       .then_inc(s["square"], 1)
            dve.wait_ge(w.tile_used, down(n_f - 1) + 1)
            for t in range(NT):
                for half in range(2):
                    xs = core.x[:, t, half * BANK:(half + 1) * BANK]
                    add_to_x(dve, xs, core.banks[4 + 2 * t + half][:], None)


def mlp_plan(steps, up, down):
    plan = [up(0)]
    for i in range(1, steps):
        plan += [up(i), down(i - 1)]
    return plan + [down(steps - 1)]


def layer(core, a, w, i):
    nc = core.nc
    norm_stage(core, "mix_norm", a["g_mix"][i], None, RMS_EPS, before=w.fill)
    brT = [None] * 3
    at = 0
    for b in range(3):
        brT[b], at = core.part(at, BW // P, T)
    br, at = core.part(at, NT, BW)
    qT, at = core.part(at, 4, T)
    kT, at = core.part(at, 4, T)
    v, at = core.part(at, NT, BW)
    projection_stage(core, "a_proj", w, [(0, "T", BW, keep_T(core, qT, HD ** -0.5)), (1, "T", BW, keep_T(core, kT)),
                                         (2, "N", BW, keep_N(core, v))])
    stick_stage(core, "stick", at, qT, kT, v, br)
    turn_stage(core, "a_turn", br, brT[0], BW // P)

    def c_cols(j):
        return core.cproj[:, :, j * BW:min(C_COLS, (j + 1) * BW)]

    projection_stage(core, "bc_proj", w, [(3, "T", BW, keep_T(core, qT, HD ** -0.5)), (4, "T", BW, keep_T(core, kT)),
                                          (5, "N", BW, keep_N(core, v))]
                     + [(6 + j, "N", c_cols(j).shape[2], keep_N(core, c_cols(j))) for j in range(3)])
    cum, at2 = core.part(at, T)
    tmp, at2 = core.part(at2, 40)
    decay_stage(core, "decay", core.cproj[:, :, 0:8], a["b_forget"][i], cum, tmp)

    def head_rows(x, chunk=lambda h: h // 2):
        return lambda h: x[HD * (h % 2):HD * (h % 2) + HD, chunk(h), :]

    softmax_stage(core, "forget", at2, 8, head_rows(qT), head_rows(kT),
                  lambda h, j: v[:, j, h * HD:(h + 1) * HD], lambda h, t: core.const("neg")[:, P * t:P + 2 * P * t], br,
                  bias=(lambda h: core.const("ident")[0:8, h:h + 1].broadcast_to([8, P]), cum[0:8, :]))
    turn_stage(core, "b_turn", br, brT[1], BW // P)

    at = 3 * (BW // P) * T + NT * BW
    flat, end = core.part(at, NT, 9 * P)
    tmp, end = core.part(end, 320)
    rope_stage(core, "rope", core.cproj, flat, core.cos, core.sin, tmp)
    cT, end = core.part(end, 9, T)
    turn_stage(core, "c_fold", flat, cT, 9)
    mask, free = core.part(at, TRI)
    indexer_stage(core, "index", free, cT, core.cproj[:, :, 1096:1100], mask)
    softmax_stage(core, "sparse", end, 8, head_rows(cT), head_rows(cT, lambda h: 4 + h // 4),
                  lambda h, j: core.cproj[:, j, 648 + HD * (h // 4):648 + HD * (h // 4) + HD],
                  lambda h, t: mask[:, P * t:P + 2 * P * t], br)
    turn_stage(core, "c_turn", br, brT[2], BW // P)

    y, at = core.part(3 * (BW // P) * T, NT, D)
    gate_stage(core, "gate", at, w, 9, brT, y)
    turn_stage(core, "y_turn", y, core.xT, KC, lambda t, c: y[:, t, c::KC])
    output_stage(core, "mix_out", w, 18, core.xT)
    norm_stage(core, "mlp_norm", a["g_mlp"][i], None, RMS_EPS)
    relu2_stage(core, "mlp", w, 20)
    tidy(core, core.sems)


def layer_plan(a, i):
    w_in = rows(a["w_in"][i], KC)
    cols = [(n, n + BW) for n in range(0, 6 * BW, BW)]
    cols += [(6 * BW + j * BW, 6 * BW + min(C_COLS, (j + 1) * BW)) for j in range(3)]
    plan = [(KC, [w_in[:, :, s:e]]) for s, e in cols]
    g = 6 * BW + C_COLS
    for b in range(3):
        for half in range(2):
            s = g + b * D + half * BW
            plan.append((KC, [w_in[:, :, s:s + BW]]))
        plan.append((BW // P, [rows_by_chunk(a["w_branch"][i, b])]))
    w_out = rows(a["w_out"][i], KC)
    plan += [(KC, [w_out[:, :, h * BW:(h + 1) * BW]]) for h in range(2)]
    w_up, w_down = rows(a["w_up"][i], KC), a["w_down"][i]
    plan += mlp_plan(D_FF // BW, lambda n: (KC, [w_up[:, :, n * BW:(n + 1) * BW]]),
                     lambda n: (BW // P, [rows_by_chunk(w_down[n * BW:(n + 1) * BW, :])]))
    return plan


def start_stage(core, a):
    loaded = core.sem("start_loaded")
    with core.nc.Block() as block:
        @block.sync
        def _(sp):
            sp.dma_start(core.consts[:], a["consts"]).then_inc(loaded, 16)
            sp.dma_start(core.x[:], a["x"].rearrange("o (t p) d -> p (o t) d", p=P)).then_inc(loaded, 16)
            sp.wait_ge(loaded, 32)


def end_stage(core, out):
    stored = core.sem("end_stored")
    with core.nc.Block() as block:
        @block.sync
        def _(sp):
            sp.dma_start(out.rearrange("o (t p) d -> p (o t) d", p=P), core.x[:]).then_inc(stored, 16)
            sp.wait_ge(stored, 16)


def build(nc, a, out, until=9, part=None):
    ctx = ExitStack()
    with ctx:
        core = Core(nc, ctx)
        core.cproj = core.sbuf("cproj", [P, NT, C_COLS])
        core.cos = core.sbuf("cos", [P, NT, ROT // 2])
        core.sin = core.sbuf("sin", [P, NT, ROT // 2])
        start_stage(core, a)
        tmp, _ = core.part(0, 36)
        angles_stage(core, a["positions"], core.cos, core.sin, tmp)
        if until != 2:
            with core.semaphores():
                first = Weights(core, "layer", 6, None)
                with nc.Fori(0, DEPTH) as i:
                    first.plan = layer_plan(a, i)
                    layer(core, a, first, i)
            norm_stage(core, "final", a["g_final"], None, RMS_EPS, out=core.x)
        else:
            turn_stage(core, "dbg", core.x, core.xT, KC, lambda t, c: core.x[:, t, c::KC])
        if until > 1:
            second_block(core, a, part)
        end_stage(core, out)


def gdn_stages(core, a, w):
    nc = core.nc
    free = core.ring[:, 2:7, :].rearrange("p a b -> p (a b)")
    at = [0]

    def extra(*shape):
        n = int(np.prod(shape))
        v = free[:, at[0]:at[0] + n]
        at[0] += n
        assert at[0] <= 5 * SLOT
        if len(shape) == 2:
            v = v.rearrange("p (a b) -> p a b", a=shape[0])
        if len(shape) == 3:
            v = v.rearrange("p (a b c) -> p a b c", a=shape[0], b=shape[1])
        return v

    raw, end = core.part(0, 16, PAD + T)
    z, end = core.part(end, NT, D)
    ba, end = core.part(end, NT, 16)
    conv = extra(16, T)

    def keep_raw(c0):
        return keep_T(core, raw[:, c0:c0 + 4, PAD:PAD + T])

    projection_stage(core, "gdn_proj", w, [(c, "T", BW, keep_raw(4 * c)) for c in range(4)]
                     + [(4 + h, "N", BW, keep_N(core, z[:, :, h * BW:(h + 1) * BW])) for h in range(2)]
                     + [(6, "N", 16, keep_N(core, ba))])
    wconv, end2 = core.part(end, CONV * 16)
    wload, end2 = core.part(end2, P)
    conv_stage(core, a, raw, conv, wload, wconv, z, ba)
    sq, end2 = core.part(end, 8, T)
    rn, end2 = core.part(end2, 8, T)
    qk_norm_stage(core, conv, sq, rn)
    kv, raw_end = core.part(0, NT, 12, P)
    order = [(b // 12, b % 12) for b in range(24)]
    turn_stage(core, "kv_turn", None, kv.rearrange("p t c d -> p (t c d)").rearrange("p (a b) -> p a b", b=T), 12,
               lambda t, c: conv[:, 4 + order[2 * c + t][1], order[2 * c + t][0] * P:(order[2 * c + t][0] + 1) * P])
    g = {}
    for name in ("g", "gc", "eg", "minus"):
        g[name], raw_end = core.part(raw_end, NT, 8)
    for name in ("last", "dec", "be", "alog", "dt"):
        g[name], raw_end = core.part(raw_end, 8)
    kbg, end2 = core.part(end, 8, P)
    kdec, end2 = core.part(end2, 8, P)
    qd, end2 = core.part(end2, 8, P)
    o, end2 = core.part(end2, NT, D)
    assert raw_end <= 16 * (PAD + T)
    beta = ba[:, :, 0:8]
    gdn_decay_stage(core, a, ba, beta, g, kv, kbg, kdec)
    AT, S, TT, qkT, kb = extra(16, P), extra(16, P), extra(16, P), extra(16, P), extra(16, P)
    W, B, DT = extra(4, 4, P), extra(4, 4, P), extra(4, 4, P)
    gdn_scores_stage(core, conv, beta, g, kb, qd, DT, AT, qkT)
    gdn_inverse_stage(core, AT, S, TT, W, B)
    vn, vn1 = kb, W.rearrange("p a b c -> p (a b) c")
    gdn_scan_stage(core, S, qkT, kv, kbg, kdec, qd, kb[:, 0:8, :], kb[:, 8:16, :], TT[:, 0:8, :], TT[:, 8:16, :], o)
    gdn_out_stage(core, a, o, z, sqo=AT.rearrange("p a b -> p (a b)"), st=core.part(end2, 16)[0],
                  nw=core.part(end2 + 16, P)[0])
    turn_stage(core, "gdn_turn", o, core.xT, KC, lambda t, c: o[:, t, c::KC])
    output_stage(core, "gdn_out", w, 7, core.xT, ALPHA)


def conv_stage(core, a, raw, conv, wload, wconv, z, ba):
    nc = core.nc
    s = {n: core.sem(f"conv_{n}") for n in ("loaded", "turned", "taps", "padded", "tap", "silu")}
    with nc.Block() as block:
        @block.sync
        def _(sp):
            sp.dma_start(wload[0:CONV * 16, :], a["a_conv_w_2"][0].rearrange("j (c p) -> (j c) p", p=P))\
              .then_inc(s["loaded"], 16)

        @block.tensor
        def _(pe):
            pe.wait_ge(s["loaded"], 16)
            pe.transpose(core.banks[0][:, 0:CONV * 16], wload[0:CONV * 16, :], core.const("ident")[0:64, 0:64])\
              .then_inc(s["turned"], 1)

        @block.vector
        def _(dve):
            dve.memset(raw[:, :, 0:PAD], 0.0).then_inc(s["padded"], 1)
            dve.wait_ge(s["padded"], 1)
            dve.wait_ge(s["turned"], 1)
            dve.tensor_copy(wconv, core.banks[0][:, 0:CONV * 16]).then_inc(s["taps"], 1)
            dve.wait_ge(s["taps"], 1)
            n = 0
            for group in range(4):
                for j in range(CONV):
                    for c in range(4 * group, 4 * group + 4):
                        tap = wconv[:, j * 16 + c:j * 16 + c + 1]
                        if j == 0:
                            op = dve.tensor_scalar(conv[:, c, :], raw[:, c, 0:T], tap, None, ALU.mult)
                        else:
                            dve.wait_ge(s["tap"], n - 3)
                            op = dve.scalar_tensor_tensor(out=conv[:, c, :], in0=raw[:, c, j:j + T], scalar=tap,
                                                          in1=conv[:, c, :], op0=ALU.mult, op1=ALU.add)
                        op.then_inc(s["tap"], 1)
                        n += 1

        @block.scalar
        def _(act):
            act.activation(ba[:, :, 0:8], ba[:, :, 0:8], ACT.Sigmoid)
            for t in range(NT):
                act.activation(z[:, t, :], z[:, t, :], ACT.Silu)
            for group in range(4):
                act.wait_ge(s["tap"], 16 * (group + 1))
                act.activation(conv[:, 4 * group:4 * group + 4, :], conv[:, 4 * group:4 * group + 4, :], ACT.Silu)


def qk_norm_stage(core, conv, sq, rn):
    nc = core.nc
    s = {n: core.sem(f"qknorm_{n}") for n in ("squares", "sums", "shifted", "root", "inverse")}
    with nc.Block() as block:
        @block.gpsimd
        def _(pool):
            for c in range(8):
                pool.tensor_tensor(sq[:, c, :], conv[:, c, :], conv[:, c, :], ALU.mult).then_inc(s["squares"], 1)

        @block.tensor
        def _(pe):
            for n in range(4):
                pe.wait_ge(s["squares"], 2 * (n + 1))
                pe.matmul(core.banks[n][:], core.const("ones"), sq[:, 2 * n:2 * n + 2, :].rearrange("p a b -> p (a b)"),
                          start=True, stop=True).then_inc(s["sums"], 1)

        @block.vector
        def _(dve):
            for n in range(4):
                dve.wait_ge(s["sums"], n + 1)
                dve.tensor_scalar(rn[:, 2 * n:2 * n + 2, :].rearrange("p a b -> p (a b)"), core.banks[n][:], GDN_EPS,
                                  None, ALU.add).then_inc(s["shifted"], 1)
            for n in range(4):
                v = rn[:, 2 * n:2 * n + 2, :]
                dve.wait_ge(s["root"], n + 1)
                dve.reciprocal(v, v).then_inc(s["inverse"], 1)
                dve.wait_ge(s["inverse"], n + 1)
                q = conv[:, 2 * n:2 * n + 2, :]
                dve.scalar_tensor_tensor(out=q, in0=v, scalar=GDK ** -0.5 if n < 2 else 1.0, in1=q, op0=ALU.mult,
                                         op1=ALU.mult)

        @block.scalar
        def _(act):
            for n in range(4):
                act.wait_ge(s["shifted"], n + 1)
                v = rn[:, 2 * n:2 * n + 2, :]
                act.activation(v, v, ACT.Sqrt).then_inc(s["root"], 1)


def gdn_decay_stage(core, a, ba, beta, g, kv, kbg, kdec):
    nc = core.nc
    s = {n: core.sem(f"gdecay_{n}") for n in ("loaded", "exp", "step", "log", "g", "sums", "exps")}
    u = ba[:, :, 8:16]
    with nc.Block() as block:
        @block.sync
        def _(sp):
            sp.dma_start(g["alog"], row_broadcast(a["a_a_log_2"][0])).then_inc(s["loaded"], 16)
            sp.dma_start(g["dt"], row_broadcast(a["a_dt_bias_2"][0])).then_inc(s["loaded"], 16)

        @block.scalar
        def _(act):
            act.wait_ge(s["loaded"], 32)
            act.activation(g["alog"], g["alog"], ACT.Exp).then_inc(s["exp"], 1)
            act.wait_ge(s["step"], 2)
            act.activation(g["minus"], g["minus"], ACT.Exp).then_inc(s["exp"], 1)
            act.wait_ge(s["exp"], 2)
            act.activation(g["minus"], g["minus"], ACT.Ln, bias=1.0).then_inc(s["log"], 1)
            act.wait_ge(s["exps"], 1)
            act.activation(g["eg"], g["gc"], ACT.Exp).then_inc(s["exp"], 1)
            act.activation(g["dec"], g["dec"], ACT.Exp).then_inc(s["exp"], 1)

        @block.vector
        def _(dve):
            step = [0]

            def then(op):
                op.then_inc(s["step"], 1)
                step[0] += 1
                dve.wait_ge(s["step"], step[0])

            dve.wait_ge(s["loaded"], 32)
            then(dve.tensor_tensor(u, u, g["dt"].rearrange("p (o h) -> p o h", o=1).broadcast_to([P, NT, 8]), ALU.add))
            then(dve.scalar_tensor_tensor(out=g["minus"], in0=u, scalar=-1.0, in1=u, op0=ALU.mult, op1=ALU.min))
            dve.wait_ge(s["log"], 1)
            then(dve.scalar_tensor_tensor(out=g["g"], in0=u, scalar=0.0, in1=g["minus"], op0=ALU.max, op1=ALU.add))
            dve.wait_ge(s["exp"], 1)
            dve.scalar_tensor_tensor(out=g["g"], in0=g["g"], scalar=-1.0,
                                     in1=g["alog"].rearrange("p (o h) -> p o h", o=1).broadcast_to([P, NT, 8]),
                                     op0=ALU.mult, op1=ALU.mult).then_inc(s["g"], 1)
            dve.wait_ge(s["sums"], 1)
            then(dve.tensor_copy(g["gc"], core.banks[0][:, 0:16].rearrange("p (t h) -> p t h", t=NT)))
            then(dve.tensor_copy(g["last"], core.banks[0][:, 16:24]))
            dve.tensor_tensor(g["dec"], g["last"], g["gc"][:, 0, :], ALU.subtract).then_inc(s["exps"], 1)
            for t in range(NT):
                dve.tensor_tensor(kv[:, t, 4:12, :], kv[:, t, 4:12, :],
                                  beta[:, t, :].rearrange("p (h o) -> p h o", o=1).broadcast_to([P, 8, P]), ALU.mult)
            dve.wait_ge(s["exp"], 4)
            then(dve.tensor_tensor(g["be"], g["eg"][:, 1, :], beta[:, 1, :], ALU.mult))
            for out, t, factor in ((kbg, 1, g["be"]), (kdec, 0, g["dec"])):
                for r in range(2):
                    dve.tensor_tensor(out[:, r::2, :], kv[:, t, 0:4, :],
                                      factor[:, r::2].rearrange("p (h o) -> p h o", o=1).broadcast_to([P, 4, P]),
                                      ALU.mult)

        @block.tensor
        def _(pe):
            pe.wait_ge(s["g"], 1)
            gs = g["g"].rearrange("p t h -> p (t h)")
            pe.matmul(core.banks[0][:, 0:16], core.const("le"), gs, start=True, stop=True)
            pe.matmul(core.banks[0][:, 16:24], core.const("ones"), gs[:, 0:8], start=True, stop=True)\
              .then_inc(s["sums"], 1)


def gdn_scores_stage(core, conv, beta, g, kb, qd, DT, AT, qkT):
    nc = core.nc
    s = {n: core.sem(f"gscore_{n}") for n in ("rows", "diff", "decay", "kb", "qd_exp", "dots", "AT", "qk")}
    groups = [(n // 2, 4 * (n % 2)) for n in range(4)]
    with nc.Block() as block:
        @block.tensor
        def _(pe):
            def row_sums(n):
                t, h0 = groups[n]
                if n >= 1:
                    pe.wait_ge(s["kb"], n)
                    pe.wait_ge(s["diff"], n)
                    if n >= 3:
                        pe.wait_ge(s["qd_exp"], n - 2)
                for h in range(4):
                    pe.matmul(core.banks[0][:, h * P:(h + 1) * P], g["g"][:, t, h0 + h:h0 + h + 1].broadcast_to([P, P]),
                              core.const("le"), start=True, stop=True)
                for h in range(4):
                    mm = pe.matmul(core.banks[1][:, h * P:(h + 1) * P],
                                   beta[:, t, h0 + h:h0 + h + 1].broadcast_to([P, P]), core.const("ident"),
                                   start=True, stop=True)
                mm.then_inc(s["rows"], 1)

            for n, (t, h0) in enumerate(groups):
                row_sums(n)
                pe.wait_ge(s["kb"], n + 1)
                if n >= 2:
                    pe.wait_ge(s["AT"], n - 1)
                    pe.wait_ge(s["qk"], n - 1)
                ts = slice(t * P, (t + 1) * P)
                for h in range(4):
                    k = conv[:, 4 + (h0 + h) // 2, ts]
                    pe.matmul(core.banks[2 + 2 * (n % 2)][:, h * P:(h + 1) * P], k, kb[:, 4 * n + h, :], start=True,
                              stop=True)
                    mm = pe.matmul(core.banks[3 + 2 * (n % 2)][:, h * P:(h + 1) * P], k, conv[:, (h0 + h) // 2, ts],
                                   start=True, stop=True)
                mm.then_inc(s["dots"], 1)

        @block.vector
        def _(dve):
            def scores(n):
                bank = 2 + 2 * (n % 2)
                dve.wait_ge(s["dots"], n + 1)
                dve.wait_ge(s["decay"], n + 1)
                d = DT[:, n, :, :].rearrange("p a b -> p (a b)")
                dve.tensor_tensor(AT[:, 4 * n:4 * n + 4, :].rearrange("p a b -> p (a b)"), core.banks[bank][:], d,
                                  ALU.mult).then_inc(s["AT"], 1)
                dve.tensor_tensor(qkT[:, 4 * n:4 * n + 4, :].rearrange("p a b -> p (a b)"), core.banks[bank + 1][:],
                                  d, ALU.mult).then_inc(s["qk"], 1)

            for n, (t, h0) in enumerate(groups):
                dve.wait_ge(s["rows"], n + 1)
                for j in range(2):
                    k = conv[:, 4 + h0 // 2 + j:5 + h0 // 2 + j, t * P:(t + 1) * P].broadcast_to([P, 2, P])
                    op = dve.tensor_tensor(kb[:, 4 * n + 2 * j:4 * n + 2 * j + 2, :],
                                           core.banks[1][:, 2 * j * P:(2 * j + 2) * P]
                                           .rearrange("p (a b) -> p a b", a=2), k, ALU.mult)
                op.then_inc(s["kb"], 1)
                for h in range(4):
                    op = dve.tensor_scalar(DT[:, n, h, :], core.banks[0][:, h * P:(h + 1) * P],
                                           g["gc"][:, t, h0 + h:h0 + h + 1], 0.0, ALU.subtract, ALU.min)
                op.then_inc(s["diff"], 1)
                scores(n)
            for n in (2, 3):
                dve.wait_ge(s["qd_exp"], n - 1)
                h0 = groups[n][1]
                for j in range(2):
                    out = qd[:, h0 + 2 * j:h0 + 2 * j + 2, :]
                    dve.tensor_tensor(out, out, conv[:, h0 // 2 + j:h0 // 2 + j + 1, P:T].broadcast_to([P, 2, P]),
                                      ALU.mult)

        @block.scalar
        def _(act):
            for n, (t, h0) in enumerate(groups):
                act.wait_ge(s["diff"], n + 1)
                if t == 1:
                    act.activation(qd[:, h0:h0 + 4, :].rearrange("p a b -> p (a b)"), core.banks[0][:], ACT.Exp)\
                       .then_inc(s["qd_exp"], 1)
                act.activation(DT[:, n, :, :], DT[:, n, :, :], ACT.Exp).then_inc(s["decay"], 1)

        @block.gpsimd
        def _(pool):
            for n in range(4):
                for x, name, keep in ((AT, "AT", ALU.is_gt), (qkT, "qk", ALU.is_ge)):
                    pool.wait_ge(s[name], n + 1)
                    v = x[:, 4 * n:4 * n + 4, :]
                    pool.affine_select(out=v, in_=v, pattern=[[0, 4], [1, P]], compare_op=keep, fill=0.0, base=0,
                                       channel_multiplier=-1)


def gdn_inverse_stage(core, AT, S, TT, W, B):
    nc = core.nc
    s = {n: core.sem(f"ginv_{n}") for n in ("masked", "S0", "T_turned", "T0", "W_dots", "W", "TWT", "SWS", "T", "S")}
    grp = [slice(4 * n, 4 * n + 4) for n in range(4)]

    def flat(x):
        return x.rearrange("p a b -> p (a b)")

    def each(k):
        return core.level(k).rearrange("p (o m) -> p o m", o=1).broadcast_to([P, 4, P])

    with nc.Block() as block:
        @block.gpsimd
        def _(pool):
            for k in range(LEVELS):
                for n in range(4):
                    if k >= 1:
                        pool.wait_ge(s["S0"], n + 1) if k == 1 else pool.wait_ge(s["W_dots"], 4 * (k - 2) + n + 1)
                    pool.tensor_tensor(B[:, n, :, :], AT[:, grp[n], :], each(k), ALU.mult).then_inc(s["masked"], 1)

        @block.tensor
        def _(pe):
            for n in range(4):
                pe.wait_ge(s["S0"], n + 1)
                for h in range(4):
                    mm = pe.transpose(core.banks[n][:, h * P:(h + 1) * P], S[:, 4 * n + h, :], core.const("ident"))
                mm.then_inc(s["T_turned"], 1)
            for k in range(1, LEVELS):
                for n in range(4):
                    pe.wait_ge(s["masked"], 4 * k + n + 1)
                    if k == 1:
                        pe.wait_ge(s["T0"], n + 1)
                        pe.wait_ge(s["T0"], min(4, n + 3))
                    else:
                        pe.wait_ge(s["T"], 4 * (k - 2) + n + 1)
                    if n >= 2 or k >= 2:
                        m = 4 * (k - 1) + n
                        pe.wait_ge(s["W"], m - 1)
                    for h in range(4):
                        mm = pe.matmul(core.banks[n % 2][:, h * P:(h + 1) * P], B[:, n, h, :], TT[:, 4 * n + h, :],
                                       start=True, stop=True)
                    mm.then_inc(s["W_dots"], 1)
                for n in range(4):
                    m = 4 * (k - 1) + n
                    pe.wait_ge(s["W"], m + 1)
                    if m >= 2:
                        pe.wait_ge(s["S"], m - 1)
                    if k < LEVELS - 1:
                        for h in range(4):
                            mm = pe.matmul(core.banks[2 + n % 2][:, h * P:(h + 1) * P], S[:, 4 * n + h, :],
                                           W[:, n, h, :], start=True, stop=True)
                        mm.then_inc(s["TWT"], 1)
                    for h in range(4):
                        mm = pe.matmul(core.banks[4 + n % 2][:, h * P:(h + 1) * P], W[:, n, h, :],
                                       S[:, 4 * n + h, :], start=True, stop=True)
                    mm.then_inc(s["SWS"], 1)

        @block.scalar
        def _(act):
            for k in range(1, LEVELS):
                for n in range(4):
                    act.wait_ge(s["W_dots"], 4 * (k - 1) + n + 1)
                    if k >= 2:
                        act.wait_ge(s["SWS"], 4 * (k - 2) + n + 1)
                    act.copy(flat(W[:, n, :, :]), core.banks[n % 2][:]).then_inc(s["W"], 1)

        @block.vector
        def _(dve):
            for n in range(4):
                dve.wait_ge(s["masked"], n + 1)
                dve.tensor_tensor(S[:, grp[n], :], core.const("ident").rearrange("p (o m) -> p o m", o=1)
                                  .broadcast_to([P, 4, P]), B[:, n, :, :], ALU.subtract).then_inc(s["S0"], 1)
            for n in range(4):
                dve.wait_ge(s["T_turned"], n + 1)
                dve.tensor_copy(flat(TT[:, grp[n], :]), core.banks[n][:]).then_inc(s["T0"], 1)
            for k in range(1, LEVELS):
                for n in range(4):
                    m = 4 * (k - 1) + n
                    dve.wait_ge(s["SWS"], m + 1)
                    if k < LEVELS - 1:
                        dve.wait_ge(s["TWT"], m + 1)
                        dve.tensor_tensor(flat(TT[:, grp[n], :]), flat(TT[:, grp[n], :]), core.banks[2 + n % 2][:],
                                          ALU.subtract).then_inc(s["T"], 1)
                    dve.tensor_tensor(flat(S[:, grp[n], :]), flat(S[:, grp[n], :]), core.banks[4 + n % 2][:],
                                      ALU.subtract).then_inc(s["S"], 1)


def gdn_scan_stage(core, S, qkT, kv, kbg, kdec, qd, vn0, vn1, state, wT, o):
    nc = core.nc
    s = {n: core.sem(f"gscan_{n}") for n in ("u0", "vn0", "w", "wT", "s1", "state", "u1", "vn1", "o0", "o1")}

    def flat(x):
        return x.rearrange("p a b -> p (a b)")

    with nc.Block() as block:
        @block.tensor
        def _(pe):
            def per_head(bank, g, products, sem):
                for h in range(4 * g, 4 * g + 4):
                    ps = products(h)
                    for i, (lhs, rhs) in enumerate(ps):
                        mm = pe.matmul(bank[:, (h % 4) * P:(h % 4 + 1) * P], lhs, rhs, start=(i == 0),
                                       stop=(i == len(ps) - 1))
                mm.then_inc(s[sem], 1)

            for g in range(2):
                per_head(core.banks[g], g, lambda h: [(S[:, h, :], kv[:, 0, 4 + h, :])], "u0")
            for g in range(2):
                per_head(core.banks[2 + g], g, lambda h: [(kbg[:, h, :], S[:, 8 + h, :])], "w")
            for g in range(2):
                pe.wait_ge(s["vn0"], g + 1)
                per_head(core.banks[4 + g], g, lambda h: [(kdec[:, h, :], vn0[:, h, :])], "s1")
            for g in range(2):
                per_head(core.banks[6 + g], g, lambda h: [(qkT[:, h, :], vn0[:, h, :])], "o0")
            for g in range(2):
                pe.wait_ge(s["state"], g + 1)
                pe.wait_ge(s["wT"], g + 1)
                per_head(core.banks[g], g, lambda h: [(S[:, 8 + h, :], kv[:, 1, 4 + h, :]),
                                                      (wT[:, h, :], state[:, h, :])], "u1")
            for g in range(2):
                pe.wait_ge(s["vn1"], g + 1)
                per_head(core.banks[2 + g], g, lambda h: [(qkT[:, 8 + h, :], vn1[:, h, :]),
                                                          (qd[:, h, :], state[:, h, :])], "o1")

        @block.vector
        def _(dve):
            for g in range(2):
                dve.wait_ge(s["u0"], g + 1)
                dve.tensor_copy(flat(vn0[:, 4 * g:4 * g + 4, :]), core.banks[g][:]).then_inc(s["vn0"], 1)
            for g in range(2):
                dve.wait_ge(s["s1"], g + 1)
                dve.tensor_copy(flat(state[:, 4 * g:4 * g + 4, :]), core.banks[4 + g][:]).then_inc(s["state"], 1)
            for g in range(2):
                dve.wait_ge(s["u1"], g + 1)
                dve.tensor_copy(flat(vn1[:, 4 * g:4 * g + 4, :]), core.banks[g][:]).then_inc(s["vn1"], 1)
            for g in range(2):
                dve.wait_ge(s["o1"], g + 1)
                dve.tensor_copy(o[:, 1, g * BANK:(g + 1) * BANK], core.banks[2 + g][:])

        @block.scalar
        def _(act):
            for g in range(2):
                act.wait_ge(s["w"], g + 1)
                act.mul(flat(wT[:, 4 * g:4 * g + 4, :]), core.banks[2 + g][:], -1.0).then_inc(s["wT"], 1)
            for g in range(2):
                act.wait_ge(s["o0"], g + 1)
                act.copy(o[:, 0, g * BANK:(g + 1) * BANK], core.banks[6 + g][:])


def gdn_out_stage(core, a, o, z, sqo, st, nw):
    nc = core.nc
    s = {n: core.sem(f"gout_{n}") for n in ("loaded", "square", "sum", "mean", "root", "inverse", "step", "gated")}
    oh = o.rearrange("p t (h d) -> p (t h) d", d=P)
    sqh = sqo.rearrange("p (n d) -> p n d", d=P)
    nwb = nw.rearrange("p (o d) -> p o d", o=1).broadcast_to([P, 8, P])
    with nc.Block() as block:
        @block.sync
        def _(sp):
            sp.dma_start(nw, row_broadcast(a["a_norm_w_2"][0])).then_inc(s["loaded"], 16)

        @block.gpsimd
        def _(pool):
            pool.wait_ge(s["loaded"], 16)
            for t in range(NT):
                pool.wait_ge(s["square"], t + 1)
                v = z[:, t, :].rearrange("p (h d) -> p h d", d=P)
                pool.tensor_tensor(v, v, nwb, ALU.mult).then_inc(s["gated"], 1)

        @block.scalar
        def _(act):
            for t in range(NT):
                act.activation(sqo[:, t * D:(t + 1) * D], o[:, t, :], ACT.Square).then_inc(s["square"], 1)
            act.wait_ge(s["mean"], 1)
            act.activation(st, st, ACT.Sqrt).then_inc(s["root"], 1)

        @block.vector
        def _(dve):
            for t in range(NT):
                dve.wait_ge(s["square"], t + 1)
                dve.reduce_sum(st[:, 8 * t:8 * t + 8], sqh[:, 8 * t:8 * t + 8, :], AX_X).then_inc(s["sum"], 1)
            dve.wait_ge(s["sum"], NT)
            dve.tensor_scalar(st, st, 1.0 / P, GDN_EPS, ALU.mult, ALU.add).then_inc(s["mean"], 1)
            dve.wait_ge(s["root"], 1)
            dve.reciprocal(st, st).then_inc(s["inverse"], 1)
            dve.wait_ge(s["inverse"], 1)
            for t in range(NT):
                v = oh[:, 8 * t:8 * t + 8, :]
                dve.tensor_tensor(v, v, st[:, 8 * t:8 * t + 8].rearrange("p (h o) -> p h o", o=1)
                                  .broadcast_to([P, 8, P]), ALU.mult).then_inc(s["step"], 1)
            for t in range(NT):
                dve.wait_ge(s["step"], t + 1)
                dve.wait_ge(s["gated"], t + 1)
                dve.tensor_tensor(o[:, t, :], o[:, t, :], z[:, t, :], ALU.mult)


def swiglu_stage(core, tag, w, first, steps):
    nc = core.nc
    sg, at = core.part(0, 2, BW)
    hT, at = core.part(at, 2, BW)
    s = {n: core.sem(f"{tag}_{n}") for n in ("silu", "hidden")}

    def up(i):
        return first + (0 if i == 0 else 2 * i - 1)

    def down(i):
        return first + (2 * i + 2 if i < steps - 1 else 2 * steps - 1)

    with nc.Block() as block:
        @block.sync
        def _(sp):
            w.refill(sp, first, first + 2 * steps)

        @block.tensor
        def _(pe):
            for i in range(steps + 1):
                if i < steps:
                    w.wait(pe, up(i))
                    if i >= 2:
                        pe.wait_ge(s["hidden"], i - 1)
                    wt = w.tile(up(i), KC, 2 * FB)
                    for half, bank in enumerate(pair(core, i)):
                        for f in range(2):
                            for c in range(KC):
                                mm = pe.matmul(bank[:, f * T:(f + 1) * T], wt[:, c, (2 * half + f) * P:(2 * half + f + 1) * P],
                                               core.xT[:, c, :], start=(c == 0), stop=(c == KC - 1))
                    mm.then_inc(w.tile_used, 1)
                if i >= 1:
                    w.wait(pe, down(i - 1))
                    pe.wait_ge(s["hidden"], i)
                    h = hT[:, (i - 1) % 2, :].rearrange("p (c t) -> p c t", t=T)
                    down_products(pe, core, h, w.tile(down(i - 1), 2, D), 2, i == 1, i == steps)\
                        .then_inc(w.tile_used, 1)

        @block.scalar
        def _(act):
            for i in range(steps):
                act.wait_ge(w.tile_used, up(i) + 1)
                if i >= 2:
                    act.wait_ge(s["hidden"], i - 1)
                act.activation(sg[:, i % 2, :], pair(core, i)[0][:], ACT.Silu).then_inc(s["silu"], 1)

        @block.vector
        def _(dve):
            for i in range(steps):
                dve.wait_ge(s["silu"], i + 1)
                if i >= 2:
                    dve.wait_ge(w.tile_used, down(i - 2) + 1)
                dve.tensor_tensor(hT[:, i % 2, :], sg[:, i % 2, :], pair(core, i)[1][:], ALU.mult)\
                   .then_inc(s["hidden"], 1)
            dve.wait_ge(w.tile_used, down(steps - 1) + 1)
            for t in range(NT):
                for half in range(2):
                    xs = core.x[:, t, half * BANK:(half + 1) * BANK]
                    add_to_x(dve, xs, core.banks[4 + 2 * t + half][:], ALPHA)


def swa_bias_stage(core, a, rows_, bias, rel, bq, bk, bv, sink):
    nc = core.nc
    s = {n: core.sem(f"band_{n}") for n in ("loaded", "row", "windowed", "stored", "biases", "done", "scaled")}
    scratch = nc.dram_tensor("band_rows", [P, SWA_HEADS, TRI], F32).ap()
    b = a["b_b_in_2"][0]
    q_dim = SWA_HEADS * HD
    with nc.Block() as block:
        @block.sync
        def _(sp):
            sp.dma_start(rel[0:BUCKETS, :], a["rel_bias_2"]).then_inc(s["loaded"], 16)
            sp.dma_start(sink, row_broadcast(a["b_sinks_2"][0])).then_inc(s["biases"], 16)
            sp.dma_start(bq, b[0:q_dim].rearrange("(c p) -> p c", p=P), allow_slow_non_contiguous=True)\
              .then_inc(s["biases"], 16)
            for r in range(2):
                sp.dma_start(bk[HD * r:HD * r + HD, :], b[q_dim:q_dim + P].rearrange("(c p) -> p c", p=HD),
                             allow_slow_non_contiguous=True).then_inc(s["biases"], 16)
            sp.dma_start(bv, row_broadcast(b[q_dim + P:q_dim + 2 * P])).then_inc(s["biases"], 16)
            sp.wait_ge(s["windowed"], 1)
            sp.dma_start(scratch.rearrange("i h v -> h i v"),
                         rows_[0:SWA_HEADS, :].rearrange("h (o v) -> h o v", o=1).broadcast_to([SWA_HEADS, P, TRI]))\
              .then_inc(s["stored"], 16)
            sp.wait_ge(s["stored"], 16)
            sp.dma_start(bias, bass.AP(scratch.tensor, P - 1, [[SWA_HEADS * TRI - 1, P], [TRI, SWA_HEADS], [1, T]]))\
              .then_inc(s["done"], 16)
            sp.wait_ge(s["done"], 16)
            sp.wait_ge(s["biases"], 16 * 5)

        @block.tensor
        def _(pe):
            pe.wait_ge(s["loaded"], 16)
            pe.matmul(core.banks[0][0:SWA_HEADS, 0:TRI], rel[0:BUCKETS, :], core.const("bucket")[0:BUCKETS, :],
                      start=True, stop=True).then_inc(s["row"], 1)

        @block.vector
        def _(dve):
            dve.wait_ge(s["row"], 1)
            dve.tensor_tensor(rows_[0:SWA_HEADS, :], core.banks[0][0:SWA_HEADS, 0:TRI],
                              core.const("window")[0:SWA_HEADS, :], ALU.add).then_inc(s["windowed"], 1)
            dve.wait_ge(s["biases"], 16 * 5)
            dve.tensor_scalar(bq, bq, HD ** -0.5, None, ALU.mult)


def swa_stages(core, a, w, first):
    qT, at = core.part(0, 8, T)
    kT, at = core.part(at, 2, T)
    v, at = core.part(at, NT, P)
    bias, at = core.part(at, SWA_HEADS, T)
    out, at = core.part(at, NT, D)
    rows_, _ = core.part(at, TRI)
    rel, end = core.part(at + TRI, SWA_HEADS)
    small = core.cproj[:, 0, :]
    bq, bk, bv, sink = small[:, 0:8], small[:, 8:10], small[:, 16:144], small[:, 144:160]
    swa_bias_stage(core, a, rows_, bias, rel, bq, bk, bv, sink)

    def with_bias(dst, cols, c0, factor):
        def store(eng, half, bank):
            for j in range(2):
                c = c0 + 2 * half + j
                out_, in_ = dst[:, c, :], bank[:, j * T:(j + 1) * T]
                if eng is core.nc.scalar:
                    op = eng.activation(out_, in_, ACT.Identity, bias=cols[:, c:c + 1], scale=factor)
                else:
                    op = eng.tensor_scalar(out_, in_, factor, cols[:, c:c + 1], ALU.mult, ALU.add)
            return op
        return store

    def keep_kv(eng, half, bank):
        if half == 0:
            return with_bias(kT, bk, 0, 1.0)(eng, 0, bank)
        for t in range(NT):
            op = eng.tensor_tensor(v[:, t, :], bank[:, t * P:(t + 1) * P], bv, ALU.add)
        return op

    projection_stage(core, "swa_proj", w, [(first, "T", BW, with_bias(qT, bq, 0, HD ** -0.5)),
                                           (first + 1, "T", BW, with_bias(qT, bq, 4, HD ** -0.5)),
                                           (first + 2, "KV", 3 * P, keep_kv)])
    softmax_stage(core, "swa", at, SWA_HEADS, lambda h: qT[HD * (h % 2):HD * (h % 2) + HD, h // 2, :],
                  lambda h: kT[HD * (h % 2):HD * (h % 2) + HD, h // 8, :],
                  lambda h, j: v[:, j, (h // 8) * HD:(h // 8 + 1) * HD],
                  lambda h, t: bias[:, h, P:T] if t == 0 else bias[:, h, :], out, sink=sink)
    turn_stage(core, "swa_turn", out, core.xT, KC, lambda t, c: out[:, t, c::KC])
    output_stage(core, "swa_out", w, first + 3, core.xT, ALPHA)


def router_stage(core, a, r, acc):
    nc = core.nc
    s = {n: core.sem(f"route_{n}") for n in ("loaded", "logits", "step", "exp", "chosen", "ranks")}
    lg, top, oh, sel = r["logits"], r["top"], r["onehot"], r["sel"]
    with nc.Block() as block:
        @block.sync
        def _(sp):
            sp.dma_start(r["w"], rows(a["moe_router_2"][0], KC)).then_inc(s["loaded"], 16)

        @block.tensor
        def _(pe):
            pe.wait_ge(s["loaded"], 16)
            for t in range(NT):
                for c in range(KC):
                    mm = pe.matmul(core.banks[0][:, E * t:E * t + E], core.xT[:, c, t * P:(t + 1) * P], r["w"][:, c, :],
                                   start=(c == 0), stop=(c == KC - 1))
            mm.then_inc(s["logits"], 1)
            pe.wait_ge(s["chosen"], 1)
            bank = core.banks[1]
            pe.matmul(bank[:, 0:E], core.const("lt"), sel[:, 0, :], start=True, stop=True)
            pe.matmul(bank[:, E:2 * E], core.const("lt"), sel[:, 1, :], start=True, stop=False)
            pe.matmul(bank[:, E:2 * E], core.const("ones"), sel[:, 0, :], start=False, stop=True)
            pe.matmul(bank[:, 2 * E:3 * E], core.const("ones"), sel[:, 0, :], start=True, stop=False)
            pe.matmul(bank[:, 2 * E:3 * E], core.const("ones"), sel[:, 1, :], start=False, stop=True)\
              .then_inc(s["ranks"], 1)

        @block.scalar
        def _(act):
            for t in range(NT):
                act.mul(acc[:, t, :], core.x[:, t, :], ALPHA)
            act.wait_ge(s["exp"], 1)
            act.activation(r["e"], r["e"], ACT.Exp).then_inc(s["exp"], 1)

        @block.vector
        def _(dve):
            step = [0]

            def then(op):
                op.then_inc(s["step"], 1)
                step[0] += 1
                dve.wait_ge(s["step"], step[0])

            dve.wait_ge(s["logits"], 1)
            then(dve.tensor_copy(lg.rearrange("p t e -> p (t e)"), core.banks[0][:, 0:NT * E]))
            for t in range(NT):
                then(dve.max(top[:, t, :], lg[:, t, :]))
                then(dve.max_index(r["index"][:, t, :], top[:, t, :], lg[:, t, :]))
            dve.tensor_tensor(r["e"], top[:, :, 1:2].rearrange("p t o -> p (t o)"),
                              top[:, :, 0:1].rearrange("p t o -> p (t o)"), ALU.subtract).then_inc(s["exp"], 1)
            then(dve.tensor_copy(r["indexf"], r["index"]))
            dve.wait_ge(s["exp"], 2)
            then(dve.tensor_scalar(r["p"], r["e"], 1.0, None, ALU.add))
            then(dve.reciprocal(r["p"], r["p"]))
            then(dve.tensor_tensor(r["e"], r["e"], r["p"], ALU.mult))
            for t in range(NT):
                for i, weight in ((0, r["p"]), (1, r["e"])):
                    then(dve.tensor_scalar(oh[:, t, i, :], core.const("expert"), r["indexf"][:, t, i:i + 1], None,
                                           ALU.is_equal))
                    then(dve.tensor_scalar(r["part"][:, t, i, :], oh[:, t, i, :], weight[:, t:t + 1], None, ALU.mult))
                then(dve.tensor_tensor(r["gates"][:, t, :], r["part"][:, t, 0, :], r["part"][:, t, 1, :], ALU.add))
                op = dve.tensor_tensor(sel[:, t, :], oh[:, t, 0, :], oh[:, t, 1, :], ALU.add)
                if t == 0:
                    then(op)
            op.then_inc(s["chosen"], 1)
            dve.wait_ge(s["chosen"], 1)
            dve.wait_ge(s["ranks"], 1)
            ranks = core.banks[1][:, 0:NT * E].rearrange("p (t e) -> p t e", t=NT)
            then(dve.scalar_tensor_tensor(out=r["rank"], in0=ranks, scalar=1.0, in1=sel, op0=ALU.add, op1=ALU.mult))
            then(dve.tensor_scalar(r["rank"], r["rank"], -1.0, None, ALU.add))
            then(dve.tensor_reduce(r["busiest"], core.banks[1][:, 2 * E:3 * E], AX_X, ALU.max))
            then(dve.tensor_scalar(r["count"], r["busiest"], 0.5, None, ALU.is_gt))
            for n in range(1, ROUNDS):
                then(dve.tensor_scalar(r["more"], r["busiest"], float(n * CAP), None, ALU.is_gt))
                then(dve.tensor_tensor(r["count"], r["count"], r["more"], ALU.add))
            then(dve.tensor_copy(r["rounds"], r["count"]))


def moe_plan(a, e, following):
    def plan(e):
        g, u = rows(a["moe_w_gate_2"][0, e], KC), rows(a["moe_w_up_2"][0, e], KC)
        d = a["moe_w_down_2"][0, e]
        return mlp_plan(EXPERT_DIM // FB,
                        lambda n: (KC, [g[:, :, n * FB:(n + 1) * FB], u[:, :, n * FB:(n + 1) * FB]]),
                        lambda n: (2, [rows_by_chunk(d[n * FB:(n + 1) * FB, :])]))
    return plan(e) + plan(following)[0:7]


def expert_stage(core, w, e, r, acc):
    nc = core.nc
    steps = EXPERT_DIM // FB
    n_tiles = 2 * steps
    pick, at = core.part(r["end"], NT, CAP)
    weigh, at = core.part(at, NT, CAP)
    weighT, at = core.part(at, NT, P)
    xe, at = core.part(at, KC, CAP)
    sg, at = core.part(at, 2, 2 * CAP)
    hT, at = core.part(at, 2, 2, CAP)
    ye, at = core.part(at, D)
    s = r["sems"]

    def up(i):
        return 0 if i == 0 else 2 * i - 1

    def down(i):
        return 2 * i + 2 if i < steps - 1 else 2 * steps - 1

    def gathered(c):
        return core.banks[6 + c // 4][:, (c % 4) * CAP:(c % 4 + 1) * CAP]

    with nc.Block() as block:
        @block.sync
        def _(sp):
            w.refill(sp, 0, n_tiles)

        @block.tensor
        def _(pe):
            pe.wait_ge(s["picked"], NT)
            for c in range(KC):
                for t in range(NT):
                    mm = pe.matmul(gathered(c), core.x[:, t, c::KC], pick[:, t, :], start=(t == 0), stop=(t == NT - 1))
                if c % 4 == 3:
                    mm.then_inc(s["gathered"], 1)
            pe.wait_ge(s["weighed"], NT)
            for t in range(NT):
                mm = pe.transpose(core.banks[3][0:CAP, t * P:(t + 1) * P], weigh[:, t, :], core.const("ident"))
            mm.then_inc(s["weigh_turned"], 1)
            pe.wait_ge(s["xe"], 2)
            for i in range(steps + 1):
                if i < steps:
                    w.wait(pe, up(i))
                    if i == 1:
                        pe.wait_ge(s["weighT"], 1)
                    if i >= 2:
                        pe.wait_ge(s["hidden"], i - 1)
                    wt = w.tile(up(i), KC, 2 * FB)
                    for half, bank in enumerate(pair(core, i)):
                        for f in range(2):
                            for c in range(KC):
                                mm = pe.matmul(bank[:, f * CAP:(f + 1) * CAP],
                                               wt[:, c, (2 * half + f) * P:(2 * half + f + 1) * P], xe[:, c, :],
                                               start=(c == 0), stop=(c == KC - 1))
                    mm.then_inc(w.tile_used, 1)
                if i >= 1:
                    w.wait(pe, down(i - 1))
                    pe.wait_ge(s["hidden"], i)
                    wt = w.tile(down(i - 1), 2, D)
                    for half in range(2):
                        for c in range(2):
                            mm = pe.matmul(core.banks[4 + half][0:CAP, :], hT[:, (i - 1) % 2, c, :],
                                           wt[:, c, half * BANK:(half + 1) * BANK], start=(i == 1 and c == 0),
                                           stop=(i == steps and c == 1))
                    mm.then_inc(w.tile_used, 1)
            pe.wait_ge(s["ye"], 2)
            for t in range(NT):
                for half in range(2):
                    mm = pe.matmul(core.banks[2 * t + half][:], weighT[0:CAP, t, :],
                                   ye[0:CAP, half * BANK:(half + 1) * BANK], start=True, stop=True)
            mm.then_inc(s["spread"], 1)

        @block.scalar
        def _(act):
            act.wait_ge(s["gathered"], 1)
            act.copy(xe[:, 0:4, :].rearrange("p a b -> p (a b)"), core.banks[6][:, 0:4 * CAP]).then_inc(s["xe"], 1)
            act.wait_ge(s["weigh_turned"], 1)
            act.copy(weighT[0:CAP, :, :].rearrange("p a b -> p (a b)"), core.banks[3][0:CAP, 0:NT * P])\
               .then_inc(s["weighT"], 1)
            for i in range(steps):
                act.wait_ge(w.tile_used, up(i) + 1)
                if i >= 2:
                    act.wait_ge(s["hidden"], i - 1)
                act.activation(sg[:, i % 2, :], pair(core, i)[0][:, 0:2 * CAP], ACT.Silu).then_inc(s["silu"], 1)
            act.wait_ge(w.tile_used, n_tiles)
            act.copy(ye[0:CAP, 0:BANK], core.banks[4][0:CAP, :]).then_inc(s["ye"], 1)

        @block.vector
        def _(dve):
            for t in range(NT):
                dve.tensor_scalar(pick[:, t, :], core.const("slot"), r["rank"][:, t, bass.ds(e, 1)], None,
                                  ALU.is_equal).then_inc(s["picked"], 1)
            for t in range(NT):
                dve.wait_ge(s["picked"], t + 1)
                dve.tensor_scalar(weigh[:, t, :], pick[:, t, :], r["gates"][:, t, bass.ds(e, 1)], None,
                                  ALU.mult).then_inc(s["weighed"], 1)
            dve.wait_ge(s["gathered"], 2)
            dve.tensor_copy(xe[:, 4:8, :].rearrange("p a b -> p (a b)"), core.banks[7][:, 0:4 * CAP])\
               .then_inc(s["xe"], 1)
            for i in range(steps):
                dve.wait_ge(s["silu"], i + 1)
                if i >= 2:
                    dve.wait_ge(w.tile_used, down(i - 2) + 1)
                dve.tensor_tensor(hT[:, i % 2, :, :].rearrange("p a b -> p (a b)"), sg[:, i % 2, :],
                                  pair(core, i)[1][:, 0:2 * CAP], ALU.mult).then_inc(s["hidden"], 1)
            dve.wait_ge(w.tile_used, n_tiles)
            dve.tensor_copy(ye[0:CAP, BANK:D], core.banks[5][0:CAP, :]).then_inc(s["ye"], 1)
            dve.wait_ge(s["spread"], 1)
            for t in range(NT):
                for half in range(2):
                    v = acc[:, t, half * BANK:(half + 1) * BANK]
                    dve.tensor_tensor(v, v, core.banks[2 * t + half][:], ALU.add)

    with nc.Block() as block:
        @block.sync
        def _(sp):
            for x in [*s.values(), w.tile_used]:
                sp.sem_clear(x)
            for slot in range(w.slots):
                used = sum(len(w.plan[n][1]) for n in range(slot, n_tiles, w.slots))
                sp.sem_inc(w.landed[slot], -16 * used)


def moe_stages(core, a):
    nc = core.nc
    at = 0
    r = {}
    acc, at = core.part(at, NT, D)
    for name, shape in (("w", (KC, E)), ("logits", (NT, E)), ("top", (NT, 8)), ("index", (NT, 8)), ("indexf", (NT, 8)),
                        ("onehot", (NT, 2, E)), ("part", (NT, 2, E)), ("sel", (NT, E)), ("gates", (NT, E)),
                        ("rank", (NT, E)), ("e", (NT,)), ("p", (NT,)), ("busiest", (1,)), ("count", (1,)),
                        ("more", (1,)), ("rounds", (1,))):
        r[name], at = core.part(at, *shape)
    r["index"], r["rounds"] = r["index"].bitcast(U32), r["rounds"].bitcast(I32)
    r["end"] = at
    router_stage(core, a, r, acc)
    w = Weights(core, "moe", 7, moe_plan(a, 0, 0))
    r["sems"] = {n: core.sem(f"moe_{n}") for n in ("picked", "weighed", "gathered", "weigh_turned", "xe", "weighT",
                                                   "silu", "hidden", "ye", "spread")}
    with nc.Block() as block:
        @block.sync
        def _(sp):
            w.fill(sp)
    rounds = nc.values_load(r["rounds"][0:1, 0:1], min_val=1, max_val=ROUNDS,
                            skip_runtime_bounds_check_because="a sum of ROUNDS comparisons, the first always true")
    stepped = core.sem("moe_stepped")
    with nc.Fori(0, rounds):
        with nc.Fori(0, E) as e:
            w.plan = moe_plan(a, e, (e + 1) % E)
            expert_stage(core, w, e, r, acc)
        with nc.Block() as block:
            @block.vector
            def _(dve):
                dve.tensor_scalar(r["rank"], r["rank"], float(-CAP), None, ALU.add).then_inc(stepped, 1)
        tidy(core, [stepped])
    with nc.Block() as block:
        @block.sync
        def _(sp):
            for n in range(7):
                sp.wait_ge(w.landed[n], 16 * len(w.plan[n][1]))

        @block.vector
        def _(dve):
            for t in range(NT):
                dve.tensor_copy(core.x[:, t, :], acc[:, t, :])


def second_block(core, a, part=None):
    with core.semaphores():
        gdn = Weights(core, "gdn", 7, None)
        w_in = rows(a["a_w_in_2"][0], KC)
        w_out = rows(a["a_w_out_2"][0], KC)
        edges = [(c, min(c + BW, 3088)) for c in range(0, 3088, BW)]
        gdn.plan = [(KC, [w_in[:, :, s:e]]) for s, e in edges] + [(KC, [w_out[:, :, h * BW:(h + 1) * BW]]) for h in range(2)]
        mid = Weights(core, "mid", 7, None)
        g, u = rows(a["ffn_w_gate_2"][0], KC), rows(a["ffn_w_up_2"][0], KC)
        d = a["ffn_w_down_2"][0]
        mid.plan = mlp_plan(FFN_DIM // FB, lambda n: (KC, [g[:, :, n * FB:(n + 1) * FB], u[:, :, n * FB:(n + 1) * FB]]),
                            lambda n: (2, [rows_by_chunk(d[n * FB:(n + 1) * FB, :])]))
        swa_first = len(mid.plan)
        b_in, b_out = rows(a["b_w_in_2"][0], KC), rows(a["b_w_out_2"][0], KC)
        q_dim = SWA_HEADS * HD
        mid.plan += [(KC, [b_in[:, :, h * BW:(h + 1) * BW]]) for h in range(2)]
        ks = [b_in[:, :, q_dim + HD * (j // 2):q_dim + HD * (j // 2) + HD] for j in range(4)]
        mid.plan += [(KC, ks + [b_in[:, :, q_dim + P:q_dim + 2 * P]])]
        mid.plan += [(KC, [b_out[:, :, h * BW:(h + 1) * BW]]) for h in range(2)]

        ln_g, ln_b = a["ln_g_2"], a["ln_b_2"]
        with core.nc.Block() as block:
            @block.sync
            def _(sp):
                gdn.fill(sp)
        gdn_stages(core, a, gdn)
        norm_stage(core, "ln00", ln_g[0, 0], ln_b[0, 0], LN_EPS, out=core.x, before=mid.fill)
        if part == "gdn":
            return
        swiglu_stage(core, "ffn", mid, 0, FFN_DIM // FB)
        norm_stage(core, "ln01", ln_g[0, 1], ln_b[0, 1], LN_EPS, out=core.x)
        if part == "ffn":
            return
        swa_stages(core, a, mid, swa_first)
        norm_stage(core, "ln10", ln_g[1, 0], ln_b[1, 0], LN_EPS, out=core.x)
        if part == "swa":
            return
        tidy(core, core.sems)
    moe_stages(core, a)
    norm_stage(core, "ln11", ln_g[1, 1], ln_b[1, 1], LN_EPS, out=core.x)


def kernel(**inputs):
    import concourse.bacc as bacc
    from concourse.bass_utils import run_bass_kernel_spmd

    nc = bacc.Bacc("TRN2", target_bir_lowering=False, num_devices=1)
    arrays, args = {}, {}
    for name, value in [*inputs.items(), ("consts", CONSTS)]:
        value = np.ascontiguousarray(value)
        arrays[f"in_{name}"] = value
        args[name] = nc.dram_tensor(f"in_{name}", value.shape, mybir.dt.from_np(value.dtype),
                                    kind="ExternalInput").ap()
    out = nc.dram_tensor("out", (1, T, D), F32, kind="ExternalOutput").ap()
    build(nc, args, out)
    r = run_bass_kernel_spmd(nc, [arrays], core_ids=[0])
    return r.results[0]["out"]
```

```python
from contextlib import ExitStack, contextmanager

import numpy as np

import concourse.bass as bass
from concourse import mybir

F32 = mybir.dt.float32
F32R = mybir.dt.float32r
I32 = mybir.dt.int32
U32 = mybir.dt.uint32
ALU = mybir.AluOpType
ACT = mybir.ActivationFunctionType
AX_X = mybir.AxisListType.X

P = 128
T = 256
NT = T // P
D = 1024
KC = D // P
DEPTH = 2
HD = 64
BW = 512
BANK = 512
SLOT = KC * BW
SLOTS = 6
MOE_SLOTS = 4
ARENA = 15232
MOE_ARENA = 6400
LOWER, UPPER = 8192, 8064
TRI = 3 * P
NEG = -1.0e30
MASKED = -3.0e38
TAKEN = -3.4e38
DSA_TOPK = T // 4
ROPE_THETA, ROT = 500000.0, 16
ROPE_COLS = 8 + 640, 776, 1096
C_COLS = 1100
D_FF = 4096
RMS_EPS, LN_EPS, GDN_EPS = 1e-6, 1e-5, 1e-6
ALPHA = (2.0 * DEPTH) ** 0.25
GK_HEADS, GV_HEADS, GDK = 4, 8, 128
CONV = 4
PAD = CONV - 1
GDN_LOWER = 16 * (PAD + T) + NT * D + NT * 16
GDN_UPPER = 8448
SWA_HEADS, SWA_WINDOW = 16, 128
BUCKETS, MAX_DIST = 32, 128
FFN_DIM, EXPERT_DIM, E = 2816, 3584, 8
FB = 256
CAP = 128
ROUNDS = -(-T // CAP)
UNITS = 4
PER = 2
LAG = 2
LEVELS = 7


def constants():
    p = np.arange(P)[:, None]
    m = np.arange(P)[None, :]
    parts = {
        "ident": p == m, "ones": p >= 0 * m, "le": p <= m, "lt": p < m, "ge": p >= m,
        "neg": np.concatenate([np.where(m > p, NEG, 0), 0.0 * (p + m), np.where(m > p, NEG, 0)], 1),
        "level": np.concatenate([(p // (2 << k) == m // (2 << k)) & (m % (2 << k) >= 1 << k)
                                 & (p % (2 << k) < 1 << k) for k in range(LEVELS)], 1),
        "freq": np.tile((ROPE_THETA ** (-np.arange(0, ROT, 2, dtype=np.float32) / ROT)).astype(np.float32), (P, 1)),
        "slot": np.tile(np.arange(CAP), (P, 1)),
        "expert": np.tile(np.arange(E), (P, 1)),
    }
    v = np.arange(TRI)
    dist = (2 * P - 1) - v
    exact = BUCKETS // 2
    df = np.maximum(dist, 1).astype(np.float32)
    large = exact + (np.log(df / np.float32(exact)) / np.float32(np.log(MAX_DIST / exact))
                     * (BUCKETS - exact)).astype(np.int32)
    bucket = np.where(dist < exact, dist, np.minimum(large, BUCKETS - 1))
    ok = (dist >= 0) & (dist < SWA_WINDOW)
    onehot = np.zeros((P, TRI))
    onehot[:BUCKETS] = (bucket[None] == np.arange(BUCKETS)[:, None]) & ok[None]
    parts["bucket"] = onehot
    parts["window"] = np.tile(np.where(ok, 0.0, NEG), (P, 1))
    at, cols = {}, 0
    for name, a in parts.items():
        at[name] = (cols, a.shape[1])
        cols += a.shape[1]
    return np.concatenate([np.asarray(a, np.float32) for a in parts.values()], 1).copy(), at


CONSTS, CONST_AT = constants()


class Core:

    def __init__(self, nc, ctx):
        self.nc, self.ctx = nc, ctx
        self.consts = self.sbuf("consts", [P, CONSTS.shape[1]])
        self.x = self.sbuf("x", [P, NT, D])
        self.xT = self.sbuf("xT", [P, KC, T])
        self.banks = [ctx.enter_context(nc.psum_tensor(f"bank{i}", [P, BANK], F32)) for i in range(8)]
        self.scope, self.sems = ctx, []
        self.arenas = []

    def sbuf(self, name, shape, dt=F32):
        return self.ctx.enter_context(self.nc.sbuf_tensor(name, shape, dt))[:]

    @contextmanager
    def weight_ring(self, name, slots):
        with self.nc.sbuf_tensor(f"{name}_ring", [P, slots, SLOT], F32) as ring:
            self.ring = ring[:]
            yield

    @contextmanager
    def scratch(self, name, size=ARENA, start=0):
        outer = self.arenas
        with self.nc.sbuf_tensor(f"{name}_arena", [P, size], F32) as arena:
            self.arenas = outer + [(start, arena[:])]
            yield
        self.arenas = outer

    def sem(self, name):
        s = self.scope.enter_context(self.nc.semaphore(name))
        self.sems.append(s)
        return s

    @contextmanager
    def semaphores(self):
        outer, self.sems = (self.scope, self.sems), []
        with ExitStack() as self.scope:
            yield self.sems
        self.scope, self.sems = outer

    def const(self, name):
        a, n = CONST_AT[name]
        return self.consts[:, a:a + n]

    def level(self, k):
        a = CONST_AT["level"][0] + k * P
        return self.consts[:, a:a + P]

    def part(self, at, *shape):
        n = int(np.prod(shape))
        start, arena = [(s, a) for s, a in self.arenas if s <= at][-1]
        assert at + n <= start + arena.shape[1], (at, n)
        v = arena[:, at - start:at - start + n]
        if len(shape) == 2:
            v = v.rearrange("p (a b) -> p a b", a=shape[0])
        if len(shape) == 3:
            v = v.rearrange("p (a b c) -> p a b c", a=shape[0], b=shape[1])
        return v, at + n


class Weights:

    def __init__(self, core, tag, slots, plan):
        self.core, self.slots, self.plan = core, slots, plan
        self.landed = [core.sem(f"{tag}_landed{i}") for i in range(slots)]
        self.tile_used = core.sem(f"{tag}_tile_used")

    def tile(self, n, chunks, cols):
        return self.core.ring[:, n % self.slots, 0:chunks * cols].rearrange("p (c n) -> p c n", c=chunks)

    def load(self, sp, n):
        chunks, parts = self.plan[n]
        cols = sum(a.shape[2] for a in parts)
        at = 0
        for i, a in enumerate(parts):
            w = a.shape[2]
            dma = sp.dma_start(self.tile(n, chunks, cols)[:, :, at:at + w], a)
            at += w
            dma.then_inc(self.landed[n % self.slots], 16)

    def fill(self, sp, first=0, last=None):
        for n in range(first, self.slots if last is None else last):
            self.load(sp, n)

    def refill(self, sp, first, last):
        for n in range(first, last):
            if n + self.slots < len(self.plan):
                sp.wait_ge(self.tile_used, n + 1)
                self.load(sp, n + self.slots)

    def wait(self, pe, n):
        before = sum(len(self.plan[i][1]) for i in range(n % self.slots, n + 1, self.slots))
        pe.wait_ge(self.landed[n % self.slots], 16 * before)


def rows(a, chunks):
    return a.rearrange("(p k) n -> p k n", k=chunks)


def rows_by_chunk(a):
    return a.rearrange("(k p) n -> p k n", p=P)


def tidy(core, sems, last=None):
    sems = list(sems)
    with core.nc.Block() as block:
        @block.sync
        def _(sp):
            for s in sems[0::4]:
                sp.sem_clear(s)
            if last is not None:
                last(sp)

        @block.vector
        def _(dve):
            for s in sems[1::4]:
                dve.sem_clear(s)

        @block.scalar
        def _(act):
            for s in sems[2::4]:
                act.sem_clear(s)

        @block.gpsimd
        def _(pool):
            for s in sems[3::4]:
                pool.sem_clear(s)


def row_broadcast(a):
    return a.rearrange("(o n) -> o n", o=1).broadcast_to([P, a.shape[0]])


class Affine:
    NAMES = ("final", "ln00", "ln01", "ln10", "ln11")

    def __init__(self, core, a):
        self.core = core
        self.gain = core.sbuf("gain_columns", [P, len(self.NAMES), KC])
        self.shift = core.sbuf("shift_columns", [P, len(self.NAMES), KC])
        self.rows = core.sbuf("affine_rows", [P, 2, D])
        self.fetched = core.sem("affine_fetched")
        self.count = 0
        ln = [(a["ln_g_2"][i, j], a["ln_b_2"][i, j]) for i in range(2) for j in range(2)]
        self.sources = dict(zip(self.NAMES, [(a["g_final"], None)] + ln))

    def load_columns(self, sp, a, loaded):
        sp.dma_start(self.gain[:, 0, :], a["g_final"].rearrange("(p k) -> p k", k=KC)).then_inc(loaded, 16)
        for dst, name in ((self.gain, "ln_g_2"), (self.shift, "ln_b_2")):
            sp.dma_start(dst[:, 1:5, :], a[name].rearrange("i j (p k) -> p (i j) k", k=KC)).then_inc(loaded, 16)

    def fetch(self, sp, name):
        for i, source in enumerate(self.sources[name]):
            if source is not None:
                sp.dma_start(self.rows[:, i, :], row_broadcast(source)).then_inc(self.fetched, 16)
                self.count += 16


def norm_stage(core, tag, eps, gain, shift=None, natural=False, before=None, pool_first=None,
               vectors=None):
    nc = core.nc
    y, at = core.part(0, NT, D)
    stats, at = core.part(at, NT, 12)
    mv, at = core.part(at, NT, 2)
    rstd, at = core.part(at, NT, 1)
    warm, at = core.part(at, 1)
    x = core.x
    rms = shift is None
    s = {n: core.sem(f"{tag}_{n}") for n in ("squares", "mean_square", "variance", "root", "inverse", "normed",
                                               "turned", "gained0", "gained1")}

    def natural_tile(eng, t):
        eng.wait_ge(core.affine.fetched, core.affine.count)
        eng.wait_ge(s["normed"], NT)
        op = eng.tensor_tensor(x[:, t, :], y[:, t, :], core.affine.rows[:, 0, :], ALU.mult)
        if not rms:
            gained = s[f"gained{t}"]
            op.then_inc(gained, 1)
            eng.wait_ge(gained, 1)
            eng.tensor_tensor(x[:, t, :], x[:, t, :], core.affine.rows[:, 1, :], ALU.add)

    with nc.Block() as block:
        @block.sync
        def _(sp):
            if before is not None:
                before(sp)

        @block.scalar
        def _(act):
            act.activation(warm, core.const("ident")[:, 0:1], ACT.Sqrt)
            for t in range(NT):
                act.wait_ge(s["variance"], t + 1)
                act.activation(rstd[:, t, :], mv[:, t, 1:2], ACT.Sqrt).then_inc(s["root"], 1)
            if vectors is not None:
                act.wait_ge(*vectors)
            for bank in range(0, 4, 2):
                act.wait_ge(s["turned"], bank + 1)
                for c in range(2):
                    k = 2 * bank + c
                    in_ = core.banks[bank][:, c * T:(c + 1) * T]
                    if rms:
                        act.mul(core.xT[:, k, :], in_, gain[:, k:k + 1])
                    else:
                        act.activation(core.xT[:, k, :], in_, ACT.Identity, bias=shift[:, k:k + 1],
                                       scale=gain[:, k:k + 1])

        @block.vector
        def _(dve):
            for t in range(NT):
                for half in range(2):
                    dve.bn_stats(stats[:, t, 6 * half:6 * half + 6],
                                 x[:, t, half * BANK:(half + 1) * BANK]).then_inc(s["squares"], 1)
                dve.wait_ge(s["squares"], 3 * t + 2)
                dve.bn_aggr(mv[:, t, :], stats[:, t, :]).then_inc(s["squares"], 1)
                dve.wait_ge(s["squares"], 3 * t + 3)
                mean, variance = mv[:, t, 0:1], mv[:, t, 1:2]
                if rms:
                    dve.scalar_tensor_tensor(out=mean, in0=mean, scalar=mean, in1=variance, op0=ALU.mult,
                                             op1=ALU.add).then_inc(s["mean_square"], 1)
                    dve.wait_ge(s["mean_square"], t + 1)
                dve.tensor_scalar(variance, mean if rms else variance, eps, None, ALU.add).then_inc(s["variance"], 1)
            for t in range(NT):
                dve.wait_ge(s["root"], t + 1)
                dve.reciprocal(rstd[:, t, :], rstd[:, t, :]).then_inc(s["inverse"], 1)
                dve.wait_ge(s["inverse"], t + 1)
                if rms:
                    op = dve.tensor_scalar(y[:, t, :], x[:, t, :], rstd[:, t, :], None, ALU.mult)
                else:
                    op = dve.tensor_scalar(y[:, t, :], x[:, t, :], mv[:, t, 0:1], rstd[:, t, :], ALU.subtract, ALU.mult)
                op.then_inc(s["normed"], 1)
            if vectors is not None:
                dve.wait_ge(*vectors)
            for bank in range(1, 4, 2):
                dve.wait_ge(s["turned"], bank + 1)
                for c in range(2):
                    k = 2 * bank + c
                    in_ = core.banks[bank][:, c * T:(c + 1) * T]
                    if rms:
                        dve.tensor_scalar(core.xT[:, k, :], in_, gain[:, k:k + 1], None, ALU.mult)
                    else:
                        dve.tensor_scalar(core.xT[:, k, :], in_, gain[:, k:k + 1], shift[:, k:k + 1], ALU.mult, ALU.add)
            if natural:
                natural_tile(dve, 1)

        @block.gpsimd
        def _(pool):
            if pool_first is not None:
                pool_first(pool)
            if natural:
                natural_tile(pool, 0)

        @block.tensor
        def _(pe):
            for t in range(NT):
                pe.wait_ge(s["normed"], t + 1)
                for k in range(KC):
                    mm = pe.transpose(core.banks[k // 2][:, (k % 2) * T + t * P:(k % 2) * T + (t + 1) * P],
                                      y[:, t, k::KC], core.const("ident"))
                    if t == NT - 1 and k % 2:
                        mm.then_inc(s["turned"], 1)


def pair(core, n):
    return core.banks[2 * (n % 2)], core.banks[2 * (n % 2) + 1]


def projection_stage(core, tag, w, jobs, before=None):
    nc = core.nc
    act_stored = core.sem(f"{tag}_act_stored")
    dve_stored = core.sem(f"{tag}_dve_stored")
    first, last = jobs[0][0], jobs[-1][0] + 1
    with nc.Block() as block:
        @block.sync
        def _(sp):
            if before is not None:
                before(sp)
            w.refill(sp, first, last)

        @block.tensor
        def _(pe):
            for n, (tile, form, cols, store) in enumerate(jobs):
                w.wait(pe, tile)
                if n >= 2:
                    pe.wait_ge(act_stored, n - 1)
                    pe.wait_ge(dve_stored, n - 1)
                wt = w.tile(tile, KC, sum(a.shape[2] for a in w.plan[tile][1]))
                for half, bank in enumerate(pair(core, n)):
                    if form == "KV" and half == 1:
                        for t in range(NT):
                            for c in range(KC):
                                mm = pe.matmul(bank[:, t * P:(t + 1) * P], core.xT[:, c, t * P:(t + 1) * P],
                                               wt[:, c, 2 * P:3 * P], start=(c == 0), stop=(c == KC - 1))
                    elif form == "N":
                        for c in range(KC):
                            mm = pe.matmul(bank[:, 0:cols], core.xT[:, c, half * P:(half + 1) * P],
                                           wt[:, c, 0:cols], start=(c == 0), stop=(c == KC - 1))
                    else:
                        for f in range(2 * half, min(2 * half + 2, cols // P)):
                            for c in range(KC):
                                mm = pe.matmul(bank[:, (f % 2) * T:(f % 2 + 1) * T], wt[:, c, f * P:(f + 1) * P],
                                               core.xT[:, c, :], start=(c == 0), stop=(c == KC - 1))
                mm.then_inc(w.tile_used, 1)

        @block.scalar
        def _(act):
            for n, (tile, form, cols, store) in enumerate(jobs):
                act.wait_ge(w.tile_used, tile + 1)
                store(act, 0, pair(core, n)[0]).then_inc(act_stored, 1)

        @block.vector
        def _(dve):
            for n, (tile, form, cols, store) in enumerate(jobs):
                dve.wait_ge(w.tile_used, tile + 1)
                store(dve, 1, pair(core, n)[1]).then_inc(dve_stored, 1)


def split_projection_stage(core, tag, w, jobs, before=None):
    nc = core.nc
    s = {n: core.sem(f"{tag}_{n}") for n in ("x_high0", "x_high1", "x_low", "weight_high", "weight_low", "unit_used",
                                               "act_stored", "dve_stored")}
    units = []
    for n, (tile, form, cols, store) in enumerate(jobs):
        units += [(n, part) for part in (range(4) if cols == BW else [None])]
    split = [u for u, (n, part) in enumerate(units) if part is not None]
    last_unit = [max(u for u, (m, part) in enumerate(units) if m == n) for n in range(len(jobs))]
    UNIT = SLOT // 4
    half_k = KC // 2

    def stored_after(n, half):
        tile, form, cols, store = jobs[n]
        return last_unit[n] - 2 if form == "T" and half == 0 and cols == BW else last_unit[n]

    with ExitStack() as memory:
        def sbuf(name, shape):
            return memory.enter_context(nc.sbuf_tensor(f"{tag}_{name}", shape, F32R))[:]

        high, low, xh, xl = (sbuf(name, shape) for name, shape in (
            ("high", [P, 2, UNIT]), ("low", [P, 2, UNIT]), ("xh", [P, KC, T]), ("xl", [P, KC, T])))

        def raw(u):
            n, part = units[u]
            tile, form, cols, store = jobs[n]
            wt = w.tile(tile, KC, BW)
            if form == "T":
                return wt[:, :, part * P:(part + 1) * P]
            h, k = divmod(part, 2)
            return wt[:, half_k * k:half_k * (k + 1), h * 2 * P:(h + 1) * 2 * P]

        def unit(buffers, u):
            _, k, cols = raw(u).shape
            return buffers[:, split.index(u) % 2, :].rearrange("p (k n) -> p k n", k=k)

        def x_part(a, k):
            return a[:, half_k * k:half_k * (k + 1), :]

        with nc.Block() as block:
            @block.sync
            def _(sp):
                if before is not None:
                    before(sp)
                for n, (tile, form, cols, store) in enumerate(jobs):
                    u = last_unit[n]
                    if u in split:
                        sp.wait_ge(s["weight_low"], split.index(u) + 1)
                    else:
                        sp.wait_ge(s["unit_used"], u + 1)
                    sp.sem_inc(w.tile_used, 1)
                    if tile + w.slots < len(w.plan):
                        w.load(sp, tile + w.slots)

            @block.tensor
            def _(pe):
                for u, (n, part) in enumerate(units):
                    tile, form, cols, store = jobs[n]
                    banks = pair(core, n)
                    if n >= 2 and not part:
                        pe.wait_ge(s["act_stored"], n - 1)
                        pe.wait_ge(s["dve_stored"], n - 1)
                    if part is None:
                        w.wait(pe, tile)
                        wt = w.tile(tile, KC, cols)
                        for t in range(NT):
                            for c in range(KC):
                                mm = pe.matmul(banks[t][:, 0:cols], core.xT[:, c, t * P:(t + 1) * P], wt[:, c, :],
                                               start=(c == 0), stop=(c == KC - 1))
                        mm.then_inc(s["unit_used"], 1)
                        continue
                    m = split.index(u)
                    pe.wait_ge(s["weight_high"], m + 1)
                    passes = ((high, False), (high, True), (low, False))
                    if form == "T":
                        for j, (buffer, x_low) in enumerate(passes):
                            if j == 2:
                                pe.wait_ge(s["weight_low"], m + 1)
                            for c in range(KC):
                                if u == 0 and j < 2 and c % half_k == 0:
                                    if x_low:
                                        pe.wait_ge(s["x_low"], c // half_k + 1)
                                    else:
                                        pe.wait_ge(s[f"x_high{c // half_k}"], 1)
                                mm = pe.matmul(banks[part // 2][:, (part % 2) * T:(part % 2 + 1) * T],
                                               unit(buffer, u)[:, c, :], (xl if x_low else xh)[:, c, :],
                                               start=(j == 0 and c == 0), stop=(j == 2 and c == KC - 1))
                    else:
                        h, k = divmod(part, 2)
                        for t in range(NT):
                            for j, (buffer, x_low) in enumerate(passes):
                                if j == 2 and t == 0:
                                    pe.wait_ge(s["weight_low"], m + 1)
                                for c in range(half_k):
                                    mm = pe.matmul(banks[t][:, h * 2 * P:(h + 1) * 2 * P],
                                                   (xl if x_low else xh)[:, half_k * k + c, t * P:(t + 1) * P],
                                                   unit(buffer, u)[:, c, :], start=(k == 0 and j == 0 and c == 0),
                                                   stop=(k == 1 and j == 2 and c == half_k - 1))
                    mm.then_inc(s["unit_used"], 1)

            def stores(eng, half, u, sem):
                for n, (tile, form, cols, store) in enumerate(jobs):
                    if stored_after(n, half) == u - 2:
                        eng.wait_ge(s["unit_used"], u - 1)
                        store(eng, half, pair(core, n)[half]).then_inc(s[sem], 1)

            @block.scalar
            def _(act):
                for u in range(len(units) + 2):
                    stores(act, 0, u, "act_stored")
                    if u == 0:
                        act.copy(x_part(xh, 1), x_part(core.xT, 1)).then_inc(s["x_high1"], 1)
                    if u in split:
                        m = split.index(u)
                        if m == 0 or units[u][1] == 0:
                            w.wait(act, jobs[units[u][0]][0])
                        if m >= 2:
                            act.wait_ge(s["unit_used"], split[m - 2] + 1)
                        act.copy(unit(high, u), raw(u)).then_inc(s["weight_high"], 1)

            @block.vector
            def _(dve):
                for u in range(len(units) + 2):
                    stores(dve, 1, u, "dve_stored")
                    if u == 0:
                        dve.tensor_copy(x_part(xh, 0), x_part(core.xT, 0)).then_inc(s["x_high0"], 1)
                        for k in range(2):
                            dve.wait_ge(s[f"x_high{k}"], 1)
                            dve.tensor_tensor(x_part(xl, k), x_part(core.xT, k), x_part(xh, k), ALU.subtract)\
                               .then_inc(s["x_low"], 1)
                    if u in split:
                        dve.wait_ge(s["weight_high"], split.index(u) + 1)
                        dve.tensor_tensor(unit(low, u), raw(u), unit(high, u), ALU.subtract)\
                           .then_inc(s["weight_low"], 1)


def copy(eng, core, out, in_):
    return eng.copy(out, in_) if eng is core.nc.scalar else eng.tensor_copy(out, in_)


def scaled(eng, core, out, in_, factor):
    if eng is core.nc.scalar:
        return eng.mul(out, in_, factor)
    return eng.tensor_scalar(out, in_, factor, None, ALU.mult)


def keep_T(core, dst, factor=None):
    def store(eng, half, bank):
        out = dst[:, 2 * half:2 * half + 2, :]
        in_ = bank[:].rearrange("p (a b) -> p a b", a=2)
        return copy(eng, core, out, in_) if factor is None else scaled(eng, core, out, in_, factor)
    return store


def keep_N(core, dst):
    def store(eng, half, bank):
        out = dst[:, half, :]
        return copy(eng, core, out, bank[:, 0:out.shape[1]])
    return store


def turn_stage(core, tag, src, dst, chunks, column=None):
    nc = core.nc
    turned = core.sem(f"{tag}_turned")
    act_stored = core.sem(f"{tag}_act_stored")
    dve_stored = core.sem(f"{tag}_dve_stored")
    column = column or (lambda t, c: src[:, t, c * P:(c + 1) * P])
    steps = [(n, range(2 * n, min(2 * n + 2, chunks))) for n in range(-(-chunks // 2))]
    with nc.Block() as block:
        @block.tensor
        def _(pe):
            for n, cs in steps:
                if n >= 8:
                    pe.wait_ge(act_stored, (n - 8) // 2 + 1)
                    pe.wait_ge(dve_stored, (n - 8) // 2 + 1)
                for c in cs:
                    for t in range(NT):
                        mm = pe.transpose(core.banks[n % 8][:, (c % 2) * T + t * P:(c % 2) * T + (t + 1) * P],
                                          column(t, c), core.const("ident"))
                mm.then_inc(turned, 1)

        def store(eng, n, cs):
            eng.wait_ge(turned, n + 1)
            out = dst[:, cs[0]:cs[-1] + 1, :]
            return copy(eng, core, out, core.banks[n % 8][:, 0:len(cs) * T].rearrange("p (a b) -> p a b", b=T))

        @block.scalar
        def _(act):
            for n, cs in steps[0::2]:
                store(act, n, cs).then_inc(act_stored, 1)

        @block.vector
        def _(dve):
            for n, cs in steps[1::2]:
                store(dve, n, cs).then_inc(dve_stored, 1)


class GateLogits:
    STEPS = 10

    def __init__(self, core, tag, w, first, out, halves=(0, 1)):
        self.core, self.w, self.first, self.out, self.halves = core, w, first, out, halves
        self.stored = core.sem(f"{tag}_logits_stored")
        self.products = [(j, t, c) for j in range(len(halves)) for t in range(NT) for c in range(KC)]

    def refill(self, sp):
        self.w.refill(sp, self.first, self.first + len(self.halves))

    def step(self, pe, i):
        n = len(self.products)
        for j, t, c in self.products[n * i // self.STEPS:n * (i + 1) // self.STEPS]:
            if (t, c) == (0, 0):
                self.w.wait(pe, self.first + j)
            if j and c == 0:
                pe.wait_ge(self.stored, t + 1)
            mm = pe.matmul(self.core.banks[6 + t][:], self.core.xT[:, c, t * P:(t + 1) * P],
                           self.w.tile(self.first + j, KC, BW)[:, c, :], start=(c == 0), stop=(c == KC - 1))
            if (t, c) == (NT - 1, KC - 1):
                mm.then_inc(self.w.tile_used, 1)

    def all(self, pe):
        for i in range(self.STEPS):
            self.step(pe, i)

    def store(self, dve, j):
        dve.wait_ge(self.w.tile_used, self.first + j + 1)
        for t in range(NT):
            dve.tensor_copy(self.out[:, 2 * self.halves[j] + t, :], self.core.banks[6 + t][:]).then_inc(self.stored, 1)

    def store_between(self, dve, i):
        if i == self.STEPS // 2 and len(self.halves) == 2:
            self.store(dve, 0)

    def store_last(self, dve):
        self.store(dve, len(self.halves) - 1)


def softmax_stage(core, tag, at, heads, q, k, v, mask, out, bias=None, sink=None, ready=None, logits=None):
    nc = core.nc
    z, at = core.part(at, 3, TRI)
    p, at = core.part(at, 3, TRI)
    pT, at = core.part(at, 2, TRI)
    top, at = core.part(at, heads, NT)
    minus, at = core.part(at, heads, NT)
    total, at = core.part(at, heads, NT)
    extra, at = core.part(at, heads, NT)
    s = {n: core.sem(f"{tag}_{n}") for n in ("scores", "masked", "sunk", "negated", "probs", "turned", "copied",
                                               "summed", "sink_exp", "added", "inverse")}
    if bias is not None:
        bias_lhs, bias_rhs = bias
    per_bank = BANK // HD
    obank = [[core.banks[4 + t * (heads // per_bank) + g] for g in range(heads // per_bank)] for t in range(NT)]
    edges = (0, P), (P, TRI)

    with nc.Block() as block:
        @block.sync
        def _(sp):
            if logits is not None:
                logits.refill(sp)

        @block.tensor
        def _(pe):
            for i in range(heads + 3):
                h = i
                if h < heads:
                    if h >= 2:
                        pe.wait_ge(s["masked"], h - 1)
                    bank = core.banks[h % 2]
                    for t, (a, b) in enumerate(edges):
                        mm = pe.matmul(bank[:, a:b], q(h)[:, t * P:(t + 1) * P], k(h)[:, 0:b - a],
                                       start=True, stop=(bias is None))
                        if bias is not None:
                            mm = pe.matmul(bank[:, a:b], bias_lhs(h), bias_rhs[:, 0:b - a], start=False, stop=True)
                    mm.then_inc(s["scores"], 1)
                if logits is not None and i < logits.STEPS:
                    logits.step(pe, i)
                h = i - 2
                if 0 <= h < heads:
                    pe.wait_ge(s["probs"], h + 1)
                    if h >= 2:
                        pe.wait_ge(s["copied"], h - 1)
                    for j in range(3):
                        mm = pe.transpose(core.banks[2 + h % 2][:, j * P:(j + 1) * P],
                                          p[:, h % 3, j * P:(j + 1) * P], core.const("ident"))
                    mm.then_inc(s["turned"], 1)
                h = i - 3
                if h >= 0:
                    pe.wait_ge(s["copied"], h + 1)
                    g, c = h // per_bank, (h % per_bank) * HD
                    w = pT[:, h % 2, :]
                    pe.matmul(obank[0][g][:, c:c + HD], w[:, 0:P], v(h, 0), start=True, stop=True)
                    pe.matmul(obank[1][g][:, c:c + HD], w[:, P:2 * P], v(h, 0), start=True, stop=False)
                    pe.matmul(obank[1][g][:, c:c + HD], w[:, 2 * P:TRI], v(h, 1), start=False,
                              stop=True).then_inc(s["summed"], 1)

        @block.vector
        def _(dve):
            if ready is not None:
                dve.wait_ge(*ready)
            for i in range(heads + 3):
                h = i - 3
                if h >= 0:
                    dve.wait_ge(s["turned"], h + 1)
                    if h >= 2:
                        dve.wait_ge(s["summed"], h - 1)
                    dve.tensor_copy(pT[:, h % 2, :], core.banks[2 + h % 2][:, 0:TRI]).then_inc(s["copied"], 1)
                h = i
                if logits is not None:
                    logits.store_between(dve, i)
                if h < heads:
                    dve.wait_ge(s["scores"], h + 1)
                    if h >= 3:
                        dve.wait_ge(s["probs"], h - 2)
                    for t, (a, b) in enumerate(edges):
                        op = dve.tensor_tensor_reduce(z[:, h % 3, a:b], core.banks[h % 2][:, a:b], mask(h, t),
                                                      1.0, -3.0e38, ALU.add, ALU.max, top[:, h, t:t + 1])
                    op.then_inc(s["masked"], 1)
                    dve.wait_ge(s["masked"], h + 1)
                    if sink is not None:
                        dve.tensor_scalar(top[:, h, :], top[:, h, :], sink[:, h:h + 1], None,
                                          ALU.max).then_inc(s["sunk"], 1)
                        dve.wait_ge(s["sunk"], h + 1)
                    dve.tensor_scalar(minus[:, h, :], top[:, h, :], -1.0, None, ALU.mult).then_inc(s["negated"], 1)
            if logits is not None:
                logits.store_last(dve)
            if sink is not None:
                dve.wait_ge(s["sink_exp"], heads)
                dve.tensor_tensor(total, total, extra, ALU.add).then_inc(s["added"], 1)
                dve.wait_ge(s["added"], 1)
            dve.wait_ge(s["probs"], heads)
            dve.reciprocal(total, total).then_inc(s["inverse"], 1)
            dve.wait_ge(s["inverse"], 1)
            dve.wait_ge(s["summed"], heads)
            for t in range(NT):
                for g in range(heads // per_bank):
                    hs = slice(g * per_bank, (g + 1) * per_bank)
                    dve.tensor_tensor(out[:, t, g * BANK:(g + 1) * BANK].rearrange("p (h d) -> p h d", d=HD),
                                      obank[t][g][:].rearrange("p (h d) -> p h d", d=HD),
                                      total[:, hs, t:t + 1].broadcast_to([P, per_bank, HD]), ALU.mult)

        @block.scalar
        def _(act):
            for h in range(heads):
                act.wait_ge(s["negated"], h + 1)
                if h >= 3:
                    act.wait_ge(s["turned"], h - 2)
                if sink is not None:
                    for t in range(NT):
                        op = act.activation(extra[:, h, t:t + 1], sink[:, h:h + 1], ACT.Exp, bias=minus[:, h, t:t + 1])
                    op.then_inc(s["sink_exp"], 1)
                for t, (a, b) in enumerate(edges):
                    op = act.activation(p[:, h % 3, a:b], z[:, h % 3, a:b], ACT.Exp, bias=minus[:, h, t:t + 1],
                                        accum_out=total[:, h, t:t + 1])
                op.then_inc(s["probs"], 1)


def stick_stage(core, tag, at, qT, kT, v, out, logits):
    nc = core.nc
    z, at = core.part(at, 2, TRI)
    small, at = core.part(at, 2, TRI)
    sp_, at = core.part(at, 2, TRI)
    w, at = core.part(at, 2, TRI)
    s = {n: core.sem(f"{tag}_{n}") for n in ("scores", "kept", "minus_abs", "exp", "log", "soft", "soft_masked",
                                               "cum", "diff", "weights", "masked", "summed")}
    H = 8

    def q(h):
        return qT[HD * (h % 2):HD * (h % 2) + HD, h // 2, :]

    def k(h):
        return kT[HD * (h % 2):HD * (h % 2) + HD, h // 2, :]

    with nc.Block() as block:
        @block.sync
        def _(sp):
            logits.refill(sp)

        @block.tensor
        def _(pe):
            for i in range(H + 2):
                h = i
                if h < H:
                    if h >= 2:
                        pe.wait_ge(s["soft"], h - 1)
                        pe.wait_ge(s["kept"], h - 1)
                    bank = core.banks[h % 2]
                    pe.matmul(bank[:, 0:T], k(h)[:, 0:P], q(h), start=True, stop=True)
                    pe.matmul(bank[:, T:TRI], k(h)[:, P:T], q(h)[:, P:T], start=True, stop=True)\
                      .then_inc(s["scores"], 1)
                logits.step(pe, i)
                h = i - 1
                if 0 <= h < H:
                    pe.wait_ge(s["soft_masked"], h + 1)
                    if h >= 2:
                        pe.wait_ge(s["diff"], h - 1)
                    bank = core.banks[2 + h % 2]
                    pe.matmul(bank[:, 0:P], core.const("ge"), sp_[:, h % 2, 0:P], start=True, stop=True)
                    pe.matmul(bank[:, P:T], core.const("ge"), sp_[:, h % 2, P:T], start=True, stop=False)
                    pe.matmul(bank[:, P:T], core.const("ones"), sp_[:, h % 2, T:TRI], start=False, stop=True)
                    pe.matmul(bank[:, T:TRI], core.const("ge"), sp_[:, h % 2, T:TRI], start=True, stop=True)\
                      .then_inc(s["cum"], 1)
                h = i - 2
                if h >= 0:
                    pe.wait_ge(s["masked"], h + 1)
                    c = h * HD
                    u = w[:, h % 2, :]
                    pe.matmul(core.banks[4][:, c:c + HD], u[:, 0:P], v[:, 0, c:c + HD], start=True, stop=True)
                    pe.matmul(core.banks[5][:, c:c + HD], u[:, P:T], v[:, 0, c:c + HD], start=True, stop=False)
                    pe.matmul(core.banks[5][:, c:c + HD], u[:, T:TRI], v[:, 1, c:c + HD], start=False,
                              stop=True).then_inc(s["summed"], 1)

        @block.vector
        def _(dve):
            for i in range(H + 1):
                h = i
                logits.store_between(dve, i)
                if h < H:
                    if h >= 2:
                        dve.wait_ge(s["log"], h - 1)
                        dve.wait_ge(s["soft"], h - 1)
                    dve.wait_ge(s["kept"], h + 1)
                    dve.scalar_tensor_tensor(out=small[:, h % 2, :], in0=z[:, h % 2, :], scalar=-1.0,
                                             in1=z[:, h % 2, :], op0=ALU.mult, op1=ALU.min)\
                       .then_inc(s["minus_abs"], 1)
                    dve.wait_ge(s["log"], h + 1)
                    if h >= 2:
                        dve.wait_ge(s["cum"], h - 1)
                    dve.scalar_tensor_tensor(out=sp_[:, h % 2, :], in0=z[:, h % 2, :], scalar=0.0,
                                             in1=small[:, h % 2, :], op0=ALU.max, op1=ALU.add)\
                       .then_inc(s["soft"], 1)
                h = i - 1
                if h >= 0:
                    dve.wait_ge(s["cum"], h + 1)
                    if h >= 2:
                        dve.wait_ge(s["summed"], h - 1)
                    dve.scalar_tensor_tensor(out=w[:, h % 2, :], in0=core.banks[2 + h % 2][:, 0:TRI], scalar=-1.0,
                                             in1=z[:, h % 2, :], op0=ALU.mult, op1=ALU.add).then_inc(s["diff"], 1)
            logits.store_last(dve)
            dve.wait_ge(s["summed"], H)
            dve.tensor_copy(out[:, 0, :], core.banks[4][:])

        @block.scalar
        def _(act):
            for i in range(H + 1):
                h = i
                if h < H:
                    act.wait_ge(s["scores"], h + 1)
                    if h >= 2:
                        act.wait_ge(s["diff"], h - 1)
                    act.copy(z[:, h % 2, :], core.banks[h % 2][:, 0:TRI]).then_inc(s["kept"], 1)
                    act.wait_ge(s["minus_abs"], h + 1)
                    act.activation(small[:, h % 2, :], small[:, h % 2, :], ACT.Exp).then_inc(s["exp"], 1)
                    act.wait_ge(s["exp"], h + 1)
                    act.activation(small[:, h % 2, :], small[:, h % 2, :], ACT.Ln, bias=1.0).then_inc(s["log"], 1)
                h = i - 1
                if h >= 0:
                    act.wait_ge(s["diff"], h + 1)
                    act.activation(w[:, h % 2, :], w[:, h % 2, :], ACT.Exp).then_inc(s["weights"], 1)
            act.wait_ge(s["summed"], H)
            act.copy(out[:, 1, :], core.banks[5][:])

        @block.gpsimd
        def _(pool):
            def strictly_later(a):
                for c in (0, T):
                    op = pool.affine_select(out=a[:, c:c + P], in_=a[:, c:c + P], pattern=[[1, P]],
                                            compare_op=ALU.is_gt, fill=0.0, base=0, channel_multiplier=-1)
                return op
            for i in range(H + 1):
                if i < H:
                    pool.wait_ge(s["soft"], i + 1)
                    strictly_later(sp_[:, i % 2, :]).then_inc(s["soft_masked"], 1)
                if i >= 1:
                    pool.wait_ge(s["weights"], i)
                    strictly_later(w[:, (i - 1) % 2, :]).then_inc(s["masked"], 1)


def decay_stage(core, tag, fl, b, cT, tmp):
    nc = core.nc
    s = {n: core.sem(f"{tag}_{n}") for n in ("step", "exp", "log", "soft", "sums")}
    u, e = tmp[:, 8:24], tmp[:, 24:40]
    u2 = u.rearrange("p (t h) -> p t h", t=NT)
    with nc.Block() as block:
        @block.vector
        def _(dve):
            for t in range(NT):
                op = dve.tensor_tensor(u2[:, t, :], fl[:, t, :], b, ALU.add)
            op.then_inc(s["step"], 1)
            dve.wait_ge(s["step"], 1)
            dve.scalar_tensor_tensor(out=e, in0=u, scalar=-1.0, in1=u, op0=ALU.mult, op1=ALU.min).then_inc(s["step"], 1)
            dve.wait_ge(s["step"], 2)
            dve.tensor_scalar(u, u, -1.0, 0.0, ALU.mult, ALU.max).then_inc(s["step"], 1)
            dve.wait_ge(s["step"], 3)
            dve.wait_ge(s["log"], 1)
            dve.tensor_tensor(u, u, e, ALU.add).then_inc(s["soft"], 1)
            dve.wait_ge(s["sums"], 1)
            dve.tensor_copy(cT[0:8, :], core.banks[0][0:8, 0:T])

        @block.scalar
        def _(act):
            act.wait_ge(s["step"], 2)
            act.activation(e, e, ACT.Exp).then_inc(s["exp"], 1)
            act.wait_ge(s["exp"], 1)
            act.activation(e, e, ACT.Ln, bias=1.0).then_inc(s["log"], 1)

        @block.tensor
        def _(pe):
            pe.wait_ge(s["soft"], 1)
            bank = core.banks[0]
            pe.matmul(bank[0:8, 0:P], u2[:, 0, :], core.const("le"), start=True, stop=True)
            pe.matmul(bank[0:8, P:T], u2[:, 0, :], core.const("ones"), start=True, stop=False)
            pe.matmul(bank[0:8, P:T], u2[:, 1, :], core.const("le"), start=False, stop=True).then_inc(s["sums"], 1)


def angles_stage(core, positions, cos, sin, tmp):
    nc = core.nc
    s = {n: core.sem(f"angle_{n}") for n in ("loaded", "step", "done")}
    pos = tmp[:, 0:2].bitcast(I32)
    posf = tmp[:, 2:4]
    ang = tmp[:, 4:20].rearrange("p (t f) -> p t f", t=NT)
    turns = tmp[:, 20:36].rearrange("p (t f) -> p t f", t=NT)
    two_pi = (6.28125, 0.0019350051879882812, 3.019915981956753e-07)
    with nc.Block() as block:
        @block.sync
        def _(sp):
            sp.dma_start(pos, positions.rearrange("o (t p) -> p (o t)", p=P), allow_slow_non_contiguous=True)\
              .then_inc(s["loaded"], 16)

        @block.vector
        def _(dve):
            step = [0]

            def then(op):
                op.then_inc(s["step"], 1)
                step[0] += 1
                dve.wait_ge(s["step"], step[0])

            dve.wait_ge(s["loaded"], 16)
            then(dve.tensor_copy(posf, pos))
            for t in range(NT):
                then(dve.tensor_scalar(ang[:, t, :], core.const("freq"), posf[:, t:t + 1], None, ALU.mult))
            then(dve.tensor_scalar(turns, ang, 1.0 / (2.0 * np.pi), 12582912.0, ALU.mult, ALU.add))
            then(dve.tensor_scalar(turns, turns, 12582912.0, None, ALU.subtract))
            for c in two_pi:
                then(dve.scalar_tensor_tensor(out=ang, in0=turns, scalar=-c, in1=ang, op0=ALU.mult, op1=ALU.add))
            then(dve.tensor_scalar(sin, ang, np.pi - 1e-6, -np.pi + 1e-6, ALU.min, ALU.max))
            then(dve.tensor_scalar(ang, ang, np.pi / 2, None, ALU.add))
            then(dve.tensor_scalar(turns, ang, np.pi, -2.0 * np.pi, ALU.is_gt, ALU.mult))
            then(dve.tensor_tensor(ang, ang, turns, ALU.add))
            dve.tensor_scalar(cos, ang, np.pi - 1e-6, -np.pi + 1e-6, ALU.min, ALU.max).then_inc(s["done"], 1)

        @block.scalar
        def _(act):
            act.wait_ge(s["done"], 1)
            act.activation(sin, sin, ACT.Sin)
            act.activation(cos, cos, ACT.Sin)


def rope_stage(core, tag, proj, flat, cos, sin, tmp, logits):
    nc = core.nc
    s = {n: core.sem(f"{tag}_{n}") for n in ("parts", "x1", "x2", "rotated")}
    half = ROT // 2
    with nc.Block() as block:
        @block.sync
        def _(sp):
            logits.refill(sp)

        @block.tensor
        def _(pe):
            logits.all(pe)

        @block.vector
        def _(dve):
            done = 0
            for a, b in ((8, ROPE_COLS[0]), ROPE_COLS[1:3]):
                n = (b - a) // HD
                for t in range(NT):
                    x = proj[:, t, a:b].rearrange("p (h d) -> p h d", d=HD)
                    x1, x2 = x[:, :, 0:half], x[:, :, half:ROT]
                    c = cos[:, t:t + 1, :].broadcast_to([P, n, half])
                    si = sin[:, t:t + 1, :].broadcast_to([P, n, half])
                    u = [tmp[:, i * 80:i * 80 + n * half].rearrange("p (h d) -> p h d", d=half) for i in range(4)]
                    if done:
                        dve.wait_ge(s["rotated"], done)
                    dve.tensor_tensor(u[0], x1, c, ALU.mult)
                    dve.tensor_tensor(u[1], x2, si, ALU.mult)
                    dve.tensor_tensor(u[2], x2, c, ALU.mult)
                    dve.tensor_tensor(u[3], x1, si, ALU.mult).then_inc(s["parts"], 1)
                    done += 1
                    dve.wait_ge(s["parts"], done)
                    dve.tensor_tensor(x1, u[0], u[1], ALU.subtract)
                    dve.tensor_tensor(x2, u[2], u[3], ALU.add).then_inc(s["rotated"], 1)
            logits.store_last(dve)

        @block.scalar
        def _(act):
            act.wait_ge(s["rotated"], 2 * NT)
            for t in range(NT):
                act.mul(flat[:, t, 0:512], proj[:, t, 8:520], HD ** -0.5)
                act.copy(flat[:, t, 768:1024], proj[:, t, 776:1032])

        @block.gpsimd
        def _(pool):
            pool.wait_ge(s["rotated"], 2 * NT)
            for t in range(NT):
                for g in range(2):
                    pool.tensor_copy(flat[:, t, 512 + P * g:512 + P * g + P].rearrange("p (r d) -> p r d", r=2),
                                     proj[:, t:t + 1, 520 + HD * g:584 + HD * g].broadcast_to([P, 2, HD]))
                pool.tensor_copy(flat[:, t, 1024:1152].rearrange("p (r d) -> p r d", r=2),
                                 proj[:, t:t + 1, 1032:1096].broadcast_to([P, 2, HD]))


def indexer_stage(core, tag, at, cT, wi, mask, logits):
    nc = core.nc
    relu, at = core.part(at, 2, TRI)
    score, at = core.part(at, TRI)
    best, at = core.part(at, NT, 8)
    w, at = core.part(at, NT, 4)
    s = {n: core.sem(f"{tag}_{n}") for n in ("scaled", "dots", "relu", "added", "causal", "best", "taken", "chosen")}
    HI = 4
    edges = (0, P), (P, TRI)
    with nc.Block() as block:
        @block.sync
        def _(sp):
            logits.refill(sp)

        @block.tensor
        def _(pe):
            for h in range(HI):
                r = slice(HD * (h % 2), HD * (h % 2) + HD)
                for t, (a, b) in enumerate(edges):
                    mm = pe.matmul(core.banks[h][:, a:b], cT[r, 6 + h // 2, t * P:(t + 1) * P], cT[r, 8, 0:b - a],
                                   start=True, stop=True)
                mm.then_inc(s["dots"], 1)
            logits.all(pe)

        @block.scalar
        def _(act):
            for h in range(HI):
                act.wait_ge(s["dots"], h + 1)
                if h >= 2:
                    act.wait_ge(s["added"], NT * (h - 1))
                act.activation(relu[:, h % 2, :], core.banks[h][:, 0:TRI], ACT.Relu, scale=HD ** -0.5)\
                   .then_inc(s["relu"], 1)

        @block.vector
        def _(dve):
            dve.tensor_scalar(w, wi, HI ** -0.5, None, ALU.mult).then_inc(s["scaled"], 1)
            dve.wait_ge(s["scaled"], 1)
            for h in range(HI):
                dve.wait_ge(s["relu"], h + 1)
                if h:
                    dve.wait_ge(s["added"], NT * h)
                for t, (a, b) in enumerate(edges):
                    if h == 0:
                        op = dve.tensor_scalar(score[:, a:b], relu[:, 0, a:b], w[:, t, 0:1], None, ALU.mult)
                    else:
                        op = dve.scalar_tensor_tensor(out=score[:, a:b], in0=relu[:, h % 2, a:b],
                                                      scalar=w[:, t, h:h + 1], in1=score[:, a:b],
                                                      op0=ALU.mult, op1=ALU.add)
                    op.then_inc(s["added"], 1)
            dve.wait_ge(s["causal"], 1)
            for n in range(DSA_TOPK // 8):
                for t, (a, b) in enumerate(edges):
                    if n:
                        dve.wait_ge(s["taken"], NT * (n - 1) + t + 1)
                    dve.max(best[:, t, :], score[:, a:b]).then_inc(s["best"], 1)
                for t, (a, b) in enumerate(edges):
                    dve.wait_ge(s["best"], NT * n + t + 1)
                    dve.match_replace(score[:, a:b], best[:, t, :], score[:, a:b], TAKEN).then_inc(s["taken"], 1)
            dve.wait_ge(s["taken"], NT * DSA_TOPK // 8)
            dve.tensor_scalar(mask, score, -3.2e38, NEG, ALU.is_gt, ALU.mult).then_inc(s["chosen"], 1)
            dve.wait_ge(s["chosen"], 1)
            dve.tensor_tensor(mask, mask, core.const("neg"), ALU.add)
            logits.store_last(dve)

        @block.gpsimd
        def _(pool):
            pool.wait_ge(s["added"], NT * HI)
            for c in (0, T):
                op = pool.affine_select(out=score[:, c:c + P], in_=score[:, c:c + P], pattern=[[-1, P]],
                                        compare_op=ALU.is_ge, fill=MASKED, base=0, channel_multiplier=1)
                if c == 0:
                    continue
            op.then_inc(s["causal"], 1)


def gate_stage(core, tag, at, w, first, branches, logits, y):
    nc = core.nc
    prod, at = core.part(at, 4, BANK)
    s = {n: core.sem(f"{tag}_{n}") for n in ("bank", "sigmoid", "product", "sum")}
    NB = len(branches)
    with nc.Block() as block:
        @block.sync
        def _(sp):
            w.refill(sp, first, first + NB)

        @block.tensor
        def _(pe):
            for b in range(NB):
                n = first + b
                w.wait(pe, n)
                wt = w.tile(n, BW // P, D)
                for half in range(2):
                    for t in range(NT):
                        if b >= 2:
                            pe.wait_ge(s["product"], 4 * (b - 2) + 2 * half + t + 1)
                        for c in range(BW // P):
                            mm = pe.matmul(core.banks[4 * (b % 2) + 2 * half + t][:],
                                           branches[b][:, c, t * P:(t + 1) * P],
                                           wt[:, c, half * BANK:(half + 1) * BANK], start=(c == 0),
                                           stop=(c == BW // P - 1))
                        if (half, t) != (1, NT - 1):
                            mm.then_inc(s["bank"], 1)
                mm.then_inc(w.tile_used, 1)

        @block.scalar
        def _(act):
            for b in range(NB):
                for n in range(4):
                    act.activation(logits[b][:, n, :], logits[b][:, n, :], ACT.Sigmoid).then_inc(s["sigmoid"], 1)

        @block.vector
        def _(dve):
            for b in range(NB):
                for n in range(4):
                    half, t = divmod(n, 2)
                    if n < 3:
                        dve.wait_ge(s["bank"], 3 * b + n + 1)
                    else:
                        dve.wait_ge(w.tile_used, first + b + 1)
                    dve.wait_ge(s["sigmoid"], 4 * b + n + 1)
                    if b >= 2:
                        dve.wait_ge(s["sum"], 4 * (b - 2) + n + 1)
                    out = y[:, t, half * BANK:(half + 1) * BANK] if b == 0 else prod[:, n, :]
                    dve.tensor_tensor(out, core.banks[4 * (b % 2) + n][:], logits[b][:, n, :], ALU.mult)\
                       .then_inc(s["product"], 1)

        @block.gpsimd
        def _(pool):
            for b in range(1, NB):
                for n in range(4):
                    pool.wait_ge(s["product"], 4 * b + n + 1)
                    if b >= 2:
                        pool.wait_ge(s["sum"], 4 * (b - 2) + n + 1)
                    out = y[:, n % 2, (n // 2) * BANK:(n // 2 + 1) * BANK]
                    pool.tensor_tensor(out, out, prod[:, n, :], ALU.add).then_inc(s["sum"], 1)


def output_stage(core, tag, w, first, alpha=None, before=None):
    nc = core.nc
    s = {n: core.sem(f"{tag}_{n}") for n in ("x_high0", "x_high1", "x_low", "weight_high", "weight_low", "unit_used")}
    half_k = KC // 2
    with ExitStack() as memory:
        def sbuf(name, shape):
            return memory.enter_context(nc.sbuf_tensor(f"{tag}_{name}", shape, F32R))[:]

        high, low = sbuf("high", [P, 2, half_k, BW]), sbuf("low", [P, 2, half_k, BW])
        xh, xl = sbuf("xh", [P, KC, T]), sbuf("xl", [P, KC, T])

        def raw(u):
            return w.tile(first + u // 2, KC, BW)[:, half_k * (u % 2):half_k * (u % 2 + 1), :]

        def x_part(a, k):
            return a[:, half_k * k:half_k * (k + 1), :]

        with nc.Block() as block:
            @block.sync
            def _(sp):
                if before is not None:
                    before(sp)
                for n in range(2):
                    sp.wait_ge(s["weight_low"], 2 * (n + 1))
                    sp.sem_inc(w.tile_used, 1)
                    if first + n + w.slots < len(w.plan):
                        w.load(sp, first + n + w.slots)

            @block.scalar
            def _(act):
                for u in range(4):
                    if u == 1:
                        act.copy(x_part(xh, 1), x_part(core.xT, 1)).then_inc(s["x_high1"], 1)
                    if u % 2 == 0:
                        w.wait(act, first + u // 2)
                    if u >= 2:
                        act.wait_ge(s["unit_used"], u - 1)
                    act.copy(high[:, u % 2, :, :], raw(u)).then_inc(s["weight_high"], 1)

            @block.tensor
            def _(pe):
                for u in range(4):
                    n, part = divmod(u, 2)
                    pe.wait_ge(s[f"x_high{part}"], 1)
                    pe.wait_ge(s["weight_high"], u + 1)
                    for t in range(NT):
                        for j, (x, wt) in enumerate(((xh, high), (xl, high), (xh, low))):
                            if t == 0 and j == 1:
                                pe.wait_ge(s["x_low"], min(u, 1) + 1)
                            if t == 0 and j == 2:
                                pe.wait_ge(s["weight_low"], u + 1)
                            for c in range(half_k):
                                mm = pe.matmul(core.banks[2 * n + t][:],
                                               x[:, half_k * part + c, t * P:(t + 1) * P], wt[:, u % 2, c, :],
                                               start=(part == 0 and j == 0 and c == 0),
                                               stop=(part == 1 and j == 2 and c == half_k - 1))
                    mm.then_inc(s["unit_used"], 1)

            @block.vector
            def _(dve):
                def add(n):
                    dve.wait_ge(s["unit_used"], 2 * n + 2)
                    for t in range(NT):
                        xs = core.x[:, t, n * BANK:(n + 1) * BANK]
                        add_to_x(dve, xs, core.banks[2 * n + t][:], alpha)

                for u in range(4):
                    if u == 0:
                        dve.tensor_copy(x_part(xh, 0), x_part(core.xT, 0)).then_inc(s["x_high0"], 1)
                    if u < 2:
                        dve.wait_ge(s[f"x_high{u}"], 1)
                        dve.tensor_tensor(x_part(xl, u), x_part(core.xT, u), x_part(xh, u), ALU.subtract)\
                           .then_inc(s["x_low"], 1)
                    dve.wait_ge(s["weight_high"], u + 1)
                    dve.tensor_tensor(low[:, u % 2, :, :], raw(u), high[:, u % 2, :, :], ALU.subtract)\
                       .then_inc(s["weight_low"], 1)
                for n in range(2):
                    add(n)


def add_to_x(dve, xs, more, alpha):
    if alpha is None:
        return dve.tensor_tensor(xs, more, xs, ALU.add)
    return dve.scalar_tensor_tensor(out=xs, in0=xs, scalar=alpha, in1=more, op0=ALU.mult, op1=ALU.add)


def mlp_stage(core, tag, w, first, steps, gated, alpha=None, before=None):
    nc = core.nc
    chunks = 2 if gated else BW // P
    n_tiles = 2 * steps
    ups = [0] + [2 * i - 1 for i in range(1, steps)]
    downs = [2 * i + 2 for i in range(steps - 1)] + [n_tiles - 1]
    role = {n: ("up", i) for i, n in enumerate(ups)}
    role.update({n: ("down", i) for i, n in enumerate(downs)})
    n_units = 2 * n_tiles
    yields = (1,) if gated else (0, 1)
    names = ("x_high0", "x_high1", "x_low", "weight_high", "weight_low", "unit_used", "active", "product",
             "hidden_high",
             "hidden_low")
    s = {n: core.sem(f"{tag}_{n}") for n in names}

    def hidden_count(i, half):
        return len(yields) * i + yields.index(half) + 1

    with ExitStack() as memory:
        def sbuf(name, shape, dt):
            return memory.enter_context(nc.sbuf_tensor(f"{tag}_{name}", shape, dt))[:]

        high, low = sbuf("high", [P, 2, SLOT // 2], F32R), sbuf("low", [P, 2, SLOT // 2], F32R)
        xh, xl = sbuf("xh", [P, KC, T], F32R), sbuf("xl", [P, KC, T], F32R)
        hh, hl = sbuf("hh", [P, 2, chunks, T], F32R), sbuf("hl", [P, 2, chunks, T], F32R)
        hidden = sbuf("hidden", [P, 2, len(yields), BANK], F32)

        def raw(u):
            n, half = divmod(u, 2)
            if role[n][0] == "up":
                return w.tile(first + n, KC, BW)[:, :, half * 2 * P:(half + 1) * 2 * P]
            return w.tile(first + n, chunks, D)[:, :, half * BANK:(half + 1) * BANK]

        def unit(buffers, u):
            _, k, cols = raw(u).shape
            return buffers[:, u % 2, 0:k * cols].rearrange("p (k n) -> p k n", k=k)

        def hidden_piece(i, half):
            return hidden[:, i % 2, yields.index(half), :]

        def split_piece(buffer, i, half):
            c = 2 * yields.index(half)
            return buffer[:, i % 2, c:c + 2, :].rearrange("p a b -> p (a b)")

        def pending(u, behind):
            v = u - behind
            if 0 <= v < n_units and role[v // 2][0] == "up":
                return role[v // 2][1], v % 2
            return None

        with nc.Block() as block:
            @block.sync
            def _(sp):
                if before is not None:
                    before(sp)
                for n in range(n_tiles):
                    sp.wait_ge(s["weight_low"], 2 * (n + 1))
                    sp.sem_inc(w.tile_used, 1)
                    if first + n + w.slots < len(w.plan):
                        w.load(sp, first + n + w.slots)

            @block.tensor
            def _(pe):
                def passes(u):
                    return ((unit(high, u), False), (unit(high, u), True), (unit(low, u), False))

                for u in range(n_units):
                    n, half = divmod(u, 2)
                    kind, i = role[n]
                    pe.wait_ge(s["weight_high"], u + 1)
                    if kind == "up":
                        bank = pair(core, i)[half]
                        if i >= 2:
                            if half in yields and gated:
                                pe.wait_ge(s["product"], hidden_count(i - 2, half))
                            else:
                                pe.wait_ge(s["active"], i - 1 if gated else hidden_count(i - 2, half))
                        for f in range(2):
                            for j, (wt, x_low) in enumerate(passes(u)):
                                if j == 2 and f == 0:
                                    pe.wait_ge(s["weight_low"], u + 1)
                                for c in range(KC):
                                    if u == 0 and f == 0 and j < 2 and c % 4 == 0:
                                        if x_low:
                                            pe.wait_ge(s["x_low"], c // 4 + 1)
                                        else:
                                            pe.wait_ge(s[f"x_high{c // 4}"], 1)
                                    mm = pe.matmul(bank[:, f * T:(f + 1) * T], wt[:, c, f * P:(f + 1) * P],
                                                   (xl if x_low else xh)[:, c, :], start=(j == 0 and c == 0),
                                                   stop=(j == 2 and c == KC - 1))
                    else:
                        pe.wait_ge(s["hidden_low"], hidden_count(i, yields[-1]))
                        for t in range(NT):
                            for j, (wt, h_low) in enumerate(passes(u)):
                                if j == 2 and t == 0:
                                    pe.wait_ge(s["weight_low"], u + 1)
                                for c in range(chunks):
                                    mm = pe.matmul(core.banks[4 + 2 * t + half][:],
                                                   (hl if h_low else hh)[:, i % 2, c, t * P:(t + 1) * P], wt[:, c, :],
                                                   start=(i == 0 and j == 0 and c == 0),
                                                   stop=(i == steps - 1 and j == 2 and c == chunks - 1))
                    mm.then_inc(s["unit_used"], 1)

            @block.scalar
            def _(act):
                act.copy(xh[:, 4:8, :], core.xT[:, 4:8, :]).then_inc(s["x_high1"], 1)
                for u in range(n_units + 1):
                    if u < n_units:
                        if u % 2 == 0:
                            w.wait(act, first + u // 2)
                        if u >= 2:
                            act.wait_ge(s["unit_used"], u - 1)
                        act.copy(unit(high, u), raw(u)).then_inc(s["weight_high"], 1)
                    step = pending(u, 2)
                    if step is not None:
                        i, half = step
                        act.wait_ge(s["unit_used"], u - 1)
                        if not gated or half == 0:
                            if i >= 2:
                                act.wait_ge(s["hidden_low"], hidden_count(i - 2, yields[-1] if gated else half))
                            act.activation(hidden_piece(i, yields[0] if gated else half), pair(core, i)[half][:],
                                           ACT.Silu if gated else ACT.Relu).then_inc(s["active"], 1)
                    step = pending(u, 3)
                    if step is not None and step[1] in yields:
                        i, half = step
                        act.wait_ge(s["product"], hidden_count(i, half))
                        if i >= 2:
                            act.wait_ge(s["unit_used"], 2 * (downs[i - 2] + 1))
                        act.copy(split_piece(hh, i, half), hidden_piece(i, half)).then_inc(s["hidden_high"], 1)

            @block.vector
            def _(dve):
                dve.tensor_copy(xh[:, 0:4, :], core.xT[:, 0:4, :]).then_inc(s["x_high0"], 1)
                for k in range(2):
                    dve.wait_ge(s[f"x_high{k}"], 1)
                    c = slice(4 * k, 4 * k + 4)
                    dve.tensor_tensor(xl[:, c, :], core.xT[:, c, :], xh[:, c, :], ALU.subtract).then_inc(s["x_low"], 1)
                for u in range(n_units + 1):
                    if u < n_units:
                        dve.wait_ge(s["weight_high"], u + 1)
                        dve.tensor_tensor(unit(low, u), raw(u), unit(high, u), ALU.subtract)\
                           .then_inc(s["weight_low"], 1)
                    step = pending(u, 2)
                    if step is not None and step[1] in yields:
                        i, half = step
                        h = hidden_piece(i, half)
                        if gated:
                            dve.wait_ge(s["unit_used"], u - 1)
                            dve.wait_ge(s["active"], i + 1)
                            other = pair(core, i)[half][:]
                        else:
                            dve.wait_ge(s["active"], hidden_count(i, half))
                            other = h
                        dve.tensor_tensor(h, h, other, ALU.mult).then_inc(s["product"], 1)
                    step = pending(u, 3)
                    if step is not None and step[1] in yields:
                        i, half = step
                        dve.wait_ge(s["hidden_high"], hidden_count(i, half))
                        dve.tensor_tensor(split_piece(hl, i, half), hidden_piece(i, half), split_piece(hh, i, half),
                                          ALU.subtract).then_inc(s["hidden_low"], 1)
                for half in range(2):
                    dve.wait_ge(s["unit_used"], n_units - 1 + half)
                    for t in range(NT):
                        xs = core.x[:, t, half * BANK:(half + 1) * BANK]
                        add_to_x(dve, xs, core.banks[4 + 2 * t + half][:], alpha)


def mlp_plan(steps, up, down, lag=1):
    plan = []
    for i in range(steps + lag):
        if i < steps:
            plan.append(up(i))
        if i >= lag:
            plan.append(down(i - lag))
    return plan


def head_rows(x, chunk=lambda h: h // 2):
    return lambda h: x[HD * (h % 2):HD * (h % 2) + HD, chunk(h), :]


def later_branches(core, w, brT, qT, kT, v, logits):
    br, at = core.part(LOWER, NT, BW)
    logits.append(core.part(at, 4, BANK)[0])
    at += 4 * BANK
    cum, end = core.part(at, T)
    tmp, end = core.part(end, 40)
    decay_stage(core, "decay", core.cproj[:, :, 0:8], core.layer_vectors[:, 0, 2 * KC:], cum, tmp)
    softmax_stage(core, "forget", end, 8, head_rows(qT), head_rows(kT), lambda h, j: v[:, j, h * HD:(h + 1) * HD],
                  lambda h, t: core.const("neg")[:, P * t:P + 2 * P * t], br,
                  bias=(lambda h: core.const("ident")[0:8, h:h + 1].broadcast_to([8, P]), cum[0:8, :]),
                  logits=GateLogits(core, "forget", w, 11, logits[1], (0,)))
    for _ in range(2):
        x, at = core.part(at, BW // P, T)
        brT.append(x)
    turn_stage(core, "b_turn", br, brT[1], BW // P)
    scratch = at - BW // P * T

    start = BW // P * T + 4 * BANK
    flat, end = core.part(start, NT, 9 * P)
    tmp, end = core.part(end, 320)
    rope_stage(core, "rope", core.cproj, flat, core.cos, core.sin, tmp,
               GateLogits(core, "rope", w, 12, logits[1], (1,)))
    third_at = end
    cT, end = core.part(end, 9, T)
    turn_stage(core, "c_fold", flat, cT, 9)
    mask, end = core.part(start, TRI)
    logits.append(core.part(end, 4, BANK)[0])
    end += 4 * BANK
    assert end <= third_at
    indexer_stage(core, "index", scratch, cT, core.cproj[:, :, 1096:1100], mask,
                  GateLogits(core, "index", w, 13, logits[2], (0,)))
    softmax_stage(core, "sparse", scratch, 8, head_rows(cT), head_rows(cT, lambda h: 4 + h // 4),
                  lambda h, j: core.cproj[:, j, 648 + HD * (h // 4):648 + HD * (h // 4) + HD],
                  lambda h, t: mask[:, P * t:P + 2 * P * t], br,
                  logits=GateLogits(core, "sparse", w, 14, logits[2], (1,)))
    turn_stage(core, "c_turn", br, brT[2], BW // P)
    y, at = core.part(at, NT, D)
    gate_stage(core, "gate", end, w, 15, brT, logits, y)
    turn_stage(core, "y_turn", y, core.xT, KC, lambda t, c: y[:, t, c::KC])


def layer(core, w, i):
    vectors = core.sem("layer_vectors")

    def pick_vectors(pool):
        pool.tensor_copy(core.layer_vectors, core.all_vectors[:, bass.ds(i, 1), :]).then_inc(vectors, 1)

    with core.nc.sbuf_tensor("cproj", [P, NT, C_COLS], F32) as cproj, core.scratch("lower", LOWER):
        core.cproj = cproj[:]
        norm_stage(core, "mix_norm", RMS_EPS, core.layer_vectors[:, 0, 0:KC], before=lambda sp: w.fill(sp, 0, 2),
                   pool_first=pick_vectors, vectors=(vectors, 1))
        brT, at = [core.part(0, BW // P, T)[0]], BW // P * T
        logits = [core.part(at, 4, BANK)[0]]
        at += 4 * BANK
        qT, at = core.part(at, 4, T)
        kT, at = core.part(at, 4, T)
        v, at = core.part(at, NT, BW)
        split_projection_stage(core, "a_proj", w, [
            (0, "T", BW, keep_T(core, qT, HD ** -0.5)), (1, "T", BW, keep_T(core, kT)),
            (2, "N", BW, keep_N(core, v))], before=lambda sp: w.fill(sp, 2))
        with core.scratch("upper_a", UPPER, LOWER):
            br, at = core.part(LOWER, NT, BW)
            stick_stage(core, "stick", at, qT, kT, v, br, GateLogits(core, "stick", w, 3, logits[0]))
            turn_stage(core, "a_turn", br, brT[0], BW // P)

        def c_cols(j):
            return core.cproj[:, :, j * BW:min(C_COLS, (j + 1) * BW)]

        split_projection_stage(core, "bc_proj", w, [
            (5, "T", BW, keep_T(core, qT, HD ** -0.5)), (6, "T", BW, keep_T(core, kT)), (7, "N", BW, keep_N(core, v))]
            + [(8 + j, "N", c_cols(j).shape[2], keep_N(core, c_cols(j))) for j in range(3)])
        with core.scratch("upper_bc", UPPER, LOWER):
            later_branches(core, w, brT, qT, kT, v, logits)
    output_stage(core, "mix_out", w, 18)
    with core.scratch("mlp_norm"):
        norm_stage(core, "mlp_norm", RMS_EPS, core.layer_vectors[:, 0, KC:2 * KC])
    mlp_stage(core, "mlp", w, 20, D_FF // BW, gated=False)
    tidy(core, core.sems)


def layer_plan(a, i):
    w_in = rows(a["w_in"][i], KC)
    cols = [(n, n + BW) for n in range(0, 6 * BW, BW)]
    cols += [(6 * BW + j * BW, 6 * BW + min(C_COLS, (j + 1) * BW)) for j in range(3)]
    plan = [(KC, [w_in[:, :, s:e]]) for s, e in cols]
    g = 6 * BW + C_COLS
    gates = [[(KC, [w_in[:, :, s:s + BW]]) for s in (g + b * D, g + b * D + BW)] for b in range(3)]
    plan = plan[0:3] + gates[0] + plan[3:] + gates[1] + gates[2]
    plan += [(BW // P, [rows_by_chunk(a["w_branch"][i, b])]) for b in range(3)]
    w_out = rows(a["w_out"][i], KC)
    plan += [(KC, [w_out[:, :, h * BW:(h + 1) * BW]]) for h in range(2)]
    w_up, w_down = rows(a["w_up"][i], KC), a["w_down"][i]
    plan += mlp_plan(D_FF // BW, lambda n: (KC, [w_up[:, :, n * BW:(n + 1) * BW]]),
                     lambda n: (BW // P, [rows_by_chunk(w_down[n * BW:(n + 1) * BW, :])]))
    return plan


def start_stage(core, a):
    loaded = core.sem("start_loaded")
    with core.nc.Block() as block:
        @block.sync
        def _(sp):
            sp.dma_start(core.consts[:], a["consts"]).then_inc(loaded, 16)
            sp.dma_start(core.x[:], a["x"].rearrange("o (t p) d -> p (o t) d", p=P)).then_inc(loaded, 16)
            for k, name in enumerate(("g_mix", "g_mlp")):
                sp.dma_start(core.all_vectors[:, :, k * KC:(k + 1) * KC],
                             a[name].rearrange("i (p k) -> p i k", k=KC)).then_inc(loaded, 16)
            for i in range(DEPTH):
                sp.dma_start(core.all_vectors[:, i, 2 * KC:], row_broadcast(a["b_forget"][i])).then_inc(loaded, 16)
            core.affine.load_columns(sp, a, loaded)
            core.affine.fetch(sp, "final")
            core.band.load(sp)
            sp.wait_ge(loaded, 16 * (2 + 2 + DEPTH + 3))


def end_stage(core, out):
    stored = core.sem("end_stored")
    with core.nc.Block() as block:
        @block.sync
        def _(sp):
            sp.dma_start(out.rearrange("o (t p) d -> p (o t) d", p=P), core.x[:]).then_inc(stored, 16)
            sp.wait_ge(stored, 16)


def build(nc, a, out):
    ctx = ExitStack()
    with ctx:
        core = Core(nc, ctx)
        core.cos = core.sbuf("cos", [P, NT, ROT // 2])
        core.sin = core.sbuf("sin", [P, NT, ROT // 2])
        core.all_vectors = core.sbuf("all_vectors", [P, DEPTH, 3 * KC])
        core.layer_vectors = core.sbuf("layer_vectors", [P, 1, 3 * KC])
        core.affine = Affine(core, a)
        core.band = Band(core, a)
        start_stage(core, a)
        with core.scratch("start"):
            tmp, _ = core.part(0, 36)
            angles_stage(core, a["positions"], core.cos, core.sin, tmp)
        with core.weight_ring("dense", SLOTS):
            with core.semaphores():
                first = Weights(core, "layer", SLOTS, None)
                with nc.Fori(0, DEPTH) as i:
                    first.plan = layer_plan(a, i)
                    layer(core, first, i)
            second_block(core, a)
        with core.weight_ring("moe", MOE_SLOTS), core.scratch("moe", MOE_ARENA):
            moe_stages(core, a)
            norm_stage(core, "ln11", LN_EPS, core.affine.gain[:, 4, :], core.affine.shift[:, 4, :], natural=True)
        end_stage(core, out)


def gdn_projection(core, w):
    def first(sp):
        w.fill(sp, 2)
        core.affine.fetch(sp, "ln00")

    raw, end = core.part(0, 16, PAD + T)
    z, end = core.part(end, NT, D)
    ba, end = core.part(end, NT, 16)
    assert end == GDN_LOWER

    def keep_raw(c0):
        return keep_T(core, raw[:, c0:c0 + 4, PAD:PAD + T])

    split_projection_stage(core, "gdn_proj", w, [(c, "T", BW, keep_raw(4 * c)) for c in range(4)]
                     + [(4, "N", 16, keep_N(core, ba))], before=first)
    return raw, z, ba


def gdn_stages(core, a, w, raw, z, ba, more):
    free = {"slot0": core.ring[:, 0, :], "slot3": core.ring[:, 3, :],
            "slots4-5": core.ring[:, 4:SLOTS, :].rearrange("p a b -> p (a b)"), "more": more}
    at = {name: 0 for name in free}

    def extra(*shape, where="slots4-5"):
        n = int(np.prod(shape))
        assert at[where] + n <= free[where].shape[1]
        v = free[where][:, at[where]:at[where] + n]
        at[where] += n
        if len(shape) == 2:
            v = v.rearrange("p (a b) -> p a b", a=shape[0])
        if len(shape) == 3:
            v = v.rearrange("p (a b c) -> p a b c", a=shape[0], b=shape[1])
        return v

    end = GDN_LOWER
    conv = extra(16, T, where="slot3")

    wconv, end2 = core.part(end, CONV * 16)
    wload, end2 = core.part(end2, P)
    conv_stage(core, a, w, 5, raw, conv, wload, wconv, z, ba)
    core.band.prepare_stage()
    sq, end2 = core.part(end, 8, T)
    rn, end2 = core.part(end2, 8, T)
    qk_norm_stage(core, w, 6, z, conv, sq, rn)
    kv, raw_end = core.part(0, NT, 12, P)
    order = [(b // 12, b % 12) for b in range(24)]
    turn_stage(core, "kv_turn", None, kv.rearrange("p t c d -> p (t c d)").rearrange("p (a b) -> p a b", b=T), 12,
               lambda t, c: conv[:, 4 + order[2 * c + t][1], order[2 * c + t][0] * P:(order[2 * c + t][0] + 1) * P])
    g = {}
    for name in ("g", "gc", "eg", "minus"):
        g[name], raw_end = core.part(raw_end, NT, 8)
    for name in ("last", "dec", "be", "alog", "dt"):
        g[name], raw_end = core.part(raw_end, 8)
    kbg, end2 = core.part(end, 8, P)
    kdec, end2 = core.part(end2, 8, P)
    qd, end2 = core.part(end2, 8, P)
    o, end2 = core.part(end2, NT, D)
    assert raw_end <= 16 * (PAD + T)
    beta = ba[:, :, 0:8]
    gdn_decay_stage(core, a, ba, beta, g, kv, kbg, kdec)
    AT, S, TT, qkT = extra(16, P), extra(16, P), extra(16, P), extra(16, P)
    kb = extra(16, P, where="slot0")
    W, B, DT = extra(4, 4, P, where="slot0"), extra(4, 4, P, where="more"), extra(4, 4, P, where="more")
    gdn_scores_stage(core, conv, beta, g, kb, qd, DT, AT, qkT)
    gdn_inverse_stage(core, AT, S, TT, W, B)
    gdn_scan_stage(core, S, qkT, kv, kbg, kdec, qd, kb[:, 0:8, :], kb[:, 8:16, :], TT[:, 0:8, :], TT[:, 8:16, :], o)
    gdn_out_stage(core, a, o, z, sqo=AT.rearrange("p a b -> p (a b)"), st=core.part(end2, 16)[0],
                  nw=core.part(end2 + 16, P)[0])
    turn_stage(core, "gdn_turn", o, core.xT, KC, lambda t, c: o[:, t, c::KC])



def z_products(pe, core, w, tile):
    w.wait(pe, tile)
    for t in range(NT):
        for c in range(KC):
            mm = pe.matmul(core.banks[6 + t][:], core.xT[:, c, t * P:(t + 1) * P], w.tile(tile, KC, BW)[:, c, :],
                           start=(c == 0), stop=(c == KC - 1))
    mm.then_inc(w.tile_used, 1)


def z_silu(act, core, w, tile, z, half):
    act.wait_ge(w.tile_used, tile + 1)
    for t in range(NT):
        act.activation(z[:, t, half * BANK:(half + 1) * BANK], core.banks[6 + t][:], ACT.Silu)


def conv_stage(core, a, w, first, raw, conv, wload, wconv, z, ba):
    nc = core.nc
    s = {n: core.sem(f"conv_{n}") for n in ("loaded", "turned", "taps", "padded", "tap", "silu")}
    with nc.Block() as block:
        @block.sync
        def _(sp):
            sp.dma_start(wload[0:CONV * 16, :], a["a_conv_w_2"][0].rearrange("j (c p) -> (j c) p", p=P))\
              .then_inc(s["loaded"], 16)

        @block.tensor
        def _(pe):
            pe.wait_ge(s["loaded"], 16)
            pe.transpose(core.banks[0][:, 0:CONV * 16], wload[0:CONV * 16, :], core.const("ident")[0:64, 0:64])\
              .then_inc(s["turned"], 1)
            z_products(pe, core, w, first)

        @block.vector
        def _(dve):
            dve.memset(raw[:, :, 0:PAD], 0.0).then_inc(s["padded"], 1)
            dve.wait_ge(s["padded"], 1)
            dve.wait_ge(s["turned"], 1)
            dve.tensor_copy(wconv, core.banks[0][:, 0:CONV * 16]).then_inc(s["taps"], 1)
            dve.wait_ge(s["taps"], 1)
            n = 0
            for group in range(4):
                for j in range(CONV):
                    for c in range(4 * group, 4 * group + 4):
                        tap = wconv[:, j * 16 + c:j * 16 + c + 1]
                        if j == 0:
                            op = dve.tensor_scalar(conv[:, c, :], raw[:, c, 0:T], tap, None, ALU.mult)
                        else:
                            dve.wait_ge(s["tap"], n - 3)
                            op = dve.scalar_tensor_tensor(out=conv[:, c, :], in0=raw[:, c, j:j + T], scalar=tap,
                                                          in1=conv[:, c, :], op0=ALU.mult, op1=ALU.add)
                        op.then_inc(s["tap"], 1)
                        n += 1

        @block.scalar
        def _(act):
            act.activation(ba[:, :, 0:8], ba[:, :, 0:8], ACT.Sigmoid)
            for group in range(4):
                act.wait_ge(s["tap"], 16 * (group + 1))
                act.activation(conv[:, 4 * group:4 * group + 4, :], conv[:, 4 * group:4 * group + 4, :], ACT.Silu)
                if group == 2:
                    z_silu(act, core, w, first, z, 0)


def qk_norm_stage(core, w, tile, z, conv, sq, rn):
    nc = core.nc
    s = {n: core.sem(f"qknorm_{n}") for n in ("squares", "sums", "shifted", "root", "inverse")}
    with nc.Block() as block:
        @block.gpsimd
        def _(pool):
            for c in range(8):
                pool.tensor_tensor(sq[:, c, :], conv[:, c, :], conv[:, c, :], ALU.mult).then_inc(s["squares"], 1)

        @block.tensor
        def _(pe):
            for n in range(4):
                pe.wait_ge(s["squares"], 2 * (n + 1))
                pe.matmul(core.banks[n][:], core.const("ones"), sq[:, 2 * n:2 * n + 2, :].rearrange("p a b -> p (a b)"),
                          start=True, stop=True).then_inc(s["sums"], 1)
            z_products(pe, core, w, tile)

        @block.vector
        def _(dve):
            for n in range(4):
                dve.wait_ge(s["sums"], n + 1)
                dve.tensor_scalar(rn[:, 2 * n:2 * n + 2, :].rearrange("p a b -> p (a b)"), core.banks[n][:], GDN_EPS,
                                  None, ALU.add).then_inc(s["shifted"], 1)
            for n in range(4):
                v = rn[:, 2 * n:2 * n + 2, :]
                dve.wait_ge(s["root"], n + 1)
                dve.reciprocal(v, v).then_inc(s["inverse"], 1)
                dve.wait_ge(s["inverse"], n + 1)
                q = conv[:, 2 * n:2 * n + 2, :]
                dve.scalar_tensor_tensor(out=q, in0=v, scalar=GDK ** -0.5 if n < 2 else 1.0, in1=q, op0=ALU.mult,
                                         op1=ALU.mult)

        @block.scalar
        def _(act):
            for n in range(4):
                act.wait_ge(s["shifted"], n + 1)
                v = rn[:, 2 * n:2 * n + 2, :]
                act.activation(v, v, ACT.Sqrt).then_inc(s["root"], 1)
            z_silu(act, core, w, tile, z, 1)


def gdn_decay_stage(core, a, ba, beta, g, kv, kbg, kdec):
    nc = core.nc
    s = {n: core.sem(f"gdecay_{n}") for n in ("loaded", "exp", "step", "log", "g", "sums", "exps")}
    u = ba[:, :, 8:16]
    with nc.Block() as block:
        @block.sync
        def _(sp):
            sp.dma_start(g["alog"], row_broadcast(a["a_a_log_2"][0])).then_inc(s["loaded"], 16)
            sp.dma_start(g["dt"], row_broadcast(a["a_dt_bias_2"][0])).then_inc(s["loaded"], 16)

        @block.scalar
        def _(act):
            act.wait_ge(s["loaded"], 32)
            act.activation(g["alog"], g["alog"], ACT.Exp).then_inc(s["exp"], 1)
            act.wait_ge(s["step"], 2)
            act.activation(g["minus"], g["minus"], ACT.Exp).then_inc(s["exp"], 1)
            act.wait_ge(s["exp"], 2)
            act.activation(g["minus"], g["minus"], ACT.Ln, bias=1.0).then_inc(s["log"], 1)
            act.wait_ge(s["exps"], 1)
            act.activation(g["eg"], g["gc"], ACT.Exp).then_inc(s["exp"], 1)
            act.activation(g["dec"], g["dec"], ACT.Exp).then_inc(s["exp"], 1)

        @block.vector
        def _(dve):
            step = [0]

            def then(op):
                op.then_inc(s["step"], 1)
                step[0] += 1
                dve.wait_ge(s["step"], step[0])

            dve.wait_ge(s["loaded"], 32)
            then(dve.tensor_tensor(u, u, g["dt"].rearrange("p (o h) -> p o h", o=1).broadcast_to([P, NT, 8]), ALU.add))
            then(dve.scalar_tensor_tensor(out=g["minus"], in0=u, scalar=-1.0, in1=u, op0=ALU.mult, op1=ALU.min))
            dve.wait_ge(s["log"], 1)
            then(dve.scalar_tensor_tensor(out=g["g"], in0=u, scalar=0.0, in1=g["minus"], op0=ALU.max, op1=ALU.add))
            dve.wait_ge(s["exp"], 1)
            dve.scalar_tensor_tensor(out=g["g"], in0=g["g"], scalar=-1.0,
                                     in1=g["alog"].rearrange("p (o h) -> p o h", o=1).broadcast_to([P, NT, 8]),
                                     op0=ALU.mult, op1=ALU.mult).then_inc(s["g"], 1)
            dve.wait_ge(s["sums"], 1)
            then(dve.tensor_copy(g["gc"], core.banks[0][:, 0:16].rearrange("p (t h) -> p t h", t=NT)))
            then(dve.tensor_copy(g["last"], core.banks[0][:, 16:24]))
            dve.tensor_tensor(g["dec"], g["last"], g["gc"][:, 0, :], ALU.subtract).then_inc(s["exps"], 1)
            for t in range(NT):
                dve.tensor_tensor(kv[:, t, 4:12, :], kv[:, t, 4:12, :],
                                  beta[:, t, :].rearrange("p (h o) -> p h o", o=1).broadcast_to([P, 8, P]), ALU.mult)
            dve.wait_ge(s["exp"], 4)
            then(dve.tensor_tensor(g["be"], g["eg"][:, 1, :], beta[:, 1, :], ALU.mult))
            for out, t, factor in ((kbg, 1, g["be"]), (kdec, 0, g["dec"])):
                for r in range(2):
                    dve.tensor_tensor(out[:, r::2, :], kv[:, t, 0:4, :],
                                      factor[:, r::2].rearrange("p (h o) -> p h o", o=1).broadcast_to([P, 4, P]),
                                      ALU.mult)

        @block.tensor
        def _(pe):
            pe.wait_ge(s["g"], 1)
            gs = g["g"].rearrange("p t h -> p (t h)")
            pe.matmul(core.banks[0][:, 0:16], core.const("le"), gs, start=True, stop=True)
            pe.matmul(core.banks[0][:, 16:24], core.const("ones"), gs[:, 0:8], start=True, stop=True)\
              .then_inc(s["sums"], 1)


def gdn_scores_stage(core, conv, beta, g, kb, qd, DT, AT, qkT):
    nc = core.nc
    s = {n: core.sem(f"gscore_{n}") for n in ("rows", "diff", "decay", "kb", "qd_exp", "dots", "AT", "qk")}
    groups = [(n // 2, 4 * (n % 2)) for n in range(4)]
    with nc.Block() as block:
        @block.tensor
        def _(pe):
            def row_sums(n):
                t, h0 = groups[n]
                if n >= 1:
                    pe.wait_ge(s["kb"], n)
                    pe.wait_ge(s["diff"], n)
                    if n >= 3:
                        pe.wait_ge(s["qd_exp"], n - 2)
                for h in range(4):
                    pe.matmul(core.banks[0][:, h * P:(h + 1) * P], g["g"][:, t, h0 + h:h0 + h + 1].broadcast_to([P, P]),
                              core.const("le"), start=True, stop=True)
                for h in range(4):
                    mm = pe.matmul(core.banks[1][:, h * P:(h + 1) * P],
                                   beta[:, t, h0 + h:h0 + h + 1].broadcast_to([P, P]), core.const("ident"),
                                   start=True, stop=True)
                mm.then_inc(s["rows"], 1)

            for n, (t, h0) in enumerate(groups):
                row_sums(n)
                pe.wait_ge(s["kb"], n + 1)
                if n >= 2:
                    pe.wait_ge(s["AT"], n - 1)
                    pe.wait_ge(s["qk"], n - 1)
                ts = slice(t * P, (t + 1) * P)
                for h in range(4):
                    k = conv[:, 4 + (h0 + h) // 2, ts]
                    pe.matmul(core.banks[2 + 2 * (n % 2)][:, h * P:(h + 1) * P], k, kb[:, 4 * n + h, :], start=True,
                              stop=True)
                    mm = pe.matmul(core.banks[3 + 2 * (n % 2)][:, h * P:(h + 1) * P], k, conv[:, (h0 + h) // 2, ts],
                                   start=True, stop=True)
                mm.then_inc(s["dots"], 1)

        @block.vector
        def _(dve):
            def scores(n):
                bank = 2 + 2 * (n % 2)
                dve.wait_ge(s["dots"], n + 1)
                dve.wait_ge(s["decay"], n + 1)
                d = DT[:, n, :, :].rearrange("p a b -> p (a b)")
                dve.tensor_tensor(AT[:, 4 * n:4 * n + 4, :].rearrange("p a b -> p (a b)"), core.banks[bank][:], d,
                                  ALU.mult).then_inc(s["AT"], 1)
                dve.tensor_tensor(qkT[:, 4 * n:4 * n + 4, :].rearrange("p a b -> p (a b)"), core.banks[bank + 1][:],
                                  d, ALU.mult).then_inc(s["qk"], 1)

            for n, (t, h0) in enumerate(groups):
                dve.wait_ge(s["rows"], n + 1)
                for j in range(2):
                    k = conv[:, 4 + h0 // 2 + j:5 + h0 // 2 + j, t * P:(t + 1) * P].broadcast_to([P, 2, P])
                    op = dve.tensor_tensor(kb[:, 4 * n + 2 * j:4 * n + 2 * j + 2, :],
                                           core.banks[1][:, 2 * j * P:(2 * j + 2) * P]
                                           .rearrange("p (a b) -> p a b", a=2), k, ALU.mult)
                op.then_inc(s["kb"], 1)
                for h in range(4):
                    op = dve.tensor_scalar(DT[:, n, h, :], core.banks[0][:, h * P:(h + 1) * P],
                                           g["gc"][:, t, h0 + h:h0 + h + 1], 0.0, ALU.subtract, ALU.min)
                op.then_inc(s["diff"], 1)
                scores(n)
            for n in (2, 3):
                dve.wait_ge(s["qd_exp"], n - 1)
                h0 = groups[n][1]
                for j in range(2):
                    out = qd[:, h0 + 2 * j:h0 + 2 * j + 2, :]
                    dve.tensor_tensor(out, out, conv[:, h0 // 2 + j:h0 // 2 + j + 1, P:T].broadcast_to([P, 2, P]),
                                      ALU.mult)

        @block.scalar
        def _(act):
            for n, (t, h0) in enumerate(groups):
                act.wait_ge(s["diff"], n + 1)
                if t == 1:
                    act.activation(qd[:, h0:h0 + 4, :].rearrange("p a b -> p (a b)"), core.banks[0][:], ACT.Exp)\
                       .then_inc(s["qd_exp"], 1)
                act.activation(DT[:, n, :, :], DT[:, n, :, :], ACT.Exp).then_inc(s["decay"], 1)

        @block.gpsimd
        def _(pool):
            for n in range(4):
                for x, name, keep in ((AT, "AT", ALU.is_gt), (qkT, "qk", ALU.is_ge)):
                    pool.wait_ge(s[name], n + 1)
                    v = x[:, 4 * n:4 * n + 4, :]
                    pool.affine_select(out=v, in_=v, pattern=[[0, 4], [1, P]], compare_op=keep, fill=0.0, base=0,
                                       channel_multiplier=-1)


def gdn_inverse_stage(core, AT, S, TT, W, B):
    nc = core.nc
    s = {n: core.sem(f"ginv_{n}") for n in ("masked", "S0", "T_turned", "T0", "W_dots", "W", "TWT", "SWS", "T", "S")}
    grp = [slice(4 * n, 4 * n + 4) for n in range(4)]

    def flat(x):
        return x.rearrange("p a b -> p (a b)")

    def each(k):
        return core.level(k).rearrange("p (o m) -> p o m", o=1).broadcast_to([P, 4, P])

    with nc.Block() as block:
        @block.gpsimd
        def _(pool):
            for k in range(LEVELS):
                for n in range(4):
                    if k >= 1:
                        pool.wait_ge(s["S0"], n + 1) if k == 1 else pool.wait_ge(s["W_dots"], 4 * (k - 2) + n + 1)
                    pool.tensor_tensor(B[:, n, :, :], AT[:, grp[n], :], each(k), ALU.mult).then_inc(s["masked"], 1)

        @block.tensor
        def _(pe):
            for n in range(4):
                pe.wait_ge(s["S0"], n + 1)
                for h in range(4):
                    mm = pe.transpose(core.banks[n][:, h * P:(h + 1) * P], S[:, 4 * n + h, :], core.const("ident"))
                mm.then_inc(s["T_turned"], 1)
            for k in range(1, LEVELS):
                for n in range(4):
                    pe.wait_ge(s["masked"], 4 * k + n + 1)
                    if k == 1:
                        pe.wait_ge(s["T0"], n + 1)
                        pe.wait_ge(s["T0"], min(4, n + 3))
                    else:
                        pe.wait_ge(s["T"], 4 * (k - 2) + n + 1)
                    if n >= 2 or k >= 2:
                        m = 4 * (k - 1) + n
                        pe.wait_ge(s["W"], m - 1)
                    for h in range(4):
                        mm = pe.matmul(core.banks[n % 2][:, h * P:(h + 1) * P], B[:, n, h, :], TT[:, 4 * n + h, :],
                                       start=True, stop=True)
                    mm.then_inc(s["W_dots"], 1)
                for n in range(4):
                    m = 4 * (k - 1) + n
                    pe.wait_ge(s["W"], m + 1)
                    if m >= 2:
                        pe.wait_ge(s["S"], m - 1)
                    if k < LEVELS - 1:
                        for h in range(4):
                            mm = pe.matmul(core.banks[2 + n % 2][:, h * P:(h + 1) * P], S[:, 4 * n + h, :],
                                           W[:, n, h, :], start=True, stop=True)
                        mm.then_inc(s["TWT"], 1)
                    for h in range(4):
                        mm = pe.matmul(core.banks[4 + n % 2][:, h * P:(h + 1) * P], W[:, n, h, :],
                                       S[:, 4 * n + h, :], start=True, stop=True)
                    mm.then_inc(s["SWS"], 1)

        @block.scalar
        def _(act):
            for k in range(1, LEVELS):
                for n in range(4):
                    act.wait_ge(s["W_dots"], 4 * (k - 1) + n + 1)
                    if k >= 2:
                        act.wait_ge(s["SWS"], 4 * (k - 2) + n + 1)
                    act.copy(flat(W[:, n, :, :]), core.banks[n % 2][:]).then_inc(s["W"], 1)

        @block.vector
        def _(dve):
            for n in range(4):
                dve.wait_ge(s["masked"], n + 1)
                dve.tensor_tensor(S[:, grp[n], :], core.const("ident").rearrange("p (o m) -> p o m", o=1)
                                  .broadcast_to([P, 4, P]), B[:, n, :, :], ALU.subtract).then_inc(s["S0"], 1)
            for n in range(4):
                dve.wait_ge(s["T_turned"], n + 1)
                dve.tensor_copy(flat(TT[:, grp[n], :]), core.banks[n][:]).then_inc(s["T0"], 1)
            for k in range(1, LEVELS):
                for n in range(4):
                    m = 4 * (k - 1) + n
                    dve.wait_ge(s["SWS"], m + 1)
                    if k < LEVELS - 1:
                        dve.wait_ge(s["TWT"], m + 1)
                        dve.tensor_tensor(flat(TT[:, grp[n], :]), flat(TT[:, grp[n], :]), core.banks[2 + n % 2][:],
                                          ALU.subtract).then_inc(s["T"], 1)
                    dve.tensor_tensor(flat(S[:, grp[n], :]), flat(S[:, grp[n], :]), core.banks[4 + n % 2][:],
                                      ALU.subtract).then_inc(s["S"], 1)


def gdn_scan_stage(core, S, qkT, kv, kbg, kdec, qd, vn0, vn1, state, wT, o):
    nc = core.nc
    s = {n: core.sem(f"gscan_{n}") for n in ("u0", "vn0", "w", "wT", "s1", "state", "u1", "vn1", "o0", "o1")}

    def flat(x):
        return x.rearrange("p a b -> p (a b)")

    with nc.Block() as block:
        @block.tensor
        def _(pe):
            def per_head(bank, g, products, sem):
                for h in range(4 * g, 4 * g + 4):
                    ps = products(h)
                    for i, (lhs, rhs) in enumerate(ps):
                        mm = pe.matmul(bank[:, (h % 4) * P:(h % 4 + 1) * P], lhs, rhs, start=(i == 0),
                                       stop=(i == len(ps) - 1))
                mm.then_inc(s[sem], 1)

            for g in range(2):
                per_head(core.banks[g], g, lambda h: [(S[:, h, :], kv[:, 0, 4 + h, :])], "u0")
            for g in range(2):
                per_head(core.banks[2 + g], g, lambda h: [(kbg[:, h, :], S[:, 8 + h, :])], "w")
            for g in range(2):
                pe.wait_ge(s["vn0"], g + 1)
                per_head(core.banks[4 + g], g, lambda h: [(kdec[:, h, :], vn0[:, h, :])], "s1")
            for g in range(2):
                per_head(core.banks[6 + g], g, lambda h: [(qkT[:, h, :], vn0[:, h, :])], "o0")
            for g in range(2):
                pe.wait_ge(s["state"], g + 1)
                pe.wait_ge(s["wT"], g + 1)
                per_head(core.banks[g], g, lambda h: [(S[:, 8 + h, :], kv[:, 1, 4 + h, :]),
                                                      (wT[:, h, :], state[:, h, :])], "u1")
            for g in range(2):
                pe.wait_ge(s["vn1"], g + 1)
                per_head(core.banks[2 + g], g, lambda h: [(qkT[:, 8 + h, :], vn1[:, h, :]),
                                                          (qd[:, h, :], state[:, h, :])], "o1")

        @block.vector
        def _(dve):
            for g in range(2):
                dve.wait_ge(s["u0"], g + 1)
                dve.tensor_copy(flat(vn0[:, 4 * g:4 * g + 4, :]), core.banks[g][:]).then_inc(s["vn0"], 1)
            for g in range(2):
                dve.wait_ge(s["s1"], g + 1)
                dve.tensor_copy(flat(state[:, 4 * g:4 * g + 4, :]), core.banks[4 + g][:]).then_inc(s["state"], 1)
            for g in range(2):
                dve.wait_ge(s["u1"], g + 1)
                dve.tensor_copy(flat(vn1[:, 4 * g:4 * g + 4, :]), core.banks[g][:]).then_inc(s["vn1"], 1)
            for g in range(2):
                dve.wait_ge(s["o1"], g + 1)
                dve.tensor_copy(o[:, 1, g * BANK:(g + 1) * BANK], core.banks[2 + g][:])

        @block.scalar
        def _(act):
            for g in range(2):
                act.wait_ge(s["w"], g + 1)
                act.mul(flat(wT[:, 4 * g:4 * g + 4, :]), core.banks[2 + g][:], -1.0).then_inc(s["wT"], 1)
            for g in range(2):
                act.wait_ge(s["o0"], g + 1)
                act.copy(o[:, 0, g * BANK:(g + 1) * BANK], core.banks[6 + g][:])


def gdn_out_stage(core, a, o, z, sqo, st, nw):
    nc = core.nc
    s = {n: core.sem(f"gout_{n}") for n in ("loaded", "square", "sum", "mean", "root", "inverse", "step", "gated")}
    oh = o.rearrange("p t (h d) -> p (t h) d", d=P)
    sqh = sqo.rearrange("p (n d) -> p n d", d=P)
    nwb = nw.rearrange("p (o d) -> p o d", o=1).broadcast_to([P, 8, P])
    with nc.Block() as block:
        @block.sync
        def _(sp):
            sp.dma_start(nw, row_broadcast(a["a_norm_w_2"][0])).then_inc(s["loaded"], 16)

        @block.gpsimd
        def _(pool):
            pool.wait_ge(s["loaded"], 16)
            for t in range(NT):
                pool.wait_ge(s["square"], t + 1)
                v = z[:, t, :].rearrange("p (h d) -> p h d", d=P)
                pool.tensor_tensor(v, v, nwb, ALU.mult).then_inc(s["gated"], 1)

        @block.scalar
        def _(act):
            for t in range(NT):
                act.activation(sqo[:, t * D:(t + 1) * D], o[:, t, :], ACT.Square).then_inc(s["square"], 1)
            act.wait_ge(s["mean"], 1)
            act.activation(st, st, ACT.Sqrt).then_inc(s["root"], 1)

        @block.vector
        def _(dve):
            for t in range(NT):
                dve.wait_ge(s["square"], t + 1)
                dve.reduce_sum(st[:, 8 * t:8 * t + 8], sqh[:, 8 * t:8 * t + 8, :], AX_X).then_inc(s["sum"], 1)
            dve.wait_ge(s["sum"], NT)
            dve.tensor_scalar(st, st, 1.0 / P, GDN_EPS, ALU.mult, ALU.add).then_inc(s["mean"], 1)
            dve.wait_ge(s["root"], 1)
            dve.reciprocal(st, st).then_inc(s["inverse"], 1)
            dve.wait_ge(s["inverse"], 1)
            for t in range(NT):
                v = oh[:, 8 * t:8 * t + 8, :]
                dve.tensor_tensor(v, v, st[:, 8 * t:8 * t + 8].rearrange("p (h o) -> p h o", o=1)
                                  .broadcast_to([P, 8, P]), ALU.mult).then_inc(s["step"], 1)
            for t in range(NT):
                dve.wait_ge(s["step"], t + 1)
                dve.wait_ge(s["gated"], t + 1)
                dve.tensor_tensor(o[:, t, :], o[:, t, :], z[:, t, :], ALU.mult)


class Band:

    def __init__(self, core, a):
        self.core, self.a = core, a
        self.rows = core.sbuf("band_rows", [SWA_HEADS, TRI])
        self.rel = core.sbuf("rel_bias", [BUCKETS, SWA_HEADS])
        small = core.sbuf("swa_vectors", [P, 160])
        self.bq, self.bk, self.bv, self.sink = small[:, 0:8], small[:, 8:10], small[:, 16:144], small[:, 144:160]
        self.copies = core.nc.dram_tensor("band_copies", [P, SWA_HEADS, TRI], F32).ap()
        self.sems = {n: core.sem(f"band_{n}") for n in ("loaded", "row", "windowed", "stored", "back")}

    def load(self, sp):
        b = self.a["b_b_in_2"][0]
        q_dim = SWA_HEADS * HD
        loaded = self.sems["loaded"]
        sp.dma_start(self.rel, self.a["rel_bias_2"]).then_inc(loaded, 16)
        sp.dma_start(self.sink, row_broadcast(self.a["b_sinks_2"][0])).then_inc(loaded, 16)
        sp.dma_start(self.bq, b[0:q_dim].rearrange("(c p) -> p c", p=P), allow_slow_non_contiguous=True)\
          .then_inc(loaded, 16)
        for r in range(2):
            sp.dma_start(self.bk[HD * r:HD * r + HD, :], b[q_dim:q_dim + P].rearrange("(c p) -> p c", p=HD),
                         allow_slow_non_contiguous=True).then_inc(loaded, 16)
        sp.dma_start(self.bv, row_broadcast(b[q_dim + P:q_dim + 2 * P])).then_inc(loaded, 16)

    def prepare_stage(self):
        core, s = self.core, self.sems
        with core.nc.Block() as block:
            @block.sync
            def _(sp):
                sp.wait_ge(s["windowed"], 1)
                sp.dma_start(self.copies.rearrange("i h v -> h i v"),
                             self.rows.rearrange("h (o v) -> h o v", o=1).broadcast_to([SWA_HEADS, P, TRI]))\
                  .then_inc(s["stored"], 16)

            @block.tensor
            def _(pe):
                pe.wait_ge(s["loaded"], 16 * 6)
                pe.matmul(core.banks[0][0:SWA_HEADS, 0:TRI], self.rel, core.const("bucket")[0:BUCKETS, :],
                          start=True, stop=True).then_inc(s["row"], 1)

            @block.vector
            def _(dve):
                dve.wait_ge(s["row"], 1)
                dve.tensor_tensor(self.rows, core.banks[0][0:SWA_HEADS, 0:TRI],
                                  core.const("window")[0:SWA_HEADS, :], ALU.add).then_inc(s["windowed"], 1)

            @block.scalar
            def _(act):
                act.wait_ge(s["loaded"], 16 * 6)
                act.mul(self.bq, self.bq, HD ** -0.5)

    def fetch(self, sp, bias):
        sp.wait_ge(self.sems["stored"], 16)
        sp.dma_start(bias, bass.AP(self.copies.tensor, P - 1, [[SWA_HEADS * TRI - 1, P], [TRI, SWA_HEADS], [1, T]]))\
          .then_inc(self.sems["back"], 16)


def swa_stages(core, w, first):
    qT, at = core.part(0, 8, T)
    kT, at = core.part(at, 2, T)
    v, at = core.part(at, NT, P)
    bias, at = core.part(at, SWA_HEADS, T)
    out, at = core.part(at, NT, D)
    bq, bk, bv, sink = core.band.bq, core.band.bk, core.band.bv, core.band.sink

    def fetch(sp):
        core.band.fetch(sp, bias)
        core.affine.fetch(sp, "ln10")

    def with_bias(dst, cols, c0, factor):
        def store(eng, half, bank):
            for j in range(2):
                c = c0 + 2 * half + j
                out_, in_ = dst[:, c, :], bank[:, j * T:(j + 1) * T]
                if eng is core.nc.scalar:
                    op = eng.activation(out_, in_, ACT.Identity, bias=cols[:, c:c + 1], scale=factor)
                else:
                    op = eng.tensor_scalar(out_, in_, factor, cols[:, c:c + 1], ALU.mult, ALU.add)
            return op
        return store

    def keep_kv(eng, half, bank):
        if half == 0:
            return with_bias(kT, bk, 0, 1.0)(eng, 0, bank)
        for t in range(NT):
            op = eng.tensor_tensor(v[:, t, :], bank[:, t * P:(t + 1) * P], bv, ALU.add)
        return op

    projection_stage(core, "swa_proj", w, [(first, "T", BW, with_bias(qT, bq, 0, HD ** -0.5)),
                                           (first + 1, "T", BW, with_bias(qT, bq, 4, HD ** -0.5)),
                                           (first + 2, "KV", 3 * P, keep_kv)], before=fetch)
    softmax_stage(core, "swa", at, SWA_HEADS, lambda h: qT[HD * (h % 2):HD * (h % 2) + HD, h // 2, :],
                  lambda h: kT[HD * (h % 2):HD * (h % 2) + HD, h // 8, :],
                  lambda h, j: v[:, j, (h // 8) * HD:(h // 8 + 1) * HD],
                  lambda h, t: bias[:, h, P:T] if t == 0 else bias[:, h, :], out, sink=sink,
                  ready=(core.band.sems["back"], 16))
    turn_stage(core, "swa_turn", out, core.xT, KC, lambda t, c: out[:, t, c::KC])


def router_stage(core, a, r, acc, fill):
    nc = core.nc
    s = {n: core.sem(f"route_{n}") for n in ("loaded", "logits", "step", "exp", "chosen", "ranks")}
    lg, top, oh, sel = r["logits"], r["top"], r["onehot"], r["sel"]
    with nc.Block() as block:
        @block.sync
        def _(sp):
            sp.dma_start(r["w"], rows(a["moe_router_2"][0], KC)).then_inc(s["loaded"], 16)
            fill(sp)

        @block.tensor
        def _(pe):
            pe.wait_ge(s["loaded"], 16)
            for t in range(NT):
                for c in range(KC):
                    mm = pe.matmul(core.banks[0][:, E * t:E * t + E], core.xT[:, c, t * P:(t + 1) * P], r["w"][:, c, :],
                                   start=(c == 0), stop=(c == KC - 1))
            mm.then_inc(s["logits"], 1)
            pe.wait_ge(s["chosen"], 1)
            bank = core.banks[1]
            pe.matmul(bank[:, 0:E], core.const("lt"), sel[:, 0, :], start=True, stop=True)
            pe.matmul(bank[:, E:2 * E], core.const("lt"), sel[:, 1, :], start=True, stop=False)
            pe.matmul(bank[:, E:2 * E], core.const("ones"), sel[:, 0, :], start=False, stop=True)
            pe.matmul(bank[:, 2 * E:3 * E], core.const("ones"), sel[:, 0, :], start=True, stop=False)
            pe.matmul(bank[:, 2 * E:3 * E], core.const("ones"), sel[:, 1, :], start=False, stop=True)\
              .then_inc(s["ranks"], 1)

        @block.scalar
        def _(act):
            for t in range(NT):
                act.mul(acc[:, t, :], core.x[:, t, :], ALPHA)
            act.wait_ge(s["exp"], 1)
            act.activation(r["e"], r["e"], ACT.Exp).then_inc(s["exp"], 1)

        @block.vector
        def _(dve):
            step = [0]

            def then(op):
                op.then_inc(s["step"], 1)
                step[0] += 1
                dve.wait_ge(s["step"], step[0])

            dve.wait_ge(s["logits"], 1)
            then(dve.tensor_copy(lg.rearrange("p t e -> p (t e)"), core.banks[0][:, 0:NT * E]))
            for t in range(NT):
                then(dve.max(top[:, t, :], lg[:, t, :]))
                then(dve.max_index(r["index"][:, t, :], top[:, t, :], lg[:, t, :]))
            dve.tensor_tensor(r["e"], top[:, :, 1:2].rearrange("p t o -> p (t o)"),
                              top[:, :, 0:1].rearrange("p t o -> p (t o)"), ALU.subtract).then_inc(s["exp"], 1)
            then(dve.tensor_copy(r["indexf"], r["index"]))
            dve.wait_ge(s["exp"], 2)
            then(dve.tensor_scalar(r["p"], r["e"], 1.0, None, ALU.add))
            then(dve.reciprocal(r["p"], r["p"]))
            then(dve.tensor_tensor(r["e"], r["e"], r["p"], ALU.mult))
            for t in range(NT):
                for i, weight in ((0, r["p"]), (1, r["e"])):
                    then(dve.tensor_scalar(oh[:, t, i, :], core.const("expert"), r["indexf"][:, t, i:i + 1], None,
                                           ALU.is_equal))
                    then(dve.tensor_scalar(r["part"][:, t, i, :], oh[:, t, i, :], weight[:, t:t + 1], None, ALU.mult))
                then(dve.tensor_tensor(r["gates"][:, t, :], r["part"][:, t, 0, :], r["part"][:, t, 1, :], ALU.add))
                op = dve.tensor_tensor(sel[:, t, :], oh[:, t, 0, :], oh[:, t, 1, :], ALU.add)
                if t == 0:
                    then(op)
            op.then_inc(s["chosen"], 1)
            dve.wait_ge(s["chosen"], 1)
            dve.wait_ge(s["ranks"], 1)
            ranks = core.banks[1][:, 0:NT * E].rearrange("p (t e) -> p t e", t=NT)
            then(dve.scalar_tensor_tensor(out=r["rank"], in0=ranks, scalar=1.0, in1=sel, op0=ALU.add, op1=ALU.mult))
            then(dve.tensor_scalar(r["rank"], r["rank"], -1.0, None, ALU.add))
            then(dve.tensor_reduce(r["busiest"], core.banks[1][:, 2 * E:3 * E], AX_X, ALU.max))
            then(dve.tensor_scalar(r["count"], r["busiest"], 0.5, None, ALU.is_gt))
            for n in range(1, ROUNDS):
                then(dve.tensor_scalar(r["more"], r["busiest"], float(n * CAP), None, ALU.is_gt))
                then(dve.tensor_tensor(r["count"], r["count"], r["more"], ALU.add))
            then(dve.tensor_copy(r["rounds"], r["count"]))


def moe_plan(a, experts, following):
    def plan(e):
        g, u = rows(a["moe_w_gate_2"][0, e], KC), rows(a["moe_w_up_2"][0, e], KC)
        d = a["moe_w_down_2"][0, e]
        return mlp_plan(EXPERT_DIM // FB,
                        lambda n: (KC, [g[:, :, n * FB:(n + 1) * FB], u[:, :, n * FB:(n + 1) * FB]]),
                        lambda n: (2, [rows_by_chunk(d[n * FB:(n + 1) * FB, :])]), LAG)
    return [tile for e in experts for tile in plan(e)] + plan(following)[0:MOE_SLOTS]


def choose(dve, r, e, s, m=0):
    for t in range(NT):
        dve.tensor_scalar(r["pick"][:, t, :], r["slot"], r["rank"][:, t, bass.ds(e, 1)], None,
                          ALU.is_equal).then_inc(s["picked"], 1)
    for t in range(NT):
        dve.wait_ge(s["picked"], NT * m + t + 1)
        dve.tensor_scalar(r["weigh"][:, t, :], r["pick"][:, t, :], r["gates"][:, t, bass.ds(e, 1)], None,
                          ALU.mult).then_inc(s["weighed"], 1)


def turn_weights(pe, core, r, s, m=0):
    pe.wait_ge(s["weighed"], NT * (m + 1))
    for t in range(NT):
        mm = pe.transpose(core.banks[6][0:CAP, t * P:(t + 1) * P], r["weigh"][:, t, :], core.const("ident"))
    mm.then_inc(s["weigh_turned"], 1)


def gather(pe, core, r, s, m=0):
    pe.wait_ge(s["picked"], NT * (m + 1))
    for c in range(KC):
        for t in range(NT):
            mm = pe.matmul(core.banks[6 + c // 4][:, (c % 4) * CAP:(c % 4 + 1) * CAP], core.x[:, t, c::KC],
                           r["pick"][:, t, :], start=(t == 0), stop=(t == NT - 1))
    mm.then_inc(s["gathered"], 1)


def spread(pe, core, r, t, banks):
    for half in range(2):
        mm = pe.matmul(banks[half][:], r["weightT_before"][:, t, :], r["ye"][:, half * BANK:(half + 1) * BANK],
                       start=True, stop=True)
    return mm


def x_chunks(a, k):
    return a[:, 4 * k:4 * k + 4, :].rearrange("p a b -> p (a b)")


def round_x(act, core, r, s, m=0):
    act.wait_ge(s["gathered"], m + 1)
    for k in range(2):
        act.copy(x_chunks(r["xh"], k), core.banks[6 + k][:]).then_inc(s["x_high"], 1)


def round_off_x(dve, core, r, s, m=0):
    for k in range(2):
        dve.wait_ge(s["x_high"], 2 * m + k + 1)
        dve.tensor_tensor(x_chunks(r["xl"], k), core.banks[6 + k][:], x_chunks(r["xh"], k), ALU.subtract)\
           .then_inc(s["x_low"], 1)


def expert_stage(core, w, followers, r, acc):
    nc = core.nc
    steps = EXPERT_DIM // FB
    n_tiles = 2 * steps
    high, low, xh, xl, hh, hl, sg = (r[n] for n in ("high", "low", "xh", "xl", "hh", "hl", "sg"))
    s = r["sems"]
    SPREAD, TURN_NEXT, GATHER = (1, 3), 5, 7

    units = []
    for m in range(PER):
        for n, (kind, i) in enumerate(mlp_plan(steps, lambda i: ("up", i), lambda i: ("down", i), LAG)):
            units += [(m * n_tiles + n, kind, m * steps + i, part) for part in range(2 if kind == "up" else 1)]
    position = {(kind, i, part): u for u, (n, kind, i, part) in enumerate(units)}
    all_steps = range(PER * steps)
    up_done = [position["up", i, 1] for i in all_steps]
    down_at = [position["down", i, 0] for i in all_steps]
    turn_after = [up_done[i + 1] if i % steps < steps - 1 else down_at[i - LAG] for i in all_steps]
    tile_end = {n: u for u, (n, kind, i, part) in enumerate(units)}
    first_unit = [position["up", m * steps, 0] for m in range(PER)]

    def raw(u):
        n, kind, i, part = units[u]
        return w.tile(n, KC, 2 * FB)[:, 4 * part:4 * part + 4, :] if kind == "up" else w.tile(n, 2, D)

    def unit(buffers, u):
        k = raw(u).shape[1]
        return buffers[:, u % UNITS, :].rearrange("p (k n) -> p k n", k=k)

    def turned_bank(i):
        return core.banks[2 + i % 2][:, 0:2 * CAP]

    def flat(a, i):
        return a[:, i % 2, :, :].rearrange("p a b -> p (a b)")

    with nc.Block() as block:
        @block.sync
        def _(sp):
            for n in range(PER * n_tiles):
                sp.wait_ge(s["weight_low"], tile_end[n] + 1)
                if n + w.slots < len(w.plan):
                    w.load(sp, n + w.slots)

        @block.tensor
        def _(pe):
            for u, (n, kind, i, part) in enumerate(units):
                m, own = divmod(i, steps)
                pe.wait_ge(s["weight_high"], u + 1)
                if kind == "up" and part == 0 and i >= 2:
                    pe.wait_ge(s["product"], i - 1)
                if kind == "up" and part == 0 and own == 0 and m:
                    pe.wait_ge(s["x_high"], 2 * m)
                    pe.wait_ge(s["x_low"], 2 * m)
                if kind == "down":
                    pe.wait_ge(s["hidden_low"], i + 1)
                    if own == 0 and m:
                        pe.wait_ge(s["ye"], 2 * m)
                for j, (buffer, other_low) in enumerate(((high, False), (high, True), (low, False))):
                    wt = unit(buffer, u)
                    if j == 2:
                        pe.wait_ge(s["weight_low"], u + 1)
                    if kind == "up":
                        for c in range(4):
                            mm = pe.matmul(core.banks[i % 2][:], (xl if other_low else xh)[:, 4 * part + c, :],
                                           wt[:, c, :], start=(part == 0 and j == 0 and c == 0),
                                           stop=(part == 1 and j == 2 and c == 3))
                    else:
                        for half in range(2):
                            for c in range(2):
                                mm = pe.matmul(core.banks[4 + half][:], (hl if other_low else hh)[:, i % 2, c, :],
                                               wt[:, c, half * BANK:(half + 1) * BANK],
                                               start=(own == 0 and j == 0 and c == 0),
                                               stop=(own == steps - 1 and j == 2 and c == 1))
                mm.then_inc(s["unit_used"], 1)
                for k in all_steps:
                    if turn_after[k] != u:
                        continue
                    pe.wait_ge(s["product"], k + 1)
                    if k >= 2:
                        pe.wait_ge(s["hidden_low"], k - 1)
                    for c in range(2):
                        mm = pe.transpose(core.banks[2 + k % 2][:, c * CAP:(c + 1) * CAP],
                                          sg[:, k % 2, c * P:(c + 1) * P], core.const("ident"))
                    mm.then_inc(s["turned"], 1)
                if kind != "up" or part != 1:
                    continue
                if own in SPREAD:
                    t = SPREAD.index(own)
                    if t:
                        pe.wait_ge(s["added"], 4 * m + 2)
                    elif m:
                        pe.wait_ge(s["ye"], 2 * m)
                    spread(pe, core, r, t, core.banks[6:8]).then_inc(s["spread"], 1)
                if own == TURN_NEXT:
                    pe.wait_ge(s["added"], 4 * m + 4)
                    turn_weights(pe, core, r, s, m)
                if own == GATHER:
                    pe.wait_ge(s["weightT"], 2 * m + 2)
                    gather(pe, core, r, s, m)

        @block.scalar
        def _(act):
            for u in range(len(units) + UNITS):
                done = u - UNITS
                if done in up_done:
                    i = up_done.index(done)
                    m, own = divmod(i, steps)
                    act.wait_ge(s["unit_used"], done + 1)
                    if i >= 2:
                        act.wait_ge(s["turned"], i - 1)
                    act.activation(sg[:, i % 2, :], core.banks[i % 2][:, 0:FB], ACT.Silu).then_inc(s["silu"], 1)
                    if own == TURN_NEXT + 1:
                        act.wait_ge(s["spread"], NT * (m + 1))
                        act.copy(r["weightT_before"], r["weightT"]).then_inc(s["weightT"], 1)
                        act.wait_ge(s["weightT"], 2 * m + 1)
                        act.wait_ge(s["weigh_turned"], m + 1)
                        act.copy(r["weightT"].rearrange("p a b -> p (a b)"), core.banks[6][:, 0:NT * P])\
                           .then_inc(s["weightT"], 1)
                    if own == steps - 1:
                        round_x(act, core, r, s, m)
                if u < len(units):
                    n = units[u][0]
                    if units[u][3] == 0:
                        w.wait(act, n)
                    if u >= UNITS:
                        act.wait_ge(s["unit_used"], u - UNITS + 1)
                    act.copy(unit(high, u), raw(u)).then_inc(s["weight_high"], 1)
                if done in turn_after:
                    i = turn_after.index(done)
                    act.wait_ge(s["turned"], i + 1)
                    if i >= 2:
                        act.wait_ge(s["unit_used"], down_at[i - 2] + 1)
                    act.copy(flat(hh, i), turned_bank(i)).then_inc(s["hidden_high"], 1)
                if done in down_at and (down_at.index(done) + 1) % steps == 0:
                    m = down_at.index(done) // steps
                    act.wait_ge(s["spread"], NT * (m + 1))
                    act.wait_ge(s["unit_used"], done + 1)
                    act.copy(r["ye"][:, 0:BANK], core.banks[4][:]).then_inc(s["ye"], 1)

        @block.vector
        def _(dve):
            for u in range(len(units) + UNITS):
                done = u - UNITS
                if done in up_done:
                    i = up_done.index(done)
                    dve.wait_ge(s["silu"], i + 1)
                    dve.tensor_tensor(sg[:, i % 2, :], sg[:, i % 2, :], core.banks[i % 2][:, FB:2 * FB], ALU.mult)\
                       .then_inc(s["product"], 1)
                    if (i + 1) % steps == 0:
                        round_off_x(dve, core, r, s, i // steps)
                if u < len(units):
                    dve.wait_ge(s["weight_high"], u + 1)
                    dve.tensor_tensor(unit(low, u), raw(u), unit(high, u), ALU.subtract).then_inc(s["weight_low"], 1)
                if done in turn_after:
                    i = turn_after.index(done)
                    dve.wait_ge(s["hidden_high"], i + 1)
                    dve.tensor_tensor(flat(hl, i), turned_bank(i), flat(hh, i), ALU.subtract)\
                       .then_inc(s["hidden_low"], 1)
                if done in first_unit:
                    m = first_unit.index(done)
                    choose(dve, r, followers[m], s, m)
                if done in up_done and up_done.index(done) % steps in SPREAD:
                    m, own = divmod(up_done.index(done), steps)
                    t = SPREAD.index(own)
                    dve.wait_ge(s["spread"], NT * m + t + 1)
                    for half in range(2):
                        v = acc[:, t, half * BANK:(half + 1) * BANK]
                        dve.tensor_tensor(v, v, core.banks[6 + half][:], ALU.add).then_inc(s["added"], 1)
                if done in down_at and (down_at.index(done) + 1) % steps == 0:
                    m = down_at.index(done) // steps
                    dve.wait_ge(s["spread"], NT * (m + 1))
                    dve.wait_ge(s["unit_used"], done + 1)
                    dve.tensor_copy(r["ye"][:, BANK:D], core.banks[5][:]).then_inc(s["ye"], 1)


def expert_tidy(core, w, s):
    n_tiles = PER * 2 * (EXPERT_DIM // FB)

    def take_off(sp):
        for slot in range(w.slots):
            used = sum(len(w.plan[n][1]) for n in range(slot, n_tiles, w.slots))
            sp.sem_inc(w.landed[slot], -16 * used)

    tidy(core, s.values(), take_off)


def round_start_stage(core, r):
    s = r["sems"]
    with core.nc.Block() as block:
        @block.tensor
        def _(pe):
            turn_weights(pe, core, r, s)
            pe.wait_ge(s["weightT"], 1)
            gather(pe, core, r, s)

        @block.vector
        def _(dve):
            choose(dve, r, 0, s)
            round_off_x(dve, core, r, s)

        @block.scalar
        def _(act):
            act.wait_ge(s["weigh_turned"], 1)
            act.copy(r["weightT"].rearrange("p a b -> p (a b)"), core.banks[6][:, 0:NT * P]).then_inc(s["weightT"], 1)
            round_x(act, core, r, s)

        @block.gpsimd
        def _(pool):
            pool.memset(r["weightT_before"], 0.0)
            pool.memset(r["ye"], 0.0)
    tidy(core, s.values())


def round_end_stage(core, r, acc):
    s = r["sems"]
    with core.nc.Block() as block:
        @block.tensor
        def _(pe):
            for t in range(NT):
                spread(pe, core, r, t, core.banks[2 * t:2 * t + 2]).then_inc(s["spread"], 1)

        @block.vector
        def _(dve):
            for t in range(NT):
                dve.wait_ge(s["spread"], t + 1)
                for half in range(2):
                    v = acc[:, t, half * BANK:(half + 1) * BANK]
                    dve.tensor_tensor(v, v, core.banks[2 * t + half][:], ALU.add)

        @block.gpsimd
        def _(pool):
            pool.tensor_scalar(r["rank"], r["rank"], float(-CAP), None, ALU.add)
    tidy(core, s.values())


def moe_stages(core, a):
    nc = core.nc
    at = 0
    r = {"slot": core.const("slot")}
    acc, at = core.part(at, NT, D)
    for name, shape in (("w", (KC, E)), ("logits", (NT, E)), ("top", (NT, 8)), ("index", (NT, 8)), ("indexf", (NT, 8)),
                        ("onehot", (NT, 2, E)), ("part", (NT, 2, E)), ("sel", (NT, E)), ("gates", (NT, E)),
                        ("rank", (NT, E)), ("e", (NT,)), ("p", (NT,)), ("busiest", (1,)), ("count", (1,)),
                        ("more", (1,)), ("rounds", (1,)),
                        ("pick", (NT, CAP)), ("weigh", (NT, CAP)), ("weightT", (NT, P)), ("weightT_before", (NT, P)),
                        ("ye", (D,)), ("sg", (2, FB))):
        r[name], at = core.part(at, *shape)
    r["index"], r["rounds"] = r["index"].bitcast(U32), r["rounds"].bitcast(I32)
    w = Weights(core, "moe", MOE_SLOTS, moe_plan(a, [0], 0))
    def fill(sp):
        w.fill(sp)
        core.affine.fetch(sp, "ln11")

    router_stage(core, a, r, acc, fill)
    s = r["sems"] = {n: core.sem(f"moe_{n}") for n in (
        "picked", "weighed", "gathered", "weigh_turned", "weightT", "silu", "product", "turned", "hidden_high",
        "hidden_low", "x_high", "x_low", "ye", "weight_high", "weight_low", "unit_used", "spread", "added")}
    rounds = nc.values_load(r["rounds"][0:1, 0:1], min_val=1, max_val=ROUNDS,
                            skip_runtime_bounds_check_because="a sum of ROUNDS comparisons, the first always true")
    with ExitStack() as memory:
        for name, shape in (("high", [P, UNITS, SLOT // 2]), ("low", [P, UNITS, SLOT // 2]), ("xh", [P, KC, CAP]),
                            ("xl", [P, KC, CAP]), ("hh", [P, 2, 2, CAP]), ("hl", [P, 2, 2, CAP])):
            r[name] = memory.enter_context(nc.sbuf_tensor(f"moe_{name}", shape, F32R))[:]
        with nc.Fori(0, rounds):
            round_start_stage(core, r)
            with nc.Fori(0, E // PER) as group:
                experts = [group * PER + m for m in range(PER)]
                followers = [group * PER + m + 1 for m in range(PER - 1)] + [(group * PER + PER) % E]
                w.plan = moe_plan(a, experts, followers[-1])
                expert_stage(core, w, followers, r, acc)
                expert_tidy(core, w, s)
            round_end_stage(core, r, acc)
    with nc.Block() as block:
        @block.sync
        def _(sp):
            for n in range(w.slots):
                sp.wait_ge(w.landed[n], 16 * len(w.plan[n][1]))

        @block.vector
        def _(dve):
            dve.tensor_copy(core.x[:, 0, :], acc[:, 0, :])

        @block.scalar
        def _(act):
            act.copy(core.x[:, 1, :], acc[:, 1, :])


def first_half(core, a, mid):
    gdn = Weights(core, "gdn", SLOTS, None)
    w_in = rows(a["a_w_in_2"][0], KC)
    w_out = rows(a["a_w_out_2"][0], KC)
    edges = [(c, min(c + BW, w_in.shape[2])) for c in range(0, w_in.shape[2], BW)]
    edges = edges[0:4] + edges[6:] + edges[4:6]
    gdn.plan = [(KC, [w_in[:, :, s:e]]) for s, e in edges]
    gdn.plan += [(KC, [w_out[:, :, h * BW:(h + 1) * BW]]) for h in range(2)]
    with core.scratch("final"):
        norm_stage(core, "final", RMS_EPS, core.affine.gain[:, 0, :], natural=True,
                   before=lambda sp: gdn.fill(sp, 0, 2))
    with core.scratch("gdn_lower", GDN_LOWER):
        raw, z, ba = gdn_projection(core, gdn)
        with core.scratch("gdn_upper", GDN_UPPER, GDN_LOWER), \
                core.nc.sbuf_tensor("gdn_more", [P, SLOT], F32) as more:
            gdn_stages(core, a, gdn, raw, z, ba, more[:])

    def fill_free(sp):
        for n in range(SLOTS):
            if n not in (1, 2):
                mid.load(sp, n)

    output_stage(core, "gdn_out", gdn, 7, ALPHA, before=fill_free)
    tidy(core, core.sems, lambda sp: (mid.load(sp, 1), mid.load(sp, 2)))


def second_block(core, a):
    with core.semaphores():
        mid = Weights(core, "mid", SLOTS, None)
        g, u = rows(a["ffn_w_gate_2"][0], KC), rows(a["ffn_w_up_2"][0], KC)
        d = a["ffn_w_down_2"][0]
        mid.plan = mlp_plan(FFN_DIM // FB, lambda n: (KC, [g[:, :, n * FB:(n + 1) * FB], u[:, :, n * FB:(n + 1) * FB]]),
                            lambda n: (2, [rows_by_chunk(d[n * FB:(n + 1) * FB, :])]))
        swa_first = len(mid.plan)
        b_in, b_out = rows(a["b_w_in_2"][0], KC), rows(a["b_w_out_2"][0], KC)
        q_dim = SWA_HEADS * HD
        mid.plan += [(KC, [b_in[:, :, h * BW:(h + 1) * BW]]) for h in range(2)]
        ks = [b_in[:, :, q_dim + HD * (j // 2):q_dim + HD * (j // 2) + HD] for j in range(4)]
        mid.plan += [(KC, ks + [b_in[:, :, q_dim + P:q_dim + 2 * P]])]
        mid.plan += [(KC, [b_out[:, :, h * BW:(h + 1) * BW]]) for h in range(2)]

        with core.semaphores():
            first_half(core, a, mid)
        with core.scratch("ln00"):
            norm_stage(core, "ln00", LN_EPS, core.affine.gain[:, 1, :], core.affine.shift[:, 1, :], natural=True)
        mlp_stage(core, "ffn", mid, 0, FFN_DIM // FB, gated=True, alpha=ALPHA,
                  before=lambda sp: core.affine.fetch(sp, "ln01"))
        with core.scratch("swa"):
            norm_stage(core, "ln01", LN_EPS, core.affine.gain[:, 2, :], core.affine.shift[:, 2, :], natural=True)
            swa_stages(core, mid, swa_first)
        output_stage(core, "swa_out", mid, swa_first + 3, ALPHA)
        with core.scratch("ln10"):
            norm_stage(core, "ln10", LN_EPS, core.affine.gain[:, 3, :], core.affine.shift[:, 3, :], natural=True)
        tidy(core, core.sems)


def kernel(**inputs):
    import concourse.bacc as bacc
    from concourse.bass_utils import run_bass_kernel_spmd

    nc = bacc.Bacc("TRN2", target_bir_lowering=False, num_devices=1)
    arrays, args = {}, {}
    for name, value in [*inputs.items(), ("consts", CONSTS)]:
        value = np.ascontiguousarray(value)
        arrays[f"in_{name}"] = value
        args[name] = nc.dram_tensor(f"in_{name}", value.shape, mybir.dt.from_np(value.dtype),
                                    kind="ExternalInput").ap()
    out = nc.dram_tensor("out", (1, T, D), F32, kind="ExternalOutput").ap()
    build(nc, args, out)
    r = run_bass_kernel_spmd(nc, [arrays], core_ids=[0])
    return r.results[0]["out"]
```
